# Optimizing a Trainium2 kernel written in Bass

```python
import math
import jax, jax.numpy as jnp
from jax import lax
import numpy as np

D_MODEL = 2048
BATCH = 1
SEQ = 512
DEPTH = 1

N_META = 16
MIX_WIDTH = D_MODEL
RWKV_WIDTH = MIX_WIDTH // 2
RWKV_HEAD_DIM = 64
RWKV_HEADS = RWKV_WIDTH // RWKV_HEAD_DIM
RWKV_LORA_W = 64
RWKV_LORA_A = 64
RWKV_SHIFT_COLS = 3 * RWKV_WIDTH + RWKV_LORA_W + RWKV_LORA_A
RWKV_COLS = RWKV_SHIFT_COLS + RWKV_WIDTH
DIFF_WIDTH = MIX_WIDTH - RWKV_WIDTH
DIFF_HEAD_DIM = 64
DIFF_V_DIM = 2 * DIFF_HEAD_DIM
DIFF_HEADS = DIFF_WIDTH // DIFF_V_DIM
DIFF_COLS = 4 * DIFF_WIDTH
IN_COLS = RWKV_COLS + DIFF_COLS

ROPE_THETA = 10000.0
Q_BLOCK = 128
NORM_EPS = 1e-6
GN_EPS = 64e-5
SUBLN_EPS = 1e-5

kernel_name = "hymba_rwkv7_diffattn_hybrid"

def rms_norm(x, g, eps=NORM_EPS):
    xf = x.astype(jnp.float32)
    y = xf * lax.rsqrt(jnp.mean(xf * xf, axis=-1, keepdims=True) + eps)
    return (y * g.astype(jnp.float32)).astype(x.dtype)

def rope_tables(L):
    pos = jnp.arange(L, dtype=jnp.float32)
    inv_freq = ROPE_THETA ** (-jnp.arange(0, DIFF_HEAD_DIM, 2, dtype=jnp.float32) / DIFF_HEAD_DIM)
    ang = pos[:, None] * inv_freq[None, :]
    ang = jnp.concatenate([ang, ang], axis=-1)
    return jnp.cos(ang), jnp.sin(ang)

def apply_rope(x, cos, sin):
    half = x.shape[-1] // 2
    x1, x2 = x[..., :half], x[..., half:]
    rot = jnp.concatenate([-x2, x1], axis=-1)
    c = cos[None, :, None, :].astype(x.dtype)
    s = sin[None, :, None, :].astype(x.dtype)
    return x * c + rot * s

def rwkv7_branch(u, mu, w0, w_up, a0, a_up, k_k, k_a, r_k, gn_w, gn_b):
    Bn, L, _ = u.shape
    H, Dh, C = RWKV_HEADS, RWKV_HEAD_DIM, RWKV_WIDTH
    u_prev = jnp.pad(u, ((0, 0), (1, 0), (0, 0)))[:, :-1]
    u = u + (u_prev - u) * mu.astype(u.dtype)
    r = u[..., :C]
    k = u[..., C:2 * C]
    v = u[..., 2 * C:3 * C]
    wd = u[..., 3 * C:3 * C + RWKV_LORA_W]
    ad = u[..., 3 * C + RWKV_LORA_W:]
    w = -jax.nn.softplus(-(w0 + jnp.tanh(wd) @ w_up).astype(jnp.float32)) - 0.5
    decay = jnp.exp(-jnp.exp(w))
    a = jax.nn.sigmoid((a0 + ad @ a_up).astype(jnp.float32))
    hs = lambda t: t.reshape(Bn, L, H, Dh).astype(jnp.float32)
    r, k, v, decay, a = hs(r), hs(k), hs(v), hs(decay), hs(a)
    kk = k * k_k.reshape(H, Dh).astype(jnp.float32)
    kk = kk / jnp.maximum(jnp.sqrt(jnp.sum(kk * kk, axis=-1, keepdims=True)), 1e-12)
    k = k * (1.0 + (a - 1.0) * k_a.reshape(H, Dh).astype(jnp.float32))
    b = kk * a

    def step(S, inp):
        r_t, w_t, k_t, v_t, kk_t, b_t = inp
        sa = jnp.einsum('bhvk,bhk->bhv', S, -kk_t)
        S = S * w_t[:, :, None, :] + sa[..., None] * b_t[:, :, None, :] + v_t[..., None] * k_t[:, :, None, :]
        y = jnp.einsum('bhvk,bhk->bhv', S, r_t)
        return S, y

    tm = lambda t: jnp.moveaxis(t, 1, 0)
    S0 = jnp.zeros((Bn, H, Dh, Dh), jnp.float32)
    _, ys = lax.scan(step, S0, (tm(r), tm(decay), tm(k), tm(v), tm(kk), tm(b)))
    y = jnp.moveaxis(ys, 0, 1)
    mean = jnp.mean(y, axis=-1, keepdims=True)
    var = jnp.mean(jnp.square(y - mean), axis=-1, keepdims=True)
    y = ((y - mean) * lax.rsqrt(var + GN_EPS)).reshape(Bn, L, C)
    y = y * gn_w.astype(jnp.float32) + gn_b.astype(jnp.float32)
    bonus = jnp.sum(r * k * r_k.astype(jnp.float32)[None, None], axis=-1, keepdims=True) * v
    y = y + bonus.reshape(Bn, L, C)
    return y.astype(u.dtype)

def diff_attn_branch(q, k, v, cos, sin, lam_q1, lam_k1, lam_q2, lam_k2, subln_w, lambda_init):
    Bn, L, _ = q.shape
    H, Dh = DIFF_HEADS, DIFF_HEAD_DIM
    q = apply_rope(q.reshape(Bn, L, 2 * H, Dh), cos, sin).reshape(Bn, L, H, 2, Dh)
    k = apply_rope(k.reshape(Bn, L, 2 * H, Dh), cos, sin).reshape(Bn, L, H, 2, Dh)
    v = v.reshape(Bn, L, H, DIFF_V_DIM)
    lam = (jnp.exp(jnp.sum(lam_q1.astype(jnp.float32) * lam_k1.astype(jnp.float32)))
           - jnp.exp(jnp.sum(lam_q2.astype(jnp.float32) * lam_k2.astype(jnp.float32)))
           + lambda_init)
    scale = Dh ** -0.5
    bounds = [0] + list(range(N_META, L, Q_BLOCK)) + [L]
    outs = []
    for s, e in zip(bounds[:-1], bounds[1:]):
        qb = q[:, s:e]
        kb = k[:, :e]
        vb = v[:, :e]
        sc = jnp.einsum('bqhcd,bkhcd->bhcqk', qb, kb).astype(jnp.float32) * scale
        mask = jnp.arange(e)[None, :] <= jnp.arange(s, e)[:, None]
        sc = jnp.where(mask, sc, -jnp.inf)
        p = jax.nn.softmax(sc, axis=-1)
        attn = p[:, :, 0] - lam * p[:, :, 1]
        outs.append(jnp.einsum('bhqk,bkhd->bqhd', attn.astype(vb.dtype), vb))
    o = jnp.concatenate(outs, axis=1)
    o = rms_norm(o, subln_w, SUBLN_EPS) * (1.0 - lambda_init)
    return o.reshape(Bn, L, DIFF_WIDTH)

def setup_inputs(seed: int = 0) -> dict:
    key = jax.random.key(seed)
    ks = jax.random.split(key, 24)
    f32 = jnp.float32
    nrm = lambda k, shape, s: jax.random.normal(k, shape, f32) * s
    H, Dh = RWKV_HEADS, RWKV_HEAD_DIM
    return {
        "x": nrm(ks[0], (BATCH, SEQ, D_MODEL), 1.0),
        "meta_tokens": nrm(ks[1], (N_META, D_MODEL), 1.0),
        "pre_norm_w": 1.0 + nrm(ks[2], (DEPTH, D_MODEL), 0.05),
        "w_in": nrm(ks[3], (DEPTH, D_MODEL, IN_COLS), D_MODEL ** -0.5),
        "rwkv_mu": jax.random.uniform(ks[4], (DEPTH, RWKV_SHIFT_COLS), f32, 0.0, 1.0),
        "rwkv_w0": jax.random.uniform(ks[5], (DEPTH, RWKV_WIDTH), f32, -3.0, 1.0),
        "rwkv_w_up": nrm(ks[6], (DEPTH, RWKV_LORA_W, RWKV_WIDTH), 0.1),
        "rwkv_a0": nrm(ks[7], (DEPTH, RWKV_WIDTH), 0.1),
        "rwkv_a_up": nrm(ks[8], (DEPTH, RWKV_LORA_A, RWKV_WIDTH), 0.1),
        "rwkv_k_k": 0.85 + nrm(ks[9], (DEPTH, RWKV_WIDTH), 0.05),
        "rwkv_k_a": 1.0 + nrm(ks[10], (DEPTH, RWKV_WIDTH), 0.05),
        "rwkv_r_k": nrm(ks[11], (DEPTH, H, Dh), 0.1),
        "rwkv_gn_w": 1.0 + nrm(ks[12], (DEPTH, RWKV_WIDTH), 0.05),
        "rwkv_gn_b": nrm(ks[13], (DEPTH, RWKV_WIDTH), 0.01),
        "diff_lam_q1": nrm(ks[14], (DEPTH, DIFF_HEAD_DIM), 0.1),
        "diff_lam_k1": nrm(ks[15], (DEPTH, DIFF_HEAD_DIM), 0.1),
        "diff_lam_q2": nrm(ks[16], (DEPTH, DIFF_HEAD_DIM), 0.1),
        "diff_lam_k2": nrm(ks[17], (DEPTH, DIFF_HEAD_DIM), 0.1),
        "diff_subln_w": 1.0 + nrm(ks[18], (DEPTH, DIFF_V_DIM), 0.05),
        "w_out": nrm(ks[19], (DEPTH, MIX_WIDTH, D_MODEL), MIX_WIDTH ** -0.5),
        "post_norm_w": 1.0 + nrm(ks[20], (DEPTH, D_MODEL), 0.05),
    }

def reference(x, meta_tokens, pre_norm_w, w_in, rwkv_mu, rwkv_w0, rwkv_w_up, rwkv_a0, rwkv_a_up,
              rwkv_k_k, rwkv_k_a, rwkv_r_k, rwkv_gn_w, rwkv_gn_b, diff_lam_q1, diff_lam_k1,
              diff_lam_q2, diff_lam_k2, diff_subln_w, w_out, post_norm_w):
    Bn = x.shape[0]
    meta = jnp.broadcast_to(meta_tokens[None].astype(x.dtype), (Bn, N_META, D_MODEL))
    h = jnp.concatenate([meta, x], axis=1)
    L = h.shape[1]
    cos, sin = rope_tables(L)
    for layer in range(DEPTH):
        lambda_init = 0.8 - 0.6 * math.exp(-0.3 * layer)
        hn = rms_norm(h, pre_norm_w[layer])
        proj = hn @ w_in[layer]
        u_r = proj[..., :RWKV_SHIFT_COLS]
        g_r = proj[..., RWKV_SHIFT_COLS:RWKV_COLS]
        o = RWKV_COLS
        q_d = proj[..., o:o + DIFF_WIDTH]
        k_d = proj[..., o + DIFF_WIDTH:o + 2 * DIFF_WIDTH]
        v_d = proj[..., o + 2 * DIFF_WIDTH:o + 3 * DIFF_WIDTH]
        g_d = proj[..., o + 3 * DIFF_WIDTH:o + 4 * DIFF_WIDTH]
        y_r = rwkv7_branch(u_r, rwkv_mu[layer], rwkv_w0[layer], rwkv_w_up[layer], rwkv_a0[layer],
                           rwkv_a_up[layer], rwkv_k_k[layer], rwkv_k_a[layer], rwkv_r_k[layer],
                           rwkv_gn_w[layer], rwkv_gn_b[layer]) * jax.nn.silu(g_r)
        y_d = diff_attn_branch(q_d, k_d, v_d, cos, sin, diff_lam_q1[layer], diff_lam_k1[layer],
                               diff_lam_q2[layer], diff_lam_k2[layer], diff_subln_w[layer],
                               lambda_init) * jax.nn.silu(g_d)
        y = jnp.concatenate([y_r, y_d], axis=-1) @ w_out[layer]
        h = h + rms_norm(y, post_norm_w[layer])
    return h[:, N_META:]


_drawn_inputs = setup_inputs


def setup_inputs(seed=0):
    import zlib

    import numpy as np

    out = dict(_drawn_inputs(seed))
    spreads = {}
    factors = {'rwkv_k_k': 200.0,
     'rwkv_gn_b': 35.274,
     'diff_lam_q1': 200.0,
     'diff_subln_w': 9.322,
     'rwkv_a0': 4.271,
     'rwkv_k_a': 3.654,
     'rwkv_gn_w': 3.952,
     'diff_lam_q2': 3.097}
    for name, (base, spread) in spreads.items():
        noise = np.random.default_rng([zlib.crc32(name.encode()), seed]).standard_normal(out[name].shape)
        drawn = base * np.exp(spread * noise) if base else spread * noise
        out[name] = __import__('jax').numpy.asarray(drawn.astype(out[name].dtype))
    for name, factor in factors.items():
        out[name] = (out[name] * factor).astype(out[name].dtype)
    return out
```

```python
import math

import numpy as np
import concourse.bass as bass
from concourse import mybir
from contextlib import ExitStack

F32 = mybir.dt.float32
F32R = mybir.dt.float32r
F16 = mybir.dt.float16
ALU = mybir.AluOpType
ACT = mybir.ActivationFunctionType
AX = mybir.AxisListType.X

P = 128
D = 2048
SEQ = 512
META = 16
L = SEQ + META
KT = D // P
RW = 1024
NP_ = RW // P
HD = 64
CH = 64
PAD = CH - META
TP = PAD + L
NC = TP // CH
TG = 5
TPX = TG * P
GC = 3
NG = NC // GC
UK = 4
UPT = KT // UK
RING = 4
AHEAD = 3
LORA_COL = 3 * RW
G_COL = LORA_COL + P
ATT_COL = G_COL + RW
TILE_COLS = {"rwkv": (RW, 2 * RW, 0, G_COL),
             "attn": (ATT_COL, ATT_COL + RW, ATT_COL + 2 * RW, ATT_COL + 3 * RW)}
FULL = {"rwkv": (True, True, True, False), "attn": (False, True, True, False)}
N_TILES = 1 + 4 * 2 * NP_
SUB = 64
EDGE = 248
EPS, GN_EPS, SUB_EPS = 1e-6, 64e-5, 1e-5
LAM0 = 0.8 - 0.6 * math.exp(0.0)
C_DECAY = math.exp(-0.5)
NEG = -3.0e38
PC = {}
_n = 0
for _name, _rows in (("mu_r", 8), ("mu_k", 8), ("mu_v", 8), ("mu_l", 1), ("a0", 8), ("k_k", 8), ("k_a", 8),
                     ("r_k", 8), ("gn_w", 8), ("gn_b", 8), ("pre", 16), ("sub", 1)):
    PC[_name] = _n
    _n += _rows
N_PAR = _n


def constants():
    i = np.arange(P)
    s, t = i[:, None], i[None, :]
    same = (s // CH) == (t // CH)
    ident = (s == t).astype(np.float32)
    strict = (same & (s < t)).astype(np.float32)
    incl = ((s % CH) <= np.arange(CH)[None, :]).astype(np.float32)
    tri = (same & (s <= t)).astype(np.float32)
    tri0 = tri * (s >= PAD)
    centre = ident - same / CH
    block = same.astype(np.float32)
    heads = np.stack([(i < HD), (i >= HD)], 1).astype(np.float32)
    rot = np.zeros((P, P), np.float32)
    for m in range(P):
        if m % HD < HD // 2:
            rot[m + HD // 2, m] = -1.0
        else:
            rot[m - HD // 2, m] = 1.0
    causal = np.where(t <= s, 0.0, NEG).astype(np.float32)
    f32 = np.concatenate([ident, strict, incl, tri0, tri, centre, block, heads, heads / HD,
                          np.full((P, 1), 1.0 / P), rot, causal], 1).astype(np.float32)
    levels = [ident, -ident]
    m = 1
    while m < CH:
        levels.append(same & ((s // (2 * m)) == (t // (2 * m))) & ((s // m) % 2 == 0) & ((t // m) % 2 == 1))
        m *= 2
    f16 = np.concatenate(levels, 1).astype(np.float16)
    pos = np.arange(L, dtype=np.float32)
    inv = (np.float32(10000.0) ** (-np.arange(0, HD, 2, dtype=np.float32) / np.float32(HD))).astype(np.float32)
    ang = (pos[:, None] * inv[None, :]).astype(np.float32)
    ang = np.concatenate([ang] * 4, 1).T
    rope = np.concatenate([np.cos(ang), np.sin(ang)], 1).astype(np.float32)
    return f32, f16, rope


LEVELS = 6
C32 = {}
_n = 0
for _name, _w in (("ident", P), ("strict", P), ("incl", CH), ("tri0", P), ("tri", P), ("centre", P), ("block", P),
                  ("heads", 2), ("heads_mean", 2), ("mean", 1), ("rot", P), ("causal", P)):
    C32[_name] = (_n, _w)
    _n += _w
C32_W = _n


def hybrid_layer(nc, x, meta_tokens, pre_norm_w, w_in, rwkv_mu, rwkv_w0, rwkv_w_up, rwkv_a0, rwkv_a_up,
                 rwkv_k_k, rwkv_k_a, rwkv_r_k, rwkv_gn_w, rwkv_gn_b, lam_q1, lam_k1, lam_q2, lam_k2,
                 subln_w, w_out, post_norm_w, c32_dram, c16_dram, rope_dram, out):
    ctx = ExitStack()
    with ctx:
        def sb(name, shape, dt=F32):
            return ctx.enter_context(nc.sbuf_tensor(name, shape, dt))

        def sem(name):
            return ctx.enter_context(nc.semaphore(name))

        hn_hi = sb("hn_hi", [P, KT, L], F32R)
        hn_lo = sb("hn_lo", [P, KT, L], F32R)
        w_raw = sb("w_raw", [P, RING, UK * P])
        w_hi = sb("w_hi", [P, RING, UK * P], F32R)
        w_lo = sb("w_lo", [P, RING, UK * P], F32R)
        big = sb("big", [P, 4 * D])
        c32 = sb("c32", [P, C32_W])
        c16 = sb("c16", [P, (2 + LEVELS) * P], F16)
        par = sb("par", [P, N_PAR])
        om_mu = sb("om_mu", [P, 25])
        half_a0 = sb("half_a0", [P, 8])
        half_ka = sb("half_ka", [P, 8])
        om_ka = sb("om_ka", [P, 8])
        gate_sub = sb("gate_sub", [P, 1])
        lam = sb("lam", [P, 1])
        power = sb("power", [P, 16])
        lora = sb("lora", [P, TPX])
        xk = sb("xk", [P, TP])
        xv = sb("xv", [P, TP])
        xr = sb("xr", [P, TP])
        gate = sb("gate", [P, SEQ])
        gate2 = sb("gate2", [P, SEQ])
        tanh_g = sb("tanh_g", [P, SEQ])
        t512b = tanh_g[:]
        ARENA = 16180
        arena = sb("arena", [P, ARENA])
        taken = {}

        def carve(stage, name, n, dt=F32):
            at = taken.get(stage, 0)
            words = n if dt is F32 else n // 2
            taken[stage] = at + words
            assert taken[stage] <= ARENA, (stage, name, taken[stage])
            v = arena[:, at:at + words]
            return v if dt is F32 else v.bitcast(dt)

        ysum = carve("rwkv", "ysum", SEQ)
        bonus_v = carve("rwkv", "bonus_v", SEQ)
        t512 = carve("rwkv", "t512", SEQ)
        gn_small = carve("rwkv", "gn_small", 8)
        gn_pow = carve("rwkv", "gn_pow", 8)
        wu = carve("rwkv", "wu", P)
        au = carve("rwkv", "au", P)
        w0b = carve("rwkv", "w0b", P)
        ew = carve("rwkv", "ew", NC * (CH + 1))
        ew3 = ew.rearrange("p (c t) -> p c t", c=NC)
        kk_small = carve("rwkv", "kk_small", 2 * TG)
        kk_pow = carve("rwkv", "kk_pow", 2 * TG)
        tmp = carve("rwkv", "tmp", TPX)
        zt = tmp
        rc = carve("rwkv", "rc", TP)
        apad = carve("rwkv", "apad", NC * P).rearrange("p (c t) -> p c t", c=NC)
        bpad = carve("rwkv", "bpad", NC * P).rearrange("p (c t) -> p c t", c=NC)
        kpad = carve("rwkv", "kpad", NC * P).rearrange("p (c t) -> p c t", c=NC)
        vpad = carve("rwkv", "vpad", NC * P).rearrange("p (c t) -> p c t", c=NC)

        def two(name, n, dt=F32):
            return [carve("rwkv", f"{name}{b}", n, dt) for b in range(2)]

        bk_tok = two("bk_tok", 2 * GC * P)
        v_tok = two("v_tok", GC * P)
        ak_t = two("ak_t", GC * P)
        rb_t = two("rb_t", GC * CH)
        rk_t = two("rk_t", GC * CH)
        t_t = two("t_t", GC * P)
        state = carve("rwkv", "state", P)
        state0 = carve("rwkv", "state0", P)
        g_sb = carve("rwkv", "g_sb", P)
        u_sb = carve("rwkv", "u_sb", P)
        shared = taken["rwkv"]
        emi = carve("rwkv", "emi", TPX)
        tha = carve("rwkv", "tha", TP)
        kk = carve("rwkv", "kk", TP)
        kp = carve("rwkv", "kp", TP)
        taken["rwkv"] = shared
        ab32 = carve("rwkv", "ab32", GC * P)
        ab_hi = carve("rwkv", "ab_hi", GC * P, F16)
        ab_lo = carve("rwkv", "ab_lo", GC * P, F16)
        lv = carve("rwkv", "lv", LEVELS * GC * P, F16)
        x16 = carve("rwkv", "x16", GC * P, F16)
        xt16 = carve("rwkv", "xt16", GC * P, F16)
        z16 = carve("rwkv", "z16", GC * P, F16)
        r16 = carve("rwkv", "r16", GC * P, F16)
        taken["start"] = 3 * SEQ + TPX
        xm = carve("start", "xm", D)
        par_rows = carve("start", "par_rows", P)
        lam_in = carve("start", "lam_in", 4 * HD)
        lam_p = carve("start", "lam_p", HD)
        lam_s = carve("start", "lam_s", 4)
        norm_s = carve("start", "norm_s", 16)
        junk = carve("start", "junk", D)
        taken["attn"] = 4 * SEQ + 16
        cos_t = carve("attn", "cos_t", L)
        sin_t = carve("attn", "sin_t", L)
        qpad = [carve("attn", f"qpad{m}", SEQ) for m in range(2)]
        kr = carve("attn", "kr", L)
        vt = carve("attn", "vt", TG * P)
        rt1 = carve("attn", "rt1", L)
        rt2 = carve("attn", "rt2", L)
        prob = [carve("attn", f"prob{m}", L) for m in range(2)]
        attn_t = carve("attn", "attn_t", TG * P)
        o_sb = carve("attn", "o_sb", SEQ)
        o_sq = carve("attn", "o_sq", SEQ)
        at_max = carve("attn", "at_max", 2)
        at_neg = carve("attn", "at_neg", 2)
        at_sum = carve("attn", "at_sum", 2)
        at_inv = carve("attn", "at_inv", 2)
        at_var = carve("attn", "at_var", 4)
        at_pow = carve("attn", "at_pow", 4)
        at_bc = carve("attn", "at_bc", 4 * P)
        post_b = carve("end", "post_b", D)
        x_again = [carve("end", f"x_again{b}", D) for b in range(2)]
        sq_junk = carve("end", "sq_junk", SEQ)
        sq_sum = carve("end", "sq_sum", 16)
        sq_tot = carve("end", "sq_tot", 8)
        xin = big[:].rearrange("p (t d) -> p t d", t=4)
        ymix = big[:].rearrange("p (k t) -> p k t", k=KT)
        proj_out = xin

        def c32v(name):
            at, w = C32[name]
            return c32[:, at:at + w]

        def c16v(k):
            return c16[:, k * P:(k + 1) * P]

        ident, ident16, neg16 = c32v("ident"), c16v(0), c16v(1)
        level_masks = c16[:, 2 * P:].rearrange("p (l t) -> p l t", l=LEVELS)

        tiles = [ctx.enter_context(nc.psum_tensor(f"tile{b}", [P, 1024], F32)) for b in range(2)]
        ma = ctx.enter_context(nc.psum_tensor("ma", [P, 1024], F32))
        mb = ctx.enter_context(nc.psum_tensor("mb", [P, 1024], F32))

        S = {}

        def s(name):
            if name not in S:
                S[name] = sem(name)
            return S[name]

        arrived = [sem(f"arrived{b}") for b in range(RING)]
        block = ctx.enter_context(nc.Block())

        INV_STEPS = 18
        CHAIN_STEPS = 11

        def inv_at(g, step):
            return 14 + 12 * g + 12 * step / INV_STEPS

        def chain_at(g, step):
            return 26 + 12 * g + 12 * step / CHAIN_STEPS

        def attn_stage_at(gn):
            return 11 if gn else 1

        def attn_at(gn, qi):
            return (16 if gn else 6) + 14 * qi

        def column(table, at, i):
            return table[:, at + i:at + i + 1] if isinstance(i, int) else table[:, bass.ds(i + at, 1)]

        def out_banks(n):
            a, b = (tiles[0], tiles[1]) if n % 2 == 0 else (ma, mb)
            return [a[:, 0:512], a[:, 512:1024], b[:, 0:512], b[:, 512:1024]]

        def squares(act, n):
            for t in range(4):
                act.wait_ge(s("out_taken"), 4 * n + t + 1)
                if n + t:
                    act.wait_ge(s("out_sq"), 4 * n + t)
                nc.scalar.activation(sq_junk, proj_out[:, t, n * SEQ:(n + 1) * SEQ], ACT.Square,
                                     accum_out=sq_sum[:, 4 * t + n:4 * t + n + 1]).then_inc(s("out_sq"), 1)

        def upto(gens, place):
            while True:
                due = [g for g in gens if g[1] is not None and g[1] <= place]
                if not due:
                    return
                g = min(due, key=lambda g: g[1])
                g[1] = next(g[0], None)

        def begin(*gens):
            return [[g, next(g, None)] for g in gens]

        def unit_of(i, k):
            return i * 16 + (UPT + k)

        class Steps:
            def __init__(self, eng, name):
                self.eng, self.sm, self.n = eng, s(name), 0

            def __call__(self, ins):
                self.n += 1
                ins.then_inc(self.sm, 1)
                self.eng.wait_ge(self.sm, self.n)

            def quiet(self, ins):
                self.n += 1
                ins.then_inc(self.sm, 1)

            def clear(self):
                if self.n:
                    self.eng.wait_ge(self.sm, self.n)
                    self.eng.sem_clear(self.sm)
                self.n = 0

        ITER = ([(0, "rwkv", None, False), (1, "rwkv", "rwkv", False)], (2, 8, "rwkv", "rwkv", True),
                [(8, "attn", "rwkv", True), (9, "attn", "attn", True)], (10, 16, "attn", "attn", False),
                [(16, None, "attn", False)])

        def iterations(eng, body):
            for part in ITER:
                if isinstance(part, list):
                    for i, proj, work, gn in part:
                        body(i, proj, work, gn)
                else:
                    lo, hi, proj, work, gn = part
                    with eng.Fori(lo, hi) as i:
                        body(i, proj, work, gn)

        @block.sync
        def _(sp):
            sp.dma_start(par_rows[0:25, :], rwkv_mu[0].rearrange("(r c) -> r c", c=P)).then_inc(s("par_in"), 16)
            for name, src in (("a0", rwkv_a0[0]), ("k_k", rwkv_k_k[0]), ("k_a", rwkv_k_a[0]), ("gn_w", rwkv_gn_w[0]),
                              ("gn_b", rwkv_gn_b[0]), ("r_k", rwkv_r_k[0].rearrange("h d -> (h d)")),
                              ("pre", pre_norm_w[0]), ("sub", subln_w[0])):
                rows = src.shape[0] // P
                sp.dma_start(par_rows[PC[name]:PC[name] + rows, :],
                             src.rearrange("(r c) -> r c", c=P)).then_inc(s("par_in"), 16)
            xs = x[0].rearrange("(t p) d -> p t d", p=P)
            for t in range(4):
                sp.dma_start(xin[:, t, :], xs[:, t, :]).then_inc(s("x_in"), 16)
            sp.dma_start(xm[0:META, :], meta_tokens).then_inc(s("meta_in"), 16)
            sp.dma_start(c32[:], c32_dram).then_inc(s("const_in"), 16)
            sp.dma_start(c16[:], c16_dram).then_inc(s("const_in"), 16)
            for n, v in enumerate((lam_q1, lam_k1, lam_q2, lam_k2)):
                sp.dma_start(lam_in[:, n * HD:(n + 1) * HD],
                             v[0:1, :].broadcast_to([P, HD])).then_inc(s("lam_in"), 16)

            def load_unit(slot, col, rows0):
                src = w_in[0, rows0:rows0 + UK * P, col].rearrange("(k p) c -> p k c", p=P)
                sp.dma_start(w_raw[:, slot, :].rearrange("p (k c) -> p k c", k=UK),
                             src).then_inc(arrived[slot], 16)

            for h in range(UPT):
                load_unit(h, slice(LORA_COL, LORA_COL + P), h * UK * P)

            def body(i, proj, work, gn):
                if proj is None:
                    return
                first = 0 if proj == "rwkv" else NP_
                for k in range(16):
                    if k == 4 and isinstance(i, int) and i == 9:
                        sp.wait_ge(s("s_taken"), NP_ * NC)
                        sp.wait_ge(s("y_done"), NP_ * NG)
                        sp.dma_start(cos_t, rope_dram[:, 0:L]).then_inc(s("rope_in"), 16)
                        sp.dma_start(sin_t, rope_dram[:, L:2 * L]).then_inc(s("rope_in"), 16)
                    lora_next = k == 7 and proj == "rwkv"
                    q, h = divmod(k, UPT)
                    at = i * P + (TILE_COLS[proj][q] - first * P)
                    col = bass.ds(at if isinstance(i, int) else sp.snap(at), P)
                    sp.wait_ge(s("lo_done"), unit_of(i, k) - (RING - 1))
                    if lora_next and isinstance(i, int) and i == 0:
                        sp.wait_ge(s("zeroed"), 1)
                    elif lora_next:
                        sp.wait_ge(s("z_added"), i)
                        sp.wait_ge(s("a_done"), i)
                    load_unit(h, col, h * UK * P)
                    if lora_next:
                        c = slice(0, P) if isinstance(i, int) and i == 0 else bass.ds(i * P, P)
                        sp.dma_start(wu[0:HD, :], rwkv_w_up[0, :, c]).then_inc(s("lora_w_in"), 16)
                        sp.dma_start(au[HD:P, :], rwkv_a_up[0, :, c]).then_inc(s("lora_w_in"), 16)
                        sp.dma_start(w0b, rwkv_w0[0:1, c].broadcast_to([P, P])).then_inc(s("lora_w_in"), 16)

            iterations(sp, body)
            def out_units(n):
                for k in range(KT):
                    src = w_out[0, k * P:(k + 1) * P, bass.ds(n * SEQ, SEQ)]
                    sp.wait_ge(s("lo_done"), n * KT + (UPT * N_TILES + k - (RING - 1)))
                    sp.dma_start(w_raw[:, k % RING, :], src
                                 ).then_inc(arrived[k % RING], 16)

            out_units(0)
            sp.wait_ge(s("o_made"), NP_)
            sp.dma_start(post_b, post_norm_w[0:1, :].broadcast_to([P, D])).then_inc(s("post_in"), 16)
            for b in range(2):
                sp.dma_start(x_again[b], xs[:, b, :]).then_inc(s(f"x_back{b}"), 16)
            with sp.Fori(1, 4) as n:
                out_units(n)
            outs = out[0].rearrange("(t p) d -> p t d", p=P)
            for t in range(4):
                sp.wait_ge(s("out_made"), t + 1)
                sp.dma_start(outs[:, t, :], proj_out[:, t, :]).then_inc(s("out_stored"), 16)
                if t < 2:
                    sp.dma_start(x_again[t], xs[:, t + 2, :]).then_inc(s(f"x_back{t}"), 16)
            sp.wait_ge(s("out_stored"), 64)

        @block.tensor
        def _(pe):
            mm = nc.tensor.matmul

            def product(n, o, lhs, rhs, first=True, last=True):
                return mm(o, lhs, rhs, start=first, stop=last)

            pe.wait_ge(s("const_in"), 32)
            pe.wait_ge(s("par_in"), 16 * 9)
            nc.tensor.transpose(ma[:, 0:N_PAR], par_rows[0:N_PAR, :], ident[0:N_PAR, 0:N_PAR]
                                ).then_inc(s("par_turned"), 1)
            pe.wait_ge(s("par_made"), 1)
            for t in range(5):
                pe.wait_ge(s("x_normed"), t + 1)
            for k in range(KT):
                o = (ma, mb)[k % 2]
                if k >= 2:
                    pe.wait_ge(s("hn_lo_made"), k - 1)
                nc.tensor.transpose(o[:, EDGE:EDGE + META], xm[0:META, k * P:(k + 1) * P], ident[0:META, 0:META])
                for t in range(4):
                    at = EDGE + META + t * P
                    if at < 512 < at + P:
                        n1 = 512 - at
                        nc.tensor.matmul(o[:, at:512], xin[:, t, k * P:(k + 1) * P], ident[:, 0:n1],
                                         start=True, stop=True)
                        last = nc.tensor.matmul(o[:, 512:at + P], xin[:, t, k * P:(k + 1) * P], ident[:, n1:P],
                                                start=True, stop=True)
                    else:
                        last = nc.tensor.transpose(o[:, at:at + P], xin[:, t, k * P:(k + 1) * P], ident)
                last.then_inc(s("x_turned"), 1)

            def feature_tile(o, slot, h, kk_, full):
                kt = h * UK + kk_
                cols = slice(kk_ * P, (kk_ + 1) * P)
                parts = (((EDGE, 0, L // 2), (512, L // 2, L // 2)) if full else ((0, META, SEQ),))
                for w, t in ((w_hi, hn_hi), (w_hi, hn_lo), (w_lo, hn_hi)):
                    for at, tok, n in parts:
                        last = mm(o[:, at:at + n], w[:, slot, cols], t[:, kt, tok:tok + n],
                                  start=(kt == 0 and w is w_hi and t is hn_hi),
                                  stop=(kt == KT - 1 and w is w_lo))
                return last

            pe.wait_ge(s("hn_lo_made"), KT)
            for h in range(UPT):
                pe.wait_ge(s("lo_done"), h + 1)
                for c in range(UK):
                    last = feature_tile(tiles[0], h, h, c, True)
                last.then_inc(s("unit_used"), 1)

            def gn_pe(i, work):
                n = i - 1
                yield 3
                if work == "rwkv":
                    pe.wait_ge(s("a_made"), i)
                pe.wait_ge(s("y_taken"), n * NG)
                pe.wait_ge(s("s_taken"), n * NC)
                mm(mb[:, 0:SEQ], c32v("centre"), ysum, start=True, stop=True).then_inc(s("centre_done"), 1)
                yield 5
                pe.wait_ge(s("centre_taken"), n * 2)
                for m in range(4):
                    last = mm(mb[:, 512 + 2 * m:514 + 2 * m], t512b[:, m * P:(m + 1) * P], c32v("heads_mean"),
                              start=True, stop=True)
                last.then_inc(s("var_done"), 1)
                yield 8
                pe.wait_ge(s("gn_spread"), n)
                for m in range(4):
                    last = nc.tensor.transpose(mb[:, 512 + m * P:512 + (m + 1) * P], t512b[:, m * P:(m + 1) * P],
                                               ident)
                last.then_inc(s("gn_turned"), 1)

            def stage_pe(i, gn):
                n = i
                yield 0
                pe.wait_ge(s("lora_made"), 1)
                pe.wait_ge(s("lora_w_in"), n * 48)
                if not (isinstance(i, int) and i == 1):
                    pe.wait_ge(s("inv_taken"), (n - 1) * NG)
                    pe.wait_ge(s("s_taken"), (n - 1) * NC)
                    pe.wait_ge(s("y_taken"), (n - 1) * NG)
                for m in range(TG):
                    last = mm(ma[:, m * P:(m + 1) * P], lora[:, m * P:(m + 1) * P], wu, start=True, stop=True)
                last.then_inc(s("z_done"), 1)
                mm(mb[:, 0:512], au, lora[:, 0:512], start=True, stop=True)
                mm(mb[:, 512:TP], au, lora[:, 512:TP], start=True, stop=True).then_inc(s("a_done"), 1)
                yield 4
                pe.wait_ge(s("z_made"), n)
                for m in range(TG):
                    last = mm(ma[:, m * P:(m + 1) * P], zt[:, m * P:(m + 1) * P],
                              c32v("tri0" if m == 0 else "tri"), start=True, stop=True)
                last.then_inc(s("c_done"), 1)
                yield 6
                pe.wait_ge(s("e_made"), n * 2)
                pe.wait_ge(s("sq_made"), n)
                for m in range(TG):
                    last = mm(ma[:, 2 * m:2 * m + 2], tmp[:, m * P:(m + 1) * P], c32v("heads"), start=True, stop=True)
                last.then_inc(s("n2_done"), 1)
                yield 9
                pe.wait_ge(s("kk_spread"), n)
                for m in range(TG):
                    last = nc.tensor.transpose(ma[:, m * P:(m + 1) * P], tmp[:, m * P:(m + 1) * P], ident)
                last.then_inc(s("kk_turned"), 1)
                yield 12
                pe.wait_ge(s("stage_r_made"), n)
                pe.wait_ge(s("a_made"), n)
                if gn:
                    pe.wait_ge(s("centre_taken"), (n - 1) * 2)
                mm(mb[:, 0:SEQ], c32v("block"), kk[:, 0:SEQ], start=True, stop=True).then_inc(s("bonus_done"), 1)

            def inv_pe(i, g):
                n = i * NG + (g + 1 - NG)
                cs = [g * GC + c for c in range(GC)]
                yield inv_at(g, 0)
                if g == 0:
                    pe.wait_ge(s("pads_made"), i)
                    pe.wait_ge(s("vpad_made"), i * 2)
                else:
                    pe.wait_ge(s("inv_taken"), n - 1)
                for f, pad in enumerate((bpad, kpad)):
                    for c in range(GC):
                        at = (f * GC + c) * P
                        last = nc.tensor.transpose(ma[:, at:at + P], pad[:, cs[c], :], ident)
                last.then_inc(s("bk_turned"), 1)
                yield inv_at(g, 1)
                pe.wait_ge(s("bk_taken"), n)
                for c in range(GC):
                    last = nc.tensor.transpose(ma[:, c * P:(c + 1) * P], vpad[:, cs[c], :], ident)
                last.then_inc(s("v_turned"), 1)
                for f, (pad, done, taken_) in enumerate(((bpad, "ab_done", "v_taken"), (kpad, "kb_done", "ab_taken"))):
                    yield inv_at(g, 2 + f)
                    pe.wait_ge(s(taken_), n)
                    for c in range(GC):
                        mm(ma[:, c * P:(c + 1) * P], pad[:, cs[c], :], apad[:, cs[c], :], start=True, stop=True)
                        last = mm(ma[:, 512 + c * CH:512 + (c + 1) * CH], pad[:, cs[c], :],
                                  rc[:, cs[c] * CH:(cs[c] + 1) * CH], start=True, stop=True)
                    last.then_inc(s(done), 1)
                yield inv_at(g, 5)
                pe.wait_ge(s("kb_taken"), n)
                pe.wait_ge(s("first_made"), n)
                bl = lambda v, c: v[:, c * P:(c + 1) * P]
                for c in range(GC):
                    last = mm(ma[:, c * P:(c + 1) * P], bl(xt16, c), ident16, start=True, stop=True)
                last.then_inc(s("t0_done"), 1)
                for l in range(1, LEVELS):
                    yield inv_at(g, 4 + 2 * l)
                    if l == 1:
                        pe.wait_ge(s("t0_taken"), n)
                    else:
                        pe.wait_ge(s("x_taken"), n * 5 + (l - 1 - 5))
                        pe.wait_ge(s("xt_taken"), n * 5 + (l - 1 - 5))
                    for c in range(GC):
                        mm(ma[:, 512 + c * P:512 + (c + 1) * P], lv[:, (l * GC + c) * P:(l * GC + c + 1) * P],
                           bl(x16, c), start=True, stop=False)
                        last = mm(ma[:, 512 + c * P:512 + (c + 1) * P], ident16, ident16, start=False, stop=True)
                    last.then_inc(s("zz_done"), 1)
                    yield inv_at(g, 5 + 2 * l)
                    pe.wait_ge(s("zz_taken"), n * 5 + (l - 5))
                    for c in range(GC):
                        last = mm(ma[:, 512 + c * P:512 + (c + 1) * P], bl(z16, c), bl(xt16, c),
                                  start=True, stop=True)
                    if l == LEVELS - 1:
                        last.then_inc(s("t_done"), 1)
                        continue
                    for c in range(GC):
                        last = mm(ma[:, c * P:(c + 1) * P], bl(xt16, c), bl(z16, c), start=True, stop=True)
                    last.then_inc(s("t_done"), 1)
                yield inv_at(g, 16)
                pe.wait_ge(s("xt_taken"), n * 5)
                for c in range(GC):
                    last = mm(ma[:, c * P:(c + 1) * P], bl(xt16, c), ident16, start=True, stop=True)
                last.then_inc(s("xx_done"), 1)
                yield inv_at(g, 16.5)
                pe.wait_ge(s("x_taken"), n * 5)
                for c in range(GC):
                    o = ma[:, 512 + c * P:512 + (c + 1) * P]
                    mm(o, ident16, ident16, start=True, stop=False)
                    mm(o, neg16, bl(x16, c), start=False, stop=False)
                    mm(o, bl(ab_hi, c), bl(x16, c), start=False, stop=False)
                    last = mm(o, bl(ab_lo, c), bl(x16, c), start=False, stop=True)
                last.then_inc(s("r_done"), 1)
                yield inv_at(g, 17)
                pe.wait_ge(s("r_taken"), n)
                for c in range(GC):
                    o = ma[:, c * P:(c + 1) * P]
                    mm(o, ident16, bl(xt16, c), start=True, stop=False)
                    last = mm(o, bl(r16, c), bl(xt16, c), start=False, stop=True)
                last.then_inc(s("inv_done"), 1)

            def chain_pe(i, g):
                b = g % 2
                n = i * NG + (g + 1 - NG)
                for c in range(GC):
                    ch = g * GC + c
                    m = i * NC + (ch + 1 - NC)
                    yield chain_at(g, 0.5 + 3 * c)
                    if c == 0:
                        pe.wait_ge(s("inv_taken"), n)
                        if g == 0:
                            pe.wait_ge(s("bonus_taken"), i)
                            pe.wait_ge(s("state_zeroed"), i)
                    if ch > 0:
                        pe.wait_ge(s("s_taken"), m - 1)
                        if g > 0 and c == 0:
                            pe.wait_ge(s("y_taken"), n - 1)
                    o = mb[:, 0:P]
                    vb = v_tok[b][:, c * P:(c + 1) * P]
                    mm(o, apad[:, ch, :], state, start=True, stop=False)
                    mm(o, ak_t[b][:, c * P:(c + 1) * P], vb, start=False, stop=True).then_inc(s("g_done"), 1)
                    yo = mb[:, 512 + c * CH:512 + (c + 1) * CH]
                    if ch > 0:
                        mm(yo, state, rc[:, ch * CH:(ch + 1) * CH], start=True, stop=False)
                        mm(yo, vb, rk_t[b][:, c * CH:(c + 1) * CH], start=False, stop=False)
                    yield chain_at(g, 1.5 + 3 * c)
                    pe.wait_ge(s("g_taken"), m)
                    mm(o, t_t[b][:, c * P:(c + 1) * P], g_sb, start=True, stop=True).then_inc(s("u_done"), 1)
                    yield chain_at(g, 2.5 + 3 * c)
                    pe.wait_ge(s("u_taken"), m)
                    mm(o, bk_tok[b][:, c * P:(c + 1) * P], u_sb, start=True, stop=False)
                    mm(o, bk_tok[b][:, (GC + c) * P:(GC + c + 1) * P], vb, start=False,
                       stop=True).then_inc(s("s_done"), 1)
                    if ch > 0:
                        last = mm(yo, u_sb, rb_t[b][:, c * CH:(c + 1) * CH], start=False, stop=True)
                        if c == GC - 1:
                            last.then_inc(s("y_done"), 1)

            def attn_stage_pe(i, gn):
                n = i - NP_
                at = attn_stage_at(gn)
                yield at
                if gn:
                    pe.wait_ge(s("y_made"), NP_)
                    pe.wait_ge(s("inv_taken"), NP_ * NG)
                else:
                    pe.wait_ge(s("o_made"), n - 1)
                pe.wait_ge(s("tile_freed"), i * 4 + 1)
                mm(ma[:, 0:SEQ], c32v("rot"), xk[:, 0:SEQ], start=True, stop=True).then_inc(s("rotq_done"), 1)
                yield at + 1
                h = L // 2
                mm(mb[:, EDGE:512], c32v("rot"), xv[:, 0:h], start=True, stop=True)
                mm(mb[:, 512:512 + h], c32v("rot"), xv[:, h:L], start=True, stop=True).then_inc(s("rotk_done"), 1)
                yield at + 3
                pe.wait_ge(s("roped"), n * 2 - 1)
                for m in range(4):
                    nc.tensor.transpose(ma[:, m * P:(m + 1) * P], xr[:, m * P:(m + 1) * P], ident)
                nc.tensor.transpose(ma[0:META, 512:512 + P], xr[:, 512:L], ident).then_inc(s("vt_turned"), 1)

            def attn_pe(i, gn):
                n = i - NP_
                for qi in range(4):
                    base = attn_at(gn, qi)
                    c = n * 4 + (qi - 3)
                    width = META + (qi + 1) * P
                    yield base
                    if qi == 0:
                        pe.wait_ge(s("roped"), n * 2)
                        pe.wait_ge(s("vt_taken"), n * 2)
                    else:
                        pe.wait_ge(s("at_taken"), c - 1)
                        pe.wait_ge(s("o_taken"), c - 1)
                        pe.wait_ge(s("o_squared"), c - 1)
                    for m, o in ((0, ma), (1, mb)):
                        lhs = qpad[m][:, qi * P:(qi + 1) * P]
                        if qi == 3:
                            mm(o[:, EDGE:512], lhs, kr[:, 0:L // 2], start=True, stop=True)
                            last = mm(o[:, 512:EDGE + L], lhs, kr[:, L // 2:L], start=True, stop=True)
                        else:
                            last = mm(o[:, 0:width], lhs, kr[:, 0:width], start=True, stop=True)
                        last.then_inc(s("score_done"), 1)
                    yield base + 7
                    pe.wait_ge(s("combined"), c)
                    for m in range(qi + 1):
                        nc.tensor.transpose(ma[:, m * P:(m + 1) * P], prob[0][:, m * P:(m + 1) * P], ident)
                    m = qi + 1
                    nc.tensor.transpose(ma[0:META, 512:512 + P], prob[0][:, m * P:m * P + META],
                                        ident).then_inc(s("at_turned"), 1)
                    yield base + 10
                    pe.wait_ge(s("at_taken"), c)
                    o = mb[:, 0:P]
                    for m in range(qi + 1):
                        mm(o, vt[:, m * P:(m + 1) * P], attn_t[:, m * P:(m + 1) * P], start=(m == 0), stop=False)
                    m = qi + 1
                    mm(o, vt[0:META, m * P:(m + 1) * P], attn_t[0:META, 4 * P:5 * P], start=False,
                       stop=True).then_inc(s("pv_done"), 1)
                at = attn_at(gn, 3)
                yield at + 12
                pe.wait_ge(s("o_squared"), n * 4)
                pe.wait_ge(s("o_taken"), n * 4)
                for m in range(4):
                    last = mm(mb[:, 512 + m:513 + m], o_sq[:, m * P:(m + 1) * P], c32v("mean"), start=True, stop=True)
                last.then_inc(s("ovar_done"), 1)
                yield at + 14
                pe.wait_ge(s("o_spread"), n)
                for m in range(4):
                    last = nc.tensor.transpose(ma[:, m * P:(m + 1) * P], at_bc[:, m * P:(m + 1) * P], ident)
                last.then_inc(s("o_turned"), 1)

            def body(i, proj, work, gn):
                gens = []
                if work == "rwkv":
                    gens = [stage_pe(i, gn)] + ([gn_pe(i, work)] if gn else [])
                    for g in range(NG):
                        gens += [chain_pe(i, g), inv_pe(i, g)]
                elif work == "attn":
                    gens = ([gn_pe(i, work)] if gn else []) + [attn_stage_pe(i, gn), attn_pe(i, gn)]
                gens = begin(*gens)
                for k in range(16):
                    q, h = divmod(k, UPT)
                    if proj is not None:
                        u = unit_of(i, k)
                        g = i * 4 + (q + 1)
                        if h == 0 and not (isinstance(i, int) and i == 0 and q == 0):
                            pe.wait_ge(s("tile_freed"), g - 1)
                        pe.wait_ge(s("lo_done"), u + 1)
                    for c in range(UK):
                        if proj is not None:
                            last = feature_tile(tiles[(q + 1) % 2], h, h, c, FULL[proj][q])
                            if c == UK - 1:
                                last.then_inc(s("unit_used"), 1)
                        upto(gens, k * UK + c)
                upto(gens, 1000)

            iterations(pe, body)

            pe.wait_ge(s("y_lo"), KT)
            pe.wait_ge(s("tile_freed"), N_TILES)
            pe.wait_ge(s("o_made"), NP_)
            for n in range(4):
                banks = out_banks(n)
                if n >= 2:
                    pe.wait_ge(s("out_taken"), 4 * (n - 1))
                for k in range(KT):
                    pe.wait_ge(s("lo_done"), UPT * N_TILES + n * KT + k + 1)
                    for t in range(4):
                        y = slice(t * P, (t + 1) * P)
                        mm(banks[t], hn_hi[:, k, y], w_hi[:, k % RING, :], start=(k == 0), stop=False)
                        mm(banks[t], hn_hi[:, k, y], w_lo[:, k % RING, :], start=False, stop=False)
                        last = mm(banks[t], hn_lo[:, k, y], w_hi[:, k % RING, :], start=False, stop=(k == KT - 1))
                    last.then_inc(s("unit_used"), 1)

        @block.scalar
        def _(act):
            A = nc.scalar.activation
            steps = Steps(act, "act_step")

            def split_hi(u, slot, turn):
                act.wait_ge(arrived[slot], turn * 16)
                if not (isinstance(u, int) and u < RING):
                    act.wait_ge(s("unit_used"), u - (RING - 1))
                nc.scalar.copy(w_hi[:, slot, :], w_raw[:, slot, :]).then_inc(s("hi_done"), 1)

            for t in range(5):
                act.wait_ge(s("x_in" if t < 4 else "meta_in"), 64 if t < 4 else 16)
                if t:
                    act.wait_ge(s("norm_sq"), t)
                v = xin[:, t, :] if t < 4 else xm[0:META, :]
                rows = P if t < 4 else META
                A(junk[0:rows, :], v, ACT.Square, accum_out=norm_s[0:rows, t:t + 1]).then_inc(s("norm_sq"), 1)
            for t in range(5):
                v = xin[:, t, :] if t < 4 else xm[0:META, :]
                rows = P if t < 4 else META
                act.wait_ge(s("norm_pow"), t + 1)
                A(v, v, ACT.Copy, scale=norm_s[0:rows, 10 + t:11 + t]).then_inc(s("x_normed"), 1)
            for u in range(AHEAD):
                split_hi(u, u, 1)
            act.wait_ge(s("lam_dots"), 2)
            A(lam_s[:, 2:4], lam_s[:, 0:2], ACT.Exp).then_inc(s("lam_exp"), 1)
            act.wait_ge(s("par_made"), 1)
            for k in range(KT):
                act.wait_ge(s("x_turned"), k + 1)
                o = (ma, mb)[k % 2]
                A(hn_hi[:, k, :], o[:, EDGE:EDGE + L], ACT.Copy,
                  scale=par[:, PC["pre"] + k:PC["pre"] + k + 1]).then_inc(s("hn_hi_made"), 1)
            split_hi(AHEAD, AHEAD, 1)
            for u in range(UPT, UPT + AHEAD):
                split_hi(u, u % RING, 2)
            act.wait_ge(s("unit_used"), UPT)
            act.wait_ge(s("zeroed"), 1)
            A(lora[:, PAD:TP], tiles[0][:, EDGE:EDGE + L], ACT.Copy, scale=om_mu[:, 24:25]).then_inc(s("lora_base"), 1)
            act.wait_ge(s("tile_freed"), 1)
            A(lora[0:HD, PAD:TP], lora[0:HD, PAD:TP], ACT.Tanh).then_inc(s("lora_made"), 1)

            def tile_act(i, proj, work):
                if proj == "rwkv":
                    for q, (xt, mu) in enumerate(((xk, 8), (xv, 16), (xr, 0))):
                        yield 16 * q + 15.5
                        act.wait_ge(s("unit_used"), i * 16 + (8 + 4 * q))
                        if work == "rwkv":
                            act.wait_ge(s("bonus_taken"), i)
                            act.wait_ge(s("pads_made"), i)
                        A(xt[:, PAD:TP], tiles[(q + 1) % 2][:, EDGE:EDGE + L], ACT.Copy,
                          scale=column(om_mu, mu, i)).then_inc(s("x_based"), 1)
                yield 63.5
                act.wait_ge(s("unit_used"), i * 16 + 20)
                A(tanh_g[:], tiles[0][:, 0:SEQ], ACT.Tanh, scale=0.5).then_inc(s("gate_tanh"), 1)

            def gn_act(i):
                n = i - 1
                yield 3.5
                act.wait_ge(s("centre_done"), n)
                act.wait_ge(s("tile_freed"), i * 4 + 1)
                A(t512, mb[:, 0:SEQ], ACT.Copy).then_inc(s("centre_taken"), 1)
                A(t512b, mb[:, 0:SEQ], ACT.Square).then_inc(s("centre_taken"), 1)
                yield 7
                act.wait_ge(s("gn_powed"), n)
                A(t512b.rearrange("p (m d) -> p m d", d=HD), gn_pow.unsqueeze(2).broadcast_to([P, 8, HD]),
                  ACT.Copy).then_inc(s("gn_spread"), 1)

            def stage_act(i, gn):
                n = i
                yield 0.5
                act.wait_ge(s("a_done"), n)
                act.wait_ge(s("zeroed"), 1)
                A(tha, mb[:, 0:TP], ACT.Tanh, scale=0.5, bias=column(half_a0, 0, i - 1)).then_inc(s("a_made"), 1)
                yield 1.5
                act.wait_ge(s("z_added"), n)
                A(zt, zt, ACT.Tanh, scale=0.5).then_inc(s("z_tanh"), 1)
                yield 5
                act.wait_ge(s("c_done"), n)
                cum = ma[:, 0:TP]
                A(ew3[:, :, 1:], cum.rearrange("p (c t) -> p c t", c=NC), ACT.Exp).then_inc(s("e_made"), 1)
                A(emi[:, 0:TP], cum, ACT.Exp, scale=-1.0).then_inc(s("e_made"), 1)
                act.wait_ge(s("tile_freed"), i * 4 - 2)
                A(tmp[:, 0:TP], xk[:], ACT.Square, scale=column(par, PC["k_k"], i - 1)).then_inc(s("sq_made"), 1)
                yield 8
                act.wait_ge(s("kk_powed"), n)
                A(tmp.rearrange("p (m d) -> p m d", d=HD), kk_pow.unsqueeze(2).broadcast_to([P, 2 * TG, HD]),
                  ACT.Copy).then_inc(s("kk_spread"), 1)
                yield 13
                act.wait_ge(s("tile_freed"), i * 4 - 1)
                for h in range(2):
                    A(vpad[h * HD:(h + 1) * HD, :, h * CH:(h + 1) * CH],
                      xv[h * HD:(h + 1) * HD, :].rearrange("p (c t) -> p c t", c=NC),
                      ACT.Copy).then_inc(s("vpad_made"), 1)
                if gn:
                    act.wait_ge(s("y_made"), n - 1)
                act.wait_ge(s("tile_freed"), i * 4 + 1)
                A(gate2[:], gate[:], ACT.Copy).then_inc(s("gate_moved"), 1)

            def inv_act(i, g):
                b = g % 2
                n = i * NG + (g + 1 - NG)
                W = GC * P
                yield inv_at(g, 0.5)
                act.wait_ge(s("bk_turned"), n)
                if not (isinstance(i, int) and n <= 2):
                    act.wait_ge(s("s_done"), (n - 2) * GC)
                A(bk_tok[b], ma[:, 0:2 * W], ACT.Copy).then_inc(s("bk_taken"), 1)
                yield inv_at(g, 5.5)
                act.wait_ge(s("t0_done"), n)
                A(x16, ma[:, 0:W], ACT.Copy).then_inc(s("t0_taken"), 1)
                for l in range(1, LEVELS):
                    yield inv_at(g, 4.5 + 2 * l)
                    act.wait_ge(s("zz_done"), n * 5 + (l - 5))
                    A(z16, ma[:, 512:512 + W], ACT.Copy).then_inc(s("zz_taken"), 1)
                    yield inv_at(g, 5.5 + 2 * l)
                    if l < LEVELS - 1:
                        act.wait_ge(s("t_done"), n * 5 + (l - 5))
                        A(x16, ma[:, 0:W], ACT.Copy).then_inc(s("x_taken"), 1)
                yield inv_at(g, 16.3)
                act.wait_ge(s("xx_done"), n)
                A(x16, ma[:, 0:W], ACT.Copy).then_inc(s("x_taken"), 1)
                yield inv_at(g, 16.7)
                act.wait_ge(s("r_done"), n)
                A(r16, ma[:, 512:512 + W], ACT.Copy).then_inc(s("r_taken"), 1)

            def chain_act(i, g):
                n = i * NG + (g + 1 - NG)
                for c in range(GC):
                    ch = g * GC + c
                    m = i * NC + (ch + 1 - NC)
                    yield chain_at(g, 0.8 + 3 * c)
                    if ch == 0:
                        act.wait_ge(s("state_zeroed"), i)
                    else:
                        act.wait_ge(s("s_taken"), m - 1)
                    A(state0, state, ACT.Copy, scale=ew3[:, ch, CH:CH + 1]).then_inc(s("s_scaled"), 1)
                yield chain_at(g, 9)
                act.wait_ge(s("y_done"), n)
                lo = max(0, g * GC * CH - CH)
                w = (g + 1) * GC * CH - CH - lo
                A(ysum[:, lo:lo + w], mb[:, 512 + GC * CH - w:512 + GC * CH], ACT.Copy).then_inc(s("y_taken"), 1)

            def attn_act(i, gn):
                n = i - NP_
                at = attn_stage_at(gn)
                yield at + 3.5
                act.wait_ge(s("vt_turned"), n)
                A(vt[:, 0:SEQ], ma[:, 0:SEQ], ACT.Copy).then_inc(s("vt_taken"), 1)
                A(vt[0:META, 512:512 + P], ma[0:META, 512:512 + P], ACT.Copy).then_inc(s("vt_taken"), 1)
                if gn:
                    act.wait_ge(s("y_made"), NP_)
                else:
                    act.wait_ge(s("o_made"), n - 1)
                act.wait_ge(s("tile_freed"), i * 4 + 1)
                A(gate2[:], gate[:], ACT.Copy).then_inc(s("gate_moved"), 1)
                for qi in range(4):
                    base = attn_at(gn, qi)
                    c = n * 4 + (qi - 3)
                    at = EDGE if qi == 3 else 0
                    width = META + (qi + 1) * P
                    for m, o in ((0, ma), (1, mb)):
                        yield base + 3 + m
                        act.wait_ge(s("neg_made"), c * 2 + (m - 1))
                        A(prob[m][:, 0:width], o[:, at:at + width], ACT.Exp, scale=HD ** -0.5,
                          bias=at_neg[:, m:m + 1], accum_out=at_sum[:, m:m + 1]).then_inc(s("exp_made"), 1)
                    yield base + 8
                    act.wait_ge(s("at_turned"), c)
                    w = (qi + 1) * P
                    steps.quiet(A(attn_t[:, 0:w], ma[:, 0:w], ACT.Copy))
                    A(attn_t[0:META, 512:512 + P], ma[0:META, 512:512 + P], ACT.Copy).then_inc(s("at_taken"), 1)
                    yield base + 11.5
                    act.wait_ge(s("o_taken"), c)
                    A(o_sq[:, qi * P:(qi + 1) * P], o_sb[:, qi * P:(qi + 1) * P], ACT.Square).then_inc(s("o_squared"), 1)
                at = attn_at(gn, 3)
                yield at + 13
                act.wait_ge(s("o_powed"), n)
                A(at_bc.rearrange("p (m d) -> p m d", d=P), at_pow.unsqueeze(2).broadcast_to([P, 4, P]),
                  ACT.Copy).then_inc(s("o_spread"), 1)

            def split_y_act():
                act.wait_ge(s("unit_used"), UPT * N_TILES)
                for k in range(KT):
                    yield 4 * k + 2 if k < KT - 1 else 200
                    act.wait_ge(s("y_made" if k < NP_ else "o_made"), k % NP_ + 1)
                    A(hn_hi[:, k, 0:SEQ], ymix[:, k, :], ACT.Copy).then_inc(s("y_hi"), 1)

            def body(i, proj, work, gn):
                gens = []
                if work == "rwkv":
                    gens = [stage_act(i, gn)] + ([gn_act(i)] if gn else [])
                    for g in range(NG):
                        gens += [chain_act(i, g), inv_act(i, g)]
                elif work == "attn":
                    gens = ([gn_act(i)] if gn else []) + [attn_act(i, gn)]
                if proj is not None:
                    gens.append(tile_act(i, proj, work))
                else:
                    gens.append(split_y_act())
                gens = begin(*gens)
                for k in range(16):
                    if proj is not None:
                        split_hi(unit_of(i, k + AHEAD), (k + AHEAD) % RING, i * 4 + (2 + (k + AHEAD) // UPT))
                    upto(gens, k * UK + 3)
                upto(gens, 1000)
                steps.clear()

            iterations(act, body)

            for n in range(4):
                for k in range(KT):
                    u = UPT * N_TILES + n * KT + k + AHEAD
                    if u < UPT * N_TILES + 4 * KT:
                        split_hi(u, u % RING, u // RING + 1)
                    if k == 3 and n > 0:
                        squares(act, n - 1)
            squares(act, 3)

        @block.gpsimd
        def _(pool):
            T = nc.gpsimd.tensor_tensor

            def split_lo(u, slot):
                pool.wait_ge(s("hi_done"), u + 1)
                T(w_lo[:, slot, :], w_raw[:, slot, :], w_hi[:, slot, :].bitcast(F32),
                  ALU.subtract).then_inc(s("lo_done"), 1)

            nc.gpsimd.memset(power[:], -0.5).then_inc(s("power_made"), 1)
            pool.wait_ge(s("power_made"), 1)
            for t in range(5):
                rows = P if t < 4 else META
                pool.wait_ge(s("norm_var"), t + 1)
                T(norm_s[0:rows, 10 + t:11 + t], norm_s[0:rows, 5 + t:6 + t], power[0:rows, 0:1],
                  ALU.pow).then_inc(s("norm_pow"), 1)
            for u in range(UPT + AHEAD):
                split_lo(u, u % RING)

            def powed(done, out_, in_, w, name, n):
                pool.wait_ge(s(done), n)
                T(out_[:, 0:w], in_[:, 0:w], power[:, 0:w], ALU.pow).then_inc(s(name), 1)

            def stage_pool(i):
                yield 7.5
                powed("n2_taken", kk_pow, kk_small, 2 * TG, "kk_powed", i)

            def gn_pool(i):
                yield 6
                powed("var_taken", gn_pow, gn_small, 8, "gn_powed", i - 1)

            def attn_pool(i, gn):
                yield attn_at(gn, 3) + 12.7
                powed("ovar_taken", at_pow, at_var, 4, "o_powed", i - NP_)

            def body(i, proj, work, gn):
                gens = []
                if work == "rwkv":
                    gens.append(stage_pool(i))
                if gn:
                    gens.append(gn_pool(i))
                if work == "attn":
                    gens.append(attn_pool(i, gn))
                gens = begin(*gens)
                for k in range(16):
                    if proj is not None:
                        split_lo(unit_of(i, k + AHEAD), (k + AHEAD) % RING)
                    upto(gens, k * UK + 3)
                upto(gens, 1000)

            iterations(pool, body)
            for u in range(UPT * N_TILES + AHEAD, UPT * N_TILES + 4 * KT):
                split_lo(u, u % RING)
            for t in range(4):
                powed("tot_made", sq_tot[:, 4 + t:5 + t], sq_tot[:, t:t + 1], 1, "tot_powed", t + 1)

        @block.vector
        def _(dve):
            V = nc.vector
            steps = Steps(dve, "dve_step")
            TT, STT, TS = V.tensor_tensor, V.scalar_tensor_tensor, V.tensor_scalar

            for t in range(5):
                rows = P if t < 4 else META
                dve.wait_ge(s("norm_sq"), t + 1)
                TS(norm_s[0:rows, 5 + t:6 + t], norm_s[0:rows, t:t + 1], 1.0 / D, EPS, ALU.mult,
                   ALU.add).then_inc(s("norm_var"), 1)
            dve.wait_ge(s("par_turned"), 1)
            V.tensor_copy(par[:], ma[:, 0:N_PAR]).then_inc(s("par_made"), 1)
            dve.wait_ge(s("lam_in"), 64)
            for n in range(2):
                steps(TT(lam_p, lam_in[:, 2 * n * HD:(2 * n + 1) * HD], lam_in[:, (2 * n + 1) * HD:(2 * n + 2) * HD],
                         ALU.mult))
                V.reduce_sum(lam_s[:, n:n + 1], lam_p, AX).then_inc(s("lam_dots"), 1)
                dve.wait_ge(s("lam_dots"), n + 1)
            dve.wait_ge(s("par_made"), 1)
            TS(om_mu[:], par[:, 0:25], -1.0, 1.0, ALU.mult, ALU.add)
            TS(half_a0[:], par[:, PC["a0"]:PC["a0"] + 8], 0.5, None, ALU.mult)
            steps(TS(half_ka[:], par[:, PC["k_a"]:PC["k_a"] + 8], 0.5, None, ALU.mult))
            TS(om_ka[:], half_ka[:], -1.0, 1.0, ALU.mult, ALU.add)
            TS(gate_sub[:], par[:, PC["sub"]:PC["sub"] + 1], 0.5 * (1.0 - LAM0), None, ALU.mult)
            dve.wait_ge(s("lam_exp"), 1)
            steps(TT(lam[:], lam_s[:, 2:3], lam_s[:, 3:4], ALU.subtract))
            TS(lam[:], lam[:], LAM0, None, ALU.add)
            for v in (xk, xv, xr, lora):
                V.memset(v[:, 0:PAD], 0.0)
            V.memset(lora[:, TP:TPX], 0.0)
            for k in range(KT):
                dve.wait_ge(s("hn_hi_made"), k + 1)
                o = (ma, mb)[k % 2]
                STT(hn_lo[:, k, :], o[:, EDGE:EDGE + L], par[:, PC["pre"] + k:PC["pre"] + k + 1],
                    hn_hi[:, k, :].bitcast(F32), ALU.mult, ALU.subtract).then_inc(s("hn_lo_made"), 1)
            for v in (apad, bpad, kpad, vpad):
                V.memset(v, 0.0)
            V.memset(wu[HD:P, :], 0.0)
            V.memset(au[0:HD, :], 0.0)
            V.memset(tmp[:, TP:TPX], 0.0)
            V.memset(ew3[:, :, 0:1], 1.0).then_inc(s("zeroed"), 1)
            dve.wait_ge(s("lora_base"), 1)
            STT(lora[:, PAD + 1:TP], tiles[0][:, EDGE:EDGE + L - 1], par[:, PC["mu_l"]:PC["mu_l"] + 1],
                lora[:, PAD + 1:TP], ALU.mult, ALU.add).then_inc(s("tile_freed"), 1)

            def tile_dve(i, proj, work):
                for q in range(3):
                    yield 16 * q + 15.6
                    o = tiles[(q + 1) % 2]
                    xt = (xk, xv, xr)[q]
                    if proj == "rwkv":
                        dve.wait_ge(s("x_based"), i * 3 + (q + 1))
                        STT(xt[:, PAD + 1:TP], o[:, EDGE:EDGE + L - 1], column(par, (8, 16, 0)[q], i),
                            xt[:, PAD + 1:TP], ALU.mult, ALU.add).then_inc(s("tile_freed"), 1)
                    else:
                        dve.wait_ge(s("unit_used"), i * 16 + (8 + 4 * q))
                        if work == "rwkv":
                            dve.wait_ge(s("vpad_made"), 2 * NP_)
                        else:
                            dve.wait_ge(s("vt_turned"), i - NP_)
                        full = FULL[proj][q]
                        n, at = (L, EDGE) if full else (SEQ, 0)
                        V.tensor_copy(xt[:, 0:n], o[:, at:at + n]).then_inc(s("tile_freed"), 1)
                yield 63.6
                dve.wait_ge(s("gate_tanh"), i + 1)
                STT(gate[:], tanh_g[:], 1.0, tiles[0][:, 0:SEQ], ALU.add, ALU.mult).then_inc(s("tile_freed"), 1)

            def gn_dve(i):
                n = i - 1
                yield 5.5
                dve.wait_ge(s("var_done"), n)
                TS(gn_small, mb[:, 512:520], GN_EPS, None, ALU.add).then_inc(s("var_taken"), 1)
                yield 9.2
                dve.wait_ge(s("gn_turned"), n)
                steps(TT(t512, t512, mb[:, 512:1024], ALU.mult))
                steps(TS(t512, t512, column(par, PC["gn_w"], i - 2), column(par, PC["gn_b"], i - 2),
                         ALU.mult, ALU.add))
                steps(TT(t512, t512, bonus_v, ALU.add))
                dst = ymix[:, i - 2, :] if isinstance(i, int) else ymix[:, bass.ds(i - 2, 1), :].rearrange(
                    "p a t -> p (a t)")
                dve.wait_ge(s("gate_moved"), n)
                STT(dst, gate2[:], 0.5, t512, ALU.mult, ALU.mult).then_inc(s("y_made"), 1)

            def stage_dve(i):
                n = i
                yield 1
                dve.wait_ge(s("z_done"), n)
                dve.wait_ge(s("lora_w_in"), n * 48)
                TT(zt.rearrange("p (g c) -> p g c", g=TG), ma[:, 0:TPX].rearrange("p (g c) -> p g c", g=TG),
                   w0b.unsqueeze(1).broadcast_to([P, TG, P]), ALU.add).then_inc(s("z_added"), 1)
                yield 2
                dve.wait_ge(s("z_tanh"), n)
                TS(zt, zt, 1.0, -0.5 * C_DECAY, ALU.add, ALU.mult).then_inc(s("z_made"), 1)
                yield 7
                dve.wait_ge(s("n2_done"), n)
                TS(kk_small, ma[:, 0:2 * TG], 1e-24, None, ALU.max).then_inc(s("n2_taken"), 1)
                yield 10
                dve.wait_ge(s("kk_turned"), n)
                steps(STT(kk, xk[:], column(par, PC["k_k"], i - 1), ma[:, 0:TP], ALU.mult, ALU.mult))
                dve.wait_ge(s("e_made"), n * 2)
                e0, e1 = ew3[:, :, 0:CH], ew3[:, :, 1:CH + 1]
                c3 = lambda v: v[:, 0:TP].rearrange("p (c t) -> p c t", c=NC)
                dve.wait_ge(s("a_made"), n)
                steps.quiet(STT(tmp[:, 0:TP], tha, 1.0, kk, ALU.add, ALU.mult))
                for h in range(2):
                    r = slice(h * HD, (h + 1) * HD)
                    STT(apad[r, :, h * CH:(h + 1) * CH], c3(kk)[r], -1.0, e0[r], ALU.mult, ALU.mult)
                steps(TS(kp, tha, column(half_ka, 0, i - 1), column(om_ka, 0, i - 1), ALU.mult, ALU.add))
                steps(TT(kp, kp, xk[:], ALU.mult))
                STT(kk[:, 0:SEQ], xr[:, CH:TP], column(par, PC["r_k"], i - 1), kp[:, CH:TP], ALU.mult,
                    ALU.mult).then_inc(s("stage_r_made"), 1)
                for h in range(2):
                    r = slice(h * HD, (h + 1) * HD)
                    STT(bpad[r, :, h * CH:(h + 1) * CH], c3(tmp)[r], 0.5, c3(emi)[r], ALU.mult, ALU.mult)
                    TT(kpad[r, :, h * CH:(h + 1) * CH], c3(kp)[r], c3(emi)[r], ALU.mult)
                TT(c3(rc), c3(xr), e1, ALU.mult).then_inc(s("pads_made"), 1)
                yield 13
                dve.wait_ge(s("bonus_done"), n)
                TT(bonus_v, mb[:, 0:SEQ], xv[:, CH:TP], ALU.mult).then_inc(s("bonus_taken"), 1)
                V.memset(state, 0.0).then_inc(s("state_zeroed"), 1)

            def inv_dve(i, g):
                b = g % 2
                n = i * NG + (g + 1 - NG)
                W = GC * P
                g3 = lambda v: v.rearrange("p (c t) -> p c t", c=GC)
                strict = c32v("strict").unsqueeze(1).broadcast_to([P, GC, P])
                incl = c32v("incl").unsqueeze(1).broadcast_to([P, GC, CH])
                yield inv_at(g, 1.5)
                dve.wait_ge(s("v_turned"), n)
                V.tensor_copy(v_tok[b], ma[:, 0:W]).then_inc(s("v_taken"), 1)
                yield inv_at(g, 2.5)
                dve.wait_ge(s("ab_done"), n)
                steps.quiet(TT(g3(ab32), g3(ma[:, 0:W]), strict, ALU.mult))
                TT(g3(rb_t[b]), g3(ma[:, 512:512 + GC * CH]), incl, ALU.mult).then_inc(s("ab_taken"), 1)
                dve.wait_ge(s("ab_taken"), n)
                steps(V.tensor_copy(ab_hi, ab32))
                l4 = lv.rearrange("p (l c t) -> p l c t", l=LEVELS, c=GC)
                for l in range(LEVELS):
                    ins = TT(l4[:, l], g3(ab_hi), level_masks[:, l, :].unsqueeze(1).broadcast_to([P, GC, P]), ALU.mult)
                    if l == 0:
                        steps.quiet(ins)
                steps(TT(ab_lo, ab32, ab_hi, ALU.subtract))
                TT(g3(xt16), l4[:, 0], ident16.unsqueeze(1).broadcast_to([P, GC, P]),
                   ALU.add).then_inc(s("first_made"), 1)
                yield inv_at(g, 3.5)
                dve.wait_ge(s("kb_done"), n)
                TT(g3(ak_t[b]), g3(ma[:, 0:W]), strict, ALU.mult)
                TT(g3(rk_t[b]), g3(ma[:, 512:512 + GC * CH]), incl, ALU.mult).then_inc(s("kb_taken"), 1)
                for l in range(1, LEVELS):
                    yield inv_at(g, 5.5 + 2 * l)
                    dve.wait_ge(s("t_done"), n * 5 + (l - 5))
                    V.tensor_copy(xt16, ma[:, 512:512 + W]).then_inc(s("xt_taken"), 1)
                yield inv_at(g, 17.5)
                dve.wait_ge(s("inv_done"), n)
                V.tensor_copy(t_t[b], ma[:, 0:W]).then_inc(s("inv_taken"), 1)

            def chain_dve(i, g):
                for c in range(GC):
                    ch = g * GC + c
                    m = i * NC + (ch + 1 - NC)
                    yield chain_at(g, 0.8 + 3 * c)
                    dve.wait_ge(s("g_done"), m)
                    V.tensor_copy(g_sb, mb[:, 0:P]).then_inc(s("g_taken"), 1)
                    yield chain_at(g, 1.8 + 3 * c)
                    dve.wait_ge(s("u_done"), m)
                    V.tensor_copy(u_sb, mb[:, 0:P]).then_inc(s("u_taken"), 1)
                    yield chain_at(g, 2.8 + 3 * c)
                    dve.wait_ge(s("s_done"), m)
                    dve.wait_ge(s("s_scaled"), m)
                    STT(state, mb[:, 0:P], ew3[:, ch, CH:CH + 1], state0, ALU.mult, ALU.add).then_inc(s("s_taken"), 1)

            def attn_dve(i, gn):
                n = i - NP_
                at = attn_stage_at(gn)
                yield at - 0.5
                if gn:
                    dve.wait_ge(s("s_taken"), NP_ * NC)
                    dve.wait_ge(s("y_taken"), NP_ * NG)
                    V.memset(qpad[0][HD:P, :], 0.0)
                    V.memset(qpad[1][0:HD, :], 0.0)
                    dve.wait_ge(s("rope_in"), 32)
                yield at + 0.5
                if not gn:
                    dve.wait_ge(s("roped"), n * 2 - 2)
                steps.quiet(TT(rt1[:, 0:SEQ], xk[:, 0:SEQ], cos_t[:, META:L], ALU.mult))
                dve.wait_ge(s("rotq_done"), n)
                steps(TT(rt2[:, 0:SEQ], ma[:, 0:SEQ], sin_t[:, META:L], ALU.mult))
                TT(qpad[0][0:HD, :], rt1[0:HD, 0:SEQ], rt2[0:HD, 0:SEQ], ALU.add)
                TT(qpad[1][HD:P, :], rt1[HD:P, 0:SEQ], rt2[HD:P, 0:SEQ], ALU.add).then_inc(s("roped"), 1)
                yield at + 1.5
                dve.wait_ge(s("roped"), n * 2 - 1)
                steps.quiet(TT(rt1, xv[:, 0:L], cos_t, ALU.mult))
                dve.wait_ge(s("rotk_done"), n)
                steps(TT(rt2, mb[:, EDGE:EDGE + L], sin_t, ALU.mult))
                TT(kr, rt1, rt2, ALU.add).then_inc(s("roped"), 1)
                for qi in range(4):
                    base = attn_at(gn, qi)
                    c = n * 4 + (qi - 3)
                    at = EDGE if qi == 3 else 0
                    width = META + (qi + 1) * P
                    for m, o in ((0, ma), (1, mb)):
                        yield base + 1 + m
                        dve.wait_ge(s("score_done"), c * 2 + (m - 1))
                        d = o[:, at + width - P:at + width]
                        steps(TT(d, d, c32v("causal"), ALU.add))
                        steps(V.reduce_max(at_max[:, m:m + 1], o[:, at:at + width], AX))
                        TS(at_neg[:, m:m + 1], at_max[:, m:m + 1], -HD ** -0.5, None,
                           ALU.mult).then_inc(s("neg_made"), 1)
                    yield base + 5
                    dve.wait_ge(s("exp_made"), c * 2)
                    steps(V.reciprocal(at_inv, at_sum))
                    steps(TT(at_inv[:, 1:2], at_inv[:, 1:2], lam[:], ALU.mult))
                    steps(TS(prob[1][:, 0:width], prob[1][:, 0:width], at_inv[:, 1:2], None, ALU.mult))
                    STT(prob[0][:, 0:width], prob[0][:, 0:width], at_inv[:, 0:1], prob[1][:, 0:width], ALU.mult,
                        ALU.subtract).then_inc(s("combined"), 1)
                    yield base + 11
                    dve.wait_ge(s("pv_done"), c)
                    V.tensor_copy(o_sb[:, qi * P:(qi + 1) * P], mb[:, 0:P]).then_inc(s("o_taken"), 1)
                at = attn_at(gn, 3)
                yield at + 12.5
                dve.wait_ge(s("ovar_done"), n)
                TS(at_var, mb[:, 512:516], SUB_EPS, None, ALU.add).then_inc(s("ovar_taken"), 1)
                yield at + 14.5
                dve.wait_ge(s("o_turned"), n)
                steps(TT(o_sb, o_sb, ma[:, 0:SEQ], ALU.mult))
                dve.wait_ge(s("gate_moved"), i)
                dst = ymix[:, i - 1, :] if isinstance(i, int) else ymix[:, bass.ds(i - 1, 1), :].rearrange(
                    "p a t -> p (a t)")
                STT(dst, gate2[:], gate_sub[:], o_sb, ALU.mult, ALU.mult).then_inc(s("o_made"), 1)

            def split_y_dve():
                for k in range(KT):
                    yield 4 * k + 2.2 if k < KT - 1 else 200
                    dve.wait_ge(s("y_hi"), k + 1)
                    TT(hn_lo[:, k, 0:SEQ], ymix[:, k, :], hn_hi[:, k, 0:SEQ].bitcast(F32),
                       ALU.subtract).then_inc(s("y_lo"), 1)

            def body(i, proj, work, gn):
                gens = []
                if work == "rwkv":
                    gens = [stage_dve(i)] + ([gn_dve(i)] if gn else [])
                    for g in range(NG):
                        gens += [chain_dve(i, g), inv_dve(i, g)]
                elif work == "attn":
                    gens = ([gn_dve(i)] if gn else []) + [attn_dve(i, gn)]
                gens.append(tile_dve(i, proj, work) if proj is not None else split_y_dve())
                upto(begin(*gens), 1000)
                steps.clear()

            steps.clear()
            iterations(dve, body)

            for n in range(4):
                dve.wait_ge(s("unit_used"), UPT * N_TILES + KT * (n + 1))
                for t in range(4):
                    V.tensor_copy(proj_out[:, t, n * SEQ:(n + 1) * SEQ], out_banks(n)[t]).then_inc(s("out_taken"), 1)
            for t in range(4):
                dve.wait_ge(s("out_sq"), 16)
                steps(V.reduce_sum(sq_tot[:, t:t + 1], sq_sum[:, 4 * t:4 * t + 4], AX))
                TS(sq_tot[:, t:t + 1], sq_tot[:, t:t + 1], 1.0 / D, EPS, ALU.mult, ALU.add).then_inc(s("tot_made"), 1)
            dve.wait_ge(s("post_in"), 16)
            for t in range(4):
                dve.wait_ge(s("tot_powed"), t + 1)
                dve.wait_ge(s(f"x_back{t % 2}"), 16 * (t // 2 + 1))
                steps(STT(proj_out[:, t, :], proj_out[:, t, :], sq_tot[:, 4 + t:5 + t], post_b, ALU.mult, ALU.mult))
                TT(proj_out[:, t, :], proj_out[:, t, :], x_again[t % 2], ALU.add).then_inc(s("out_made"), 1)


INPUTS = ("x", "meta_tokens", "pre_norm_w", "w_in", "rwkv_mu", "rwkv_w0", "rwkv_w_up", "rwkv_a0", "rwkv_a_up",
          "rwkv_k_k", "rwkv_k_a", "rwkv_r_k", "rwkv_gn_w", "rwkv_gn_b", "diff_lam_q1", "diff_lam_k1",
          "diff_lam_q2", "diff_lam_k2", "diff_subln_w", "w_out", "post_norm_w")


def kernel(**inputs):
    import concourse.bacc as bacc
    from concourse.bass_utils import run_bass_kernel_spmd

    nc = bacc.Bacc("TRN2", target_bir_lowering=False, num_devices=1)
    arrays, args = {}, []
    tables = dict(zip(("table_f32", "table_f16", "table_rope"), constants()))
    for name, a in [(n, inputs[n]) for n in INPUTS] + list(tables.items()):
        a = np.ascontiguousarray(a)
        arrays[name] = a
        args.append(nc.dram_tensor(name, a.shape, mybir.dt.from_np(a.dtype), kind="ExternalInput").ap())
    out = nc.dram_tensor("out", (1, SEQ, D), F32, kind="ExternalOutput").ap()
    hybrid_layer(nc, *args, out)
    r = run_bass_kernel_spmd(nc, [arrays], core_ids=[0])
    return r.results[0]["out"]
```

```python
import math

import numpy as np
import concourse.bass as bass
from concourse import mybir
from contextlib import ExitStack

F32 = mybir.dt.float32
F32R = mybir.dt.float32r
F16 = mybir.dt.float16
ALU = mybir.AluOpType
ACT = mybir.ActivationFunctionType
AX = mybir.AxisListType.X

P = 128
D = 2048
SEQ = 512
META = 16
L = SEQ + META
KT = D // P
RW = 1024
NP_ = RW // P
HD = 64
CH = 64
PAD = CH - META
TP = PAD + L
NC = TP // CH
TG = 5
TPX = TG * P
GC = 3
NG = NC // GC
UK = 4
UPT = KT // UK
RING = 4
AHEAD = 3
LORA_COL = 3 * RW
G_COL = LORA_COL + P
ATT_COL = G_COL + RW
TILE_COLS = {"rwkv": (RW, 2 * RW, 0, G_COL),
             "attn": (ATT_COL, ATT_COL + RW, ATT_COL + 2 * RW, ATT_COL + 3 * RW)}
FULL = {"rwkv": (True, True, True, False), "attn": (False, True, True, False)}
N_TILES = 1 + 4 * 2 * NP_
SUB = 64
EDGE = 248
EPS, GN_EPS, SUB_EPS = 1e-6, 64e-5, 1e-5
LAM0 = 0.8 - 0.6 * math.exp(0.0)
C_DECAY = math.exp(-0.5)
NEG = -3.0e38
PC = {}
_n = 0
for _name, _rows in (("mu_r", 8), ("mu_k", 8), ("mu_v", 8), ("mu_l", 1), ("a0", 8), ("k_k", 8), ("k_a", 8),
                     ("r_k", 8), ("gn_w", 8), ("gn_b", 8), ("pre", 16), ("sub", 1)):
    PC[_name] = _n
    _n += _rows
N_PAR = _n


def constants():
    i = np.arange(P)
    s, t = i[:, None], i[None, :]
    same = (s // CH) == (t // CH)
    ident = (s == t).astype(np.float32)
    strict = (same & (s < t)).astype(np.float32)
    incl = ((s % CH) <= np.arange(CH)[None, :]).astype(np.float32)
    tri = (same & (s <= t)).astype(np.float32)
    tri0 = tri * (s >= PAD)
    centre = ident - same / CH
    block = same.astype(np.float32)
    heads = np.stack([(i < HD), (i >= HD)], 1).astype(np.float32)
    rot = np.zeros((P, P), np.float32)
    for m in range(P):
        if m % HD < HD // 2:
            rot[m + HD // 2, m] = -1.0
        else:
            rot[m - HD // 2, m] = 1.0
    causal = np.where(t <= s, 0.0, NEG).astype(np.float32)
    f32 = np.concatenate([ident, strict, incl, tri0, tri, centre, block, heads, heads / HD,
                          np.full((P, 1), 1.0 / P), rot, causal], 1).astype(np.float32)
    levels = [ident, -ident]
    m = 1
    while m < CH:
        levels.append(same & ((s // (2 * m)) == (t // (2 * m))) & ((s // m) % 2 == 0) & ((t // m) % 2 == 1))
        m *= 2
    f16 = np.concatenate(levels, 1).astype(np.float16)
    pos = np.arange(L, dtype=np.float32)
    inv = (np.float32(10000.0) ** (-np.arange(0, HD, 2, dtype=np.float32) / np.float32(HD))).astype(np.float32)
    ang = (pos[:, None] * inv[None, :]).astype(np.float32)
    ang = np.concatenate([ang] * 4, 1).T
    rope = np.concatenate([np.cos(ang), np.sin(ang)], 1).astype(np.float32)
    return f32, f16, rope


LEVELS = 6
C32 = {}
_n = 0
for _name, _w in (("ident", P), ("strict", P), ("incl", CH), ("tri0", P), ("tri", P), ("centre", P), ("block", P),
                  ("heads", 2), ("heads_mean", 2), ("mean", 1), ("rot", P), ("causal", P)):
    C32[_name] = (_n, _w)
    _n += _w
C32_W = _n


def hybrid_layer(nc, x, meta_tokens, pre_norm_w, w_in, rwkv_mu, rwkv_w0, rwkv_w_up, rwkv_a0, rwkv_a_up,
                 rwkv_k_k, rwkv_k_a, rwkv_r_k, rwkv_gn_w, rwkv_gn_b, lam_q1, lam_k1, lam_q2, lam_k2,
                 subln_w, w_out, post_norm_w, c32_dram, c16_dram, rope_dram, out):
    ctx = ExitStack()
    with ctx:
        def sb(name, shape, dt=F32):
            return ctx.enter_context(nc.sbuf_tensor(name, shape, dt))

        def sem(name):
            return ctx.enter_context(nc.semaphore(name))

        hn_hi = sb("hn_hi", [P, KT, L], F32R)
        hn_lo = sb("hn_lo", [P, KT, L], F32R)
        w_raw = sb("w_raw", [P, RING, UK * P])
        w_hi = sb("w_hi", [P, RING, UK * P], F32R)
        w_lo = sb("w_lo", [P, RING, UK * P], F32R)
        big = sb("big", [P, 4 * D])
        c32 = sb("c32", [P, C32_W])
        c16 = sb("c16", [P, (2 + LEVELS) * P], F16)
        par = sb("par", [P, N_PAR])
        om_mu = sb("om_mu", [P, 25])
        half_a0 = sb("half_a0", [P, 8])
        half_ka = sb("half_ka", [P, 8])
        om_ka = sb("om_ka", [P, 8])
        gate_sub = sb("gate_sub", [P, 1])
        lam = sb("lam", [P, 1])
        power = sb("power", [P, 16])
        lora = sb("lora", [P, TPX])
        xk = sb("xk", [P, TP])
        xv = sb("xv", [P, TP])
        xr = sb("xr", [P, TP])
        gate = sb("gate", [P, SEQ])
        gate2 = sb("gate2", [P, SEQ])
        tanh_g = sb("tanh_g", [P, SEQ])
        t512b = tanh_g[:]
        ARENA = 16118
        arena = sb("arena", [P, ARENA])
        taken = {}

        def carve(stage, name, n, dt=F32):
            at = taken.get(stage, 0)
            words = n if dt is F32 else n // 2
            taken[stage] = at + words
            assert taken[stage] <= ARENA, (stage, name, taken[stage])
            v = arena[:, at:at + words]
            return v if dt is F32 else v.bitcast(dt)

        ysum = carve("rwkv", "ysum", SEQ)
        t512 = carve("rwkv", "t512", SEQ)
        gn_small = carve("rwkv", "gn_small", 8)
        gn_pow = carve("rwkv", "gn_pow", 8)
        wu = carve("rwkv", "wu", P)
        au = carve("rwkv", "au", P)
        w0b = carve("rwkv", "w0b", P)
        ew = carve("rwkv", "ew", NC * (CH + 1))
        ew3 = ew.rearrange("p (c t) -> p c t", c=NC)
        w_end = carve("rwkv", "w_end", NC)
        kk_small = carve("rwkv", "kk_small", 2 * TG)
        kk_pow = carve("rwkv", "kk_pow", 2 * TG)
        rkp = carve("rwkv", "rkp", TPX)
        tmp = carve("rwkv", "tmp", TPX)
        zt = tmp
        rc = carve("rwkv", "rc", TP)
        apad = carve("rwkv", "apad", NC * P).rearrange("p (c t) -> p c t", c=NC)
        bpad = carve("rwkv", "bpad", NC * P).rearrange("p (c t) -> p c t", c=NC)
        kpad = carve("rwkv", "kpad", NC * P).rearrange("p (c t) -> p c t", c=NC)
        vpad = carve("rwkv", "vpad", NC * P).rearrange("p (c t) -> p c t", c=NC)

        def two(name, n, dt=F32):
            return [carve("rwkv", f"{name}{b}", n, dt) for b in range(2)]

        bk_tok = two("bk_tok", 2 * GC * P)
        v_tok = two("v_tok", GC * P)
        ak_t = two("ak_t", GC * P)
        rb_t = two("rb_t", GC * CH)
        rk_t = two("rk_t", GC * CH)
        t_t = two("t_t", GC * P)
        state = carve("rwkv", "state", P)
        state0 = carve("rwkv", "state0", P)
        g_sb = carve("rwkv", "g_sb", P)
        u_sb = carve("rwkv", "u_sb", P)
        shared = taken["rwkv"]
        emi = carve("rwkv", "emi", TPX)
        tha = carve("rwkv", "tha", TP)
        kk = carve("rwkv", "kk", TP)
        kp = carve("rwkv", "kp", TP)
        taken["rwkv"] = shared
        ab32 = carve("rwkv", "ab32", GC * P)
        ab_hi = carve("rwkv", "ab_hi", GC * P, F16)
        ab_lo = carve("rwkv", "ab_lo", GC * P, F16)
        lv = carve("rwkv", "lv", LEVELS * GC * P, F16)
        x16 = carve("rwkv", "x16", GC * P, F16)
        xt16 = carve("rwkv", "xt16", GC * P, F16)
        z16 = carve("rwkv", "z16", GC * P, F16)
        r16 = z16
        taken["start"] = 3 * SEQ + TPX
        xm = carve("start", "xm", D)
        par_rows = carve("start", "par_rows", P)
        lam_in = carve("start", "lam_in", 4 * HD)
        lam_p = carve("start", "lam_p", HD)
        lam_s = carve("start", "lam_s", 4)
        norm_s = carve("start", "norm_s", 16)
        junk = carve("start", "junk", D)
        norm_d = carve("start", "norm_d", 5 * P)
        taken["attn"] = 2 * SEQ + 16
        cos_t = carve("attn", "cos_t", L)
        sin_t = carve("attn", "sin_t", L)
        qpad = [carve("attn", f"qpad{m}", SEQ) for m in range(2)]
        kr = carve("attn", "kr", L)
        vt = carve("attn", "vt", TG * P)
        rt1 = carve("attn", "rt1", L)
        rt2 = carve("attn", "rt2", L)
        prob = [carve("attn", f"prob{m}", L) for m in range(2)]
        attn_t = carve("attn", "attn_t", TG * P)
        o_sb = carve("attn", "o_sb", SEQ)
        o_sq = carve("attn", "o_sq", SEQ)
        at_max = carve("attn", "at_max", 2)
        at_neg = carve("attn", "at_neg", 2)
        at_sum = carve("attn", "at_sum", 2)
        at_inv = carve("attn", "at_inv", 2)
        at_var = carve("attn", "at_var", 4)
        at_pow = carve("attn", "at_pow", 4)
        at_bc = carve("attn", "at_bc", 4 * P)
        post_b = carve("end", "post_b", D)
        x_again = [carve("end", f"x_again{b}", D) for b in range(4)]
        sq_junk = carve("end", "sq_junk", SEQ)
        sq_sum = carve("end", "sq_sum", 16)
        sq_tot = carve("end", "sq_tot", 8)
        xin = big[:].rearrange("p (t d) -> p t d", t=4)
        ymix = big[:].rearrange("p (k t) -> p k t", k=KT)
        proj_out = xin

        def c32v(name):
            at, w = C32[name]
            return c32[:, at:at + w]

        def c16v(k):
            return c16[:, k * P:(k + 1) * P]

        ident, ident16, neg16 = c32v("ident"), c16v(0), c16v(1)
        level_masks = c16[:, 2 * P:].rearrange("p (l t) -> p l t", l=LEVELS)

        tiles = [ctx.enter_context(nc.psum_tensor(f"tile{b}", [P, 1024], F32)) for b in range(2)]
        ma = ctx.enter_context(nc.psum_tensor("ma", [P, 1024], F32))
        mb = ctx.enter_context(nc.psum_tensor("mb", [P, 1024], F32))

        S = {}

        def s(name):
            if name not in S:
                S[name] = sem(name)
            return S[name]

        arrived = [sem(f"arrived{b}") for b in range(RING)]
        block = ctx.enter_context(nc.Block())

        INV_STEPS = 19
        CHAIN_STEPS = 11
        LATE_SPAN = 8
        INV_AT, INV_SPAN = 11, 17.5
        BONUS_AT = 24
        LORA_LAG = 4
        GN_AT = 12

        def inv_at(g, step):
            return INV_AT + INV_SPAN * g + INV_SPAN * step / INV_STEPS

        def chain_at(g, step, late):
            if late:
                return 4.5 + LATE_SPAN * step / CHAIN_STEPS
            return INV_AT + INV_SPAN * (g + 1) + 0.5 + 16 * step / CHAIN_STEPS

        def groups_so_far(i, g, late=0):
            return i * NG + (g + 1 - NG * (1 + late))

        def chunks_so_far(i, ch, late=0):
            return i * NC + (ch + 1 - NC * (1 + late))

        def rwkv_work(i, work, gn, stage, group_norm, inverse, chain):
            gens = []
            if gn:
                gens += [chain(i, NG - 1, 1, work, gn), group_norm(i, work)]
            if work == "rwkv":
                gens.append(stage(i, gn))
                for g in range(NG):
                    if g < NG - 1:
                        gens.append(chain(i, g, 0, work, gn))
                    gens.append(inverse(i, g))
            return gens

        def attn_stage_at(gn):
            return 24 if gn else 1

        def attn_at(gn, qi):
            return 28 + 11 * qi if gn else 6 + 14 * qi

        def mixed(i):
            return ymix[:, i, :] if isinstance(i, int) else ymix[:, bass.ds(i, 1), :].rearrange("p a t -> p (a t)")

        def column(table, at, i):
            return table[:, at + i:at + i + 1] if isinstance(i, int) else table[:, bass.ds(i + at, 1)]

        def out_banks(n):
            a, b = (tiles[0], tiles[1]) if n % 2 == 0 else (ma, mb)
            return [a[:, 0:512], a[:, 512:1024], b[:, 0:512], b[:, 512:1024]]

        def squares(act, n):
            act.wait_ge(s("unit_used"), UPT * N_TILES + KT * (n + 1))
            for t in range(4):
                if n + t:
                    act.wait_ge(s("out_sq"), 4 * n + t)
                nc.scalar.activation(sq_junk, out_banks(n)[t], ACT.Square,
                                     accum_out=sq_sum[:, 4 * t + n:4 * t + n + 1]).then_inc(s("out_sq"), 1)

        def upto(gens, place):
            while True:
                due = [g for g in gens if g[1] is not None and g[1] <= place]
                if not due:
                    return
                g = min(due, key=lambda g: g[1])
                g[1] = next(g[0], None)

        def begin(*gens):
            return [[g, next(g, None)] for g in gens]

        def unit_of(i, k):
            return i * 16 + (UPT + k)

        class Steps:
            def __init__(self, eng, name):
                self.eng, self.sm, self.n = eng, s(name), 0

            def __call__(self, ins):
                self.n += 1
                ins.then_inc(self.sm, 1)
                self.eng.wait_ge(self.sm, self.n)

            def quiet(self, ins):
                self.n += 1
                ins.then_inc(self.sm, 1)

            def clear(self):
                if self.n:
                    self.eng.wait_ge(self.sm, self.n)
                    self.eng.sem_clear(self.sm)
                self.n = 0

        ITER = ([(0, "rwkv", None, False), (1, "rwkv", "rwkv", False)], (2, 8, "rwkv", "rwkv", True),
                [(8, "attn", "rwkv", True), (9, "attn", "attn", True)], (10, 16, "attn", "attn", False),
                [(16, None, "attn", False)])

        def iterations(eng, body):
            for part in ITER:
                if isinstance(part, list):
                    for i, proj, work, gn in part:
                        body(i, proj, work, gn)
                else:
                    lo, hi, proj, work, gn = part
                    with eng.Fori(lo, hi) as i:
                        body(i, proj, work, gn)

        @block.sync
        def _(sp):
            xs = x[0].rearrange("(t p) d -> p t d", p=P)
            sp.dma_start(xm[0:META, :], meta_tokens).then_inc(s("meta_in"), 16)
            sp.dma_start(xin[:, 0, :], xs[:, 0, :]).then_inc(s("x_in0"), 16)
            sp.dma_start(c32[:], c32_dram).then_inc(s("const_in"), 16)
            for t in range(1, 4):
                sp.dma_start(xin[:, t, :], xs[:, t, :]).then_inc(s(f"x_in{t}"), 16)
            sp.dma_start(par_rows[0:25, :], rwkv_mu[0].rearrange("(r c) -> r c", c=P)).then_inc(s("par_in"), 16)
            for name, src in (("a0", rwkv_a0[0]), ("k_k", rwkv_k_k[0]), ("k_a", rwkv_k_a[0]), ("gn_w", rwkv_gn_w[0]),
                              ("gn_b", rwkv_gn_b[0]), ("r_k", rwkv_r_k[0].rearrange("h d -> (h d)")),
                              ("pre", pre_norm_w[0]), ("sub", subln_w[0])):
                rows = src.shape[0] // P
                sp.dma_start(par_rows[PC[name]:PC[name] + rows, :],
                             src.rearrange("(r c) -> r c", c=P)).then_inc(s("par_in"), 16)

            def load_unit(slot, col, rows0):
                src = w_in[0, rows0:rows0 + UK * P, col].rearrange("(k p) c -> p k c", p=P)
                sp.dma_start(w_raw[:, slot, :].rearrange("p (k c) -> p k c", k=UK),
                             src).then_inc(arrived[slot], 16)

            for h in range(UPT):
                load_unit(h, slice(LORA_COL, LORA_COL + P), h * UK * P)
            sp.dma_start(c16[:], c16_dram).then_inc(s("const16_in"), 16)
            for n, v in enumerate((lam_q1, lam_k1, lam_q2, lam_k2)):
                sp.dma_start(lam_in[:, n * HD:(n + 1) * HD],
                             v[0:1, :].broadcast_to([P, HD])).then_inc(s("lam_in"), 16)

            def body(i, proj, work, gn):
                if proj is None:
                    return
                first = 0 if proj == "rwkv" else NP_
                for k in range(16):
                    if k == 10 and isinstance(i, int) and i == 9:
                        sp.wait_ge(s("s_taken"), NP_ * NC)
                        sp.wait_ge(s("y_done"), NP_ * NG)
                        sp.dma_start(cos_t, rope_dram[:, 0:L]).then_inc(s("rope_in"), 16)
                        sp.dma_start(sin_t, rope_dram[:, L:2 * L]).then_inc(s("rope_in"), 16)
                    lora_next = k == 7 and proj == "rwkv"
                    q, h = divmod(k, UPT)
                    at = i * P + (TILE_COLS[proj][q] - first * P)
                    col = bass.ds(at if isinstance(i, int) else sp.snap(at), P)
                    sp.wait_ge(s("lo_done"), unit_of(i, k) - (RING - 1))
                    if lora_next and isinstance(i, int) and i == 0:
                        sp.wait_ge(s("zeroed"), 1)
                    elif lora_next:
                        sp.wait_ge(s("z_added"), i)
                        sp.wait_ge(s("a_done"), i)
                    load_unit(h, col, h * UK * P)
                    if lora_next:
                        c = slice(0, P) if isinstance(i, int) and i == 0 else bass.ds(i * P, P)
                        sp.dma_start(wu[0:HD, :], rwkv_w_up[0, :, c]).then_inc(s("lora_w_in"), 16)
                        sp.dma_start(au[HD:P, :], rwkv_a_up[0, :, c]).then_inc(s("lora_w_in"), 16)
                        sp.dma_start(w0b, rwkv_w0[0:1, c].broadcast_to([P, P])).then_inc(s("lora_w_in"), 16)

            iterations(sp, body)
            def out_units(n, features=range(KT)):
                for k in features:
                    src = w_out[0, k * P:(k + 1) * P, bass.ds(n * SEQ, SEQ)]
                    sp.wait_ge(s("lo_done"), n * KT + (UPT * N_TILES + k - (RING - 1)))
                    sp.dma_start(w_raw[:, k % RING, :], src
                                 ).then_inc(arrived[k % RING], 16)

            out_units(0)
            out_units(1, range(0, RING))
            sp.wait_ge(s("o_made"), NP_)
            sp.dma_start(post_b, post_norm_w[0:1, :].broadcast_to([P, D])).then_inc(s("post_in"), 16)
            out_units(1, range(RING, KT))
            for t in range(4):
                sp.dma_start(x_again[t], xs[:, t, :]).then_inc(s("x_back"), 16)
            with sp.Fori(2, 4) as n:
                out_units(n)
            outs = out[0].rearrange("(t p) d -> p t d", p=P)
            for h in range(2):
                for t in range(4):
                    cols = slice(h * (D // 2), (h + 1) * (D // 2))
                    if t < 3:
                        sp.wait_ge(s("out_made"), 3 * h + t + 1)
                    else:
                        sp.wait_ge(s("out_made_pool"), h + 1)
                    sp.dma_start(outs[:, t, cols], proj_out[:, t, cols]).then_inc(s("out_stored"), 16)
            sp.wait_ge(s("out_stored"), 16 * 8)

        @block.tensor
        def _(pe):
            mm = nc.tensor.matmul

            def feature_tile(o, slot, h, kk_, full):
                kt = h * UK + kk_
                cols = slice(kk_ * P, (kk_ + 1) * P)
                parts = (((EDGE, 0, L // 2), (512, L // 2, L // 2)) if full else ((0, META, SEQ),))
                for w, t in ((w_hi, hn_hi), (w_hi, hn_lo), (w_lo, hn_hi)):
                    for at, tok, n in parts:
                        last = mm(o[:, at:at + n], w[:, slot, cols], t[:, kt, tok:tok + n],
                                  start=(kt == 0 and w is w_hi and t is hn_hi),
                                  stop=(kt == KT - 1 and w is w_lo))
                return last

            pe.wait_ge(s("const_in"), 16)
            pe.wait_ge(s("par_in"), 16 * 9)
            nc.tensor.transpose(ma[:, 0:N_PAR], par_rows[0:N_PAR, :], ident[0:N_PAR, 0:N_PAR]
                                ).then_inc(s("par_turned"), 1)
            pe.wait_ge(s("par_made"), 1)
            pe.wait_ge(s("norm_spread"), 5)
            for k in range(KT + LORA_LAG):
                if k < KT:
                    o = (ma, mb)[k % 2]
                    if k >= 2:
                        pe.wait_ge(s("hn_lo_made"), k - 1)
                    mm(o[:, EDGE:EDGE + META], xm[0:META, k * P:(k + 1) * P], norm_d[0:META, 4 * P:4 * P + META],
                       start=True, stop=True)
                    for t in range(4):
                        at = EDGE + META + t * P
                        xt, dt_ = xin[:, t, k * P:(k + 1) * P], norm_d[:, t * P:(t + 1) * P]
                        if at < 512 < at + P:
                            n1 = 512 - at
                            mm(o[:, at:512], xt, dt_[:, 0:n1], start=True, stop=True)
                            last = mm(o[:, 512:at + P], xt, dt_[:, n1:P], start=True, stop=True)
                        else:
                            last = mm(o[:, at:at + P], xt, dt_, start=True, stop=True)
                    last.then_inc(s("x_turned"), 1)
                if k >= LORA_LAG:
                    h, c = divmod(k - LORA_LAG, UK)
                    pe.wait_ge(s("hn_lo_made"), k - LORA_LAG + 1)
                    pe.wait_ge(s("lo_done"), h + 1)
                    last = feature_tile(tiles[0], h, h, c, True)
                    if c == UK - 1:
                        last.then_inc(s("unit_used"), 1)

            pe.wait_ge(s("const16_in"), 16)

            def gn_pe(i, work):
                n = i - 1
                yield GN_AT + 2
                if work == "rwkv":
                    pe.wait_ge(s("a_made"), i)
                pe.wait_ge(s("y_taken"), n * NG)
                pe.wait_ge(s("s_taken"), n * NC)
                mm(mb[:, 0:SEQ], c32v("centre"), ysum, start=True, stop=True).then_inc(s("centre_done"), 1)
                yield GN_AT + 4
                pe.wait_ge(s("centre_taken"), n * 2)
                for m in range(4):
                    last = mm(mb[:, 512 + 2 * m:514 + 2 * m], t512b[:, m * P:(m + 1) * P], c32v("heads_mean"),
                              start=True, stop=True)
                last.then_inc(s("var_done"), 1)
                yield GN_AT + 7
                pe.wait_ge(s("gn_spread"), n)
                for m in range(4):
                    last = nc.tensor.transpose(mb[:, 512 + m * P:512 + (m + 1) * P], t512b[:, m * P:(m + 1) * P],
                                               ident)
                last.then_inc(s("gn_turned"), 1)

            def stage_pe(i, gn):
                n = i
                yield 0
                pe.wait_ge(s("lora_made"), 1)
                pe.wait_ge(s("lora_w_in"), n * 48)
                if gn:
                    pe.wait_ge(s("inv_taken"), n * NG - NG)
                    pe.wait_ge(s("s_taken"), n * NC - (NC + GC))
                    pe.wait_ge(s("y_taken"), n * NG - (NG + 1))
                for m in range(TG):
                    last = mm(ma[:, m * P:(m + 1) * P], lora[:, m * P:(m + 1) * P], wu, start=True, stop=True)
                last.then_inc(s("z_done"), 1)
                pe.wait_ge(s("sq_made"), n)
                for m in range(TG):
                    last = mm(mb[:, 2 * m:2 * m + 2], rkp[:, m * P:(m + 1) * P], c32v("heads"), start=True, stop=True)
                last.then_inc(s("n2_done"), 1)
                yield 1.5
                pe.wait_ge(s("n2_taken"), n)
                mm(mb[:, 0:512], au, lora[:, 0:512], start=True, stop=True)
                mm(mb[:, 512:TP], au, lora[:, 512:TP], start=True, stop=True).then_inc(s("a_done"), 1)
                yield 3
                pe.wait_ge(s("z_made"), n)
                for m in range(TG):
                    last = mm(ma[:, m * P:(m + 1) * P], zt[:, m * P:(m + 1) * P],
                              c32v("tri0" if m == 0 else "tri"), start=True, stop=True)
                last.then_inc(s("c_done"), 1)
                yield 3.5
                pe.wait_ge(s("a_made"), n)
                pe.wait_ge(s("kk_spread"), n)
                for m in range(TG):
                    last = nc.tensor.transpose(mb[:, m * P:(m + 1) * P], emi[:, m * P:(m + 1) * P], ident)
                last.then_inc(s("kk_turned"), 1)
                yield BONUS_AT
                pe.wait_ge(s("rkp_made"), n)
                pe.wait_ge(s("kk_made"), n)
                if gn:
                    pe.wait_ge(s("y_made"), n - 1)
                mm(mb[:, 0:SEQ], c32v("block"), rkp[:, CH:TP], start=True, stop=True).then_inc(s("bonus_done"), 1)

            def inv_pe(i, g):
                n = groups_so_far(i, g)
                cs = [g * GC + c for c in range(GC)]
                yield inv_at(g, 0)
                if g == 0:
                    pe.wait_ge(s("bk_made"), i)
                    pe.wait_ge(s("e_made"), i * 2)
                    pe.wait_ge(s("vpad_made"), i * 2)
                else:
                    pe.wait_ge(s("inv_taken"), n - 1)
                for f, pad in enumerate((bpad, kpad)):
                    for c in range(GC):
                        at = f * 512 + c * P
                        last = nc.tensor.transpose(ma[:, at:at + P], pad[:, cs[c], :], ident)
                last.then_inc(s("bk_turned"), 1)
                yield inv_at(g, 1)
                pe.wait_ge(s("bk_taken"), n)
                for c in range(GC):
                    last = nc.tensor.transpose(ma[:, c * P:(c + 1) * P], vpad[:, cs[c], :], ident)
                last.then_inc(s("v_turned"), 1)
                for f, (pad, done, taken_) in enumerate(((bpad, "ab_done", "v_taken"), (kpad, "kb_done", "ab_taken"))):
                    yield inv_at(g, 2 + f)
                    pe.wait_ge(s(taken_), n)
                    if g == 0 and f == 0:
                        pe.wait_ge(s("pads_made"), i)
                    for c in range(GC):
                        mm(ma[:, c * P:(c + 1) * P], pad[:, cs[c], :], apad[:, cs[c], :], start=True, stop=True)
                        last = mm(ma[:, 512 + c * CH:512 + (c + 1) * CH], pad[:, cs[c], :],
                                  rc[:, cs[c] * CH:(cs[c] + 1) * CH], start=True, stop=True)
                    last.then_inc(s(done), 1)
                yield inv_at(g, 5)
                pe.wait_ge(s("kb_taken"), n)
                pe.wait_ge(s("first_made"), n)
                bl = lambda v, c: v[:, c * P:(c + 1) * P]
                for c in range(GC):
                    last = mm(ma[:, c * P:(c + 1) * P], bl(xt16, c), ident16, start=True, stop=True)
                last.then_inc(s("t0_done"), 1)
                for l in range(1, LEVELS):
                    yield inv_at(g, 4 + 2 * l)
                    if l == 1:
                        pe.wait_ge(s("t0_taken"), n)
                        pe.wait_ge(s("levels_made"), n)
                    else:
                        pe.wait_ge(s("x_taken"), n * 5 + (l - 1 - 5))
                        pe.wait_ge(s("xt_taken"), n * 5 + (l - 1 - 5))
                    for c in range(GC):
                        last = mm(ma[:, 512 + c * P:512 + (c + 1) * P],
                                  lv[:, (l * GC + c) * P:(l * GC + c + 1) * P], bl(x16, c), start=True, stop=True)
                    last.then_inc(s("zz_done"), 1)
                    yield inv_at(g, 5 + 2 * l)
                    pe.wait_ge(s("zz_taken"), n * 5 + (l - 5))
                    for c in range(GC):
                        last = mm(ma[:, 512 + c * P:512 + (c + 1) * P], bl(z16, c), bl(xt16, c),
                                  start=True, stop=True)
                    if l == LEVELS - 1:
                        last.then_inc(s("t_done"), 1)
                        continue
                    for c in range(GC):
                        last = mm(ma[:, c * P:(c + 1) * P], bl(xt16, c), bl(z16, c), start=True, stop=True)
                    last.then_inc(s("t_done"), 1)
                yield inv_at(g, 16)
                pe.wait_ge(s("xt_taken"), n * 5)
                for c in range(GC):
                    last = mm(ma[:, c * P:(c + 1) * P], bl(xt16, c), ident16, start=True, stop=True)
                last.then_inc(s("xx_done"), 1)
                yield inv_at(g, 17)
                pe.wait_ge(s("x_taken"), n * 5)
                for c in range(GC):
                    o = ma[:, 512 + c * P:512 + (c + 1) * P]
                    mm(o, ident16, ident16, start=True, stop=False)
                    mm(o, neg16, bl(x16, c), start=False, stop=False)
                    mm(o, bl(ab_hi, c), bl(x16, c), start=False, stop=False)
                    last = mm(o, bl(ab_lo, c), bl(x16, c), start=False, stop=True)
                last.then_inc(s("r_done"), 1)
                yield inv_at(g, 18)
                pe.wait_ge(s("r_taken"), n)
                for c in range(GC):
                    last = mm(ma[:, c * P:(c + 1) * P], bl(r16, c), bl(xt16, c), start=True, stop=True)
                last.then_inc(s("inv_done"), 1)

            def chain_pe(i, g, late, work, gn):
                b = g % 2
                n = groups_so_far(i, g, late)
                for c in range(GC):
                    ch = g * GC + c
                    m = chunks_so_far(i, ch, late)
                    yield chain_at(g, 0.5 + 3 * c, late)
                    if c == 0:
                        pe.wait_ge(s("inv_taken"), n)
                        if late and work == "rwkv":
                            pe.wait_ge(s("kk_made"), i)
                        if g == 0:
                            pe.wait_ge(s("state_zeroed"), i)
                            pe.wait_ge(s("bonus_taken"), i)
                    if ch > 0:
                        pe.wait_ge(s("s_taken"), m - 1)
                        if g > 0 and c == 0:
                            pe.wait_ge(s("y_taken"), n - 1)
                    o = mb[:, 0:P]
                    vb = v_tok[b][:, c * P:(c + 1) * P]
                    mm(o, apad[:, ch, :], state, start=True, stop=False)
                    mm(o, ak_t[b][:, c * P:(c + 1) * P], vb, start=False, stop=True).then_inc(s("g_done"), 1)
                    yo = mb[:, 512 + c * CH:512 + (c + 1) * CH]
                    if ch > 0:
                        mm(yo, state, rc[:, ch * CH:(ch + 1) * CH], start=True, stop=False)
                        mm(yo, vb, rk_t[b][:, c * CH:(c + 1) * CH], start=False, stop=False)
                    yield chain_at(g, 1.5 + 3 * c, late)
                    pe.wait_ge(s("g_taken"), m)
                    mm(o, t_t[b][:, c * P:(c + 1) * P], g_sb, start=True, stop=True).then_inc(s("u_done"), 1)
                    yield chain_at(g, 2.5 + 3 * c, late)
                    pe.wait_ge(s("u_taken"), m)
                    mm(o, bk_tok[b][:, c * P:(c + 1) * P], u_sb, start=True, stop=False)
                    mm(o, bk_tok[b][:, (GC + c) * P:(GC + c + 1) * P], vb, start=False,
                       stop=True).then_inc(s("s_done"), 1)
                    if ch > 0:
                        last = mm(yo, u_sb, rb_t[b][:, c * CH:(c + 1) * CH], start=False, stop=True)
                        if c == GC - 1:
                            last.then_inc(s("y_done"), 1)

            def attn_stage_pe(i, gn):
                n = i - NP_
                at = attn_stage_at(gn)
                yield at
                if gn:
                    pe.wait_ge(s("y_made"), NP_)
                    pe.wait_ge(s("inv_taken"), NP_ * NG)
                else:
                    pe.wait_ge(s("o_made"), n - 1)
                pe.wait_ge(s("tile_freed"), i * 4 + 1)
                mm(ma[:, 0:SEQ], c32v("rot"), xk[:, 0:SEQ], start=True, stop=True).then_inc(s("rotq_done"), 1)
                yield at + 1
                h = L // 2
                mm(mb[:, EDGE:512], c32v("rot"), xv[:, 0:h], start=True, stop=True)
                mm(mb[:, 512:512 + h], c32v("rot"), xv[:, h:L], start=True, stop=True).then_inc(s("rotk_done"), 1)
                yield at + 3
                pe.wait_ge(s("roped"), n * 2 - 1)
                for m in range(4):
                    nc.tensor.transpose(ma[:, m * P:(m + 1) * P], xr[:, m * P:(m + 1) * P], ident)
                nc.tensor.transpose(ma[0:META, 512:512 + P], xr[:, 512:L], ident).then_inc(s("vt_turned"), 1)

            def attn_pe(i, gn):
                n = i - NP_
                for qi in range(4):
                    base = attn_at(gn, qi)
                    c = n * 4 + (qi - 3)
                    width = META + (qi + 1) * P
                    yield base
                    if qi == 0:
                        pe.wait_ge(s("roped"), n * 2)
                        pe.wait_ge(s("vt_taken"), n * 2)
                    else:
                        pe.wait_ge(s("at_taken"), c - 1)
                        pe.wait_ge(s("o_taken"), c - 1)
                        pe.wait_ge(s("o_squared"), c - 1)
                    for m, o in ((0, ma), (1, mb)):
                        lhs = qpad[m][:, qi * P:(qi + 1) * P]
                        if qi == 3:
                            mm(o[:, EDGE:512], lhs, kr[:, 0:L // 2], start=True, stop=True)
                            last = mm(o[:, 512:EDGE + L], lhs, kr[:, L // 2:L], start=True, stop=True)
                        else:
                            last = mm(o[:, 0:width], lhs, kr[:, 0:width], start=True, stop=True)
                        last.then_inc(s("score_done"), 1)
                    yield base + 7
                    pe.wait_ge(s("combined"), c)
                    for m in range(qi + 1):
                        nc.tensor.transpose(ma[:, m * P:(m + 1) * P], prob[0][:, m * P:(m + 1) * P], ident)
                    m = qi + 1
                    nc.tensor.transpose(ma[0:META, 512:512 + P], prob[0][:, m * P:m * P + META],
                                        ident).then_inc(s("at_turned"), 1)
                    yield base + 10
                    pe.wait_ge(s("at_taken"), c)
                    o = mb[:, 0:P]
                    for m in range(qi + 1):
                        mm(o, vt[:, m * P:(m + 1) * P], attn_t[:, m * P:(m + 1) * P], start=(m == 0), stop=False)
                    m = qi + 1
                    mm(o, vt[0:META, m * P:(m + 1) * P], attn_t[0:META, 4 * P:5 * P], start=False,
                       stop=True).then_inc(s("pv_done"), 1)
                at = attn_at(gn, 3)
                yield at + 12
                pe.wait_ge(s("o_squared"), n * 4)
                pe.wait_ge(s("o_taken"), n * 4)
                for m in range(4):
                    last = mm(mb[:, 512 + m:513 + m], o_sq[:, m * P:(m + 1) * P], c32v("mean"), start=True, stop=True)
                last.then_inc(s("ovar_done"), 1)
                yield at + 14
                pe.wait_ge(s("o_spread"), n)
                for m in range(4):
                    last = nc.tensor.transpose(ma[:, m * P:(m + 1) * P], at_bc[:, m * P:(m + 1) * P], ident)
                last.then_inc(s("o_turned"), 1)

            def out_feature(n, k, gens=()):
                banks = out_banks(n)
                pe.wait_ge(s("lo_done"), UPT * N_TILES + n * KT + k + 1)
                if n == 0:
                    pe.wait_ge(s("y_lo"), k + 1)
                for t in range(4):
                    y = slice(t * P, (t + 1) * P)
                    mm(banks[t], hn_hi[:, k, y], w_hi[:, k % RING, :], start=(k == 0), stop=False)
                    mm(banks[t], hn_hi[:, k, y], w_lo[:, k % RING, :], start=False, stop=False)
                    last = mm(banks[t], hn_lo[:, k, y], w_hi[:, k % RING, :], start=False, stop=(k == KT - 1))
                    if t == 3:
                        last.then_inc(s("unit_used"), 1)
                    upto(gens, 4 * k + t)

            def body(i, proj, work, gn):
                gens = rwkv_work(i, work, gn, stage_pe, gn_pe, inv_pe, chain_pe)
                if work == "attn":
                    gens += [attn_stage_pe(i, gn), attn_pe(i, gn)]
                gens = begin(*gens)
                if proj is None:
                    upto(gens, -1)
                    pe.wait_ge(s("tile_freed"), N_TILES)
                    for k in range(KT - 1):
                        out_feature(0, k, gens)
                    upto(gens, 1000)
                    out_feature(0, KT - 1)
                    return
                for k in range(16):
                    q, h = divmod(k, UPT)
                    if proj is not None:
                        u = unit_of(i, k)
                        g = i * 4 + (q + 1)
                        if h == 0 and not (isinstance(i, int) and i == 0 and q == 0):
                            pe.wait_ge(s("tile_freed"), g - 1)
                        pe.wait_ge(s("lo_done"), u + 1)
                    for c in range(UK):
                        if proj is not None:
                            last = feature_tile(tiles[(q + 1) % 2], h, h, c, FULL[proj][q])
                            if c == UK - 1:
                                last.then_inc(s("unit_used"), 1)
                        upto(gens, k * UK + c)
                upto(gens, 1000)

            iterations(pe, body)

            pe.wait_ge(s("o_made"), NP_)
            for n in range(1, 4):
                if n >= 2:
                    pe.wait_ge(s("out_taken"), 4 * (n - 1))
                for k in range(KT):
                    out_feature(n, k)

        @block.scalar
        def _(act):
            A = nc.scalar.activation
            steps = Steps(act, "act_step")

            def split_hi(u, slot, turn):
                act.wait_ge(arrived[slot], turn * 16)
                if not (isinstance(u, int) and u < RING):
                    act.wait_ge(s("unit_used"), u - (RING - 1))
                nc.scalar.copy(w_hi[:, slot, :], w_raw[:, slot, :]).then_inc(s("hi_done"), 1)

            for n, t in enumerate((4, 0, 1, 2, 3)):
                act.wait_ge(s(f"x_in{t}" if t < 4 else "meta_in"), 16)
                if n:
                    act.wait_ge(s("norm_sq"), n)
                v = xin[:, t, :] if t < 4 else xm[0:META, :]
                rows = P if t < 4 else META
                A(junk[0:rows, :], v, ACT.Square, accum_out=norm_s[0:rows, t:t + 1]).then_inc(s("norm_sq"), 1)
            act.wait_ge(s("par_made"), 1)
            for k in range(KT):
                act.wait_ge(s("x_turned"), k + 1)
                o = (ma, mb)[k % 2]
                A(hn_hi[:, k, :], o[:, EDGE:EDGE + L], ACT.Copy,
                  scale=par[:, PC["pre"] + k:PC["pre"] + k + 1]).then_inc(s("hn_hi_made"), 1)
                if k < UPT:
                    split_hi(k, k, 1)
                elif k % UK == 2 and k >= UPT + UK:
                    u = UPT + (k - UPT) // UK - 1
                    split_hi(u, u % RING, 2)
            split_hi(UPT + 2, (UPT + 2) % RING, 2)
            act.wait_ge(s("lam_dots"), 2)
            A(lam_s[:, 2:4], lam_s[:, 0:2], ACT.Exp).then_inc(s("lam_exp"), 1)
            act.wait_ge(s("unit_used"), UPT)
            act.wait_ge(s("zeroed"), 1)
            A(lora[:, PAD:TP], tiles[0][:, EDGE:EDGE + L], ACT.Copy, scale=om_mu[:, 24:25]).then_inc(s("lora_base"), 1)
            act.wait_ge(s("tile_freed"), 1)
            A(lora[0:HD, PAD:TP], lora[0:HD, PAD:TP], ACT.Tanh).then_inc(s("lora_made"), 1)

            def tile_act(i, proj, work):
                if proj == "rwkv":
                    for q, (xt, mu) in enumerate(((xk, 8), (xv, 16), (xr, 0))):
                        yield 16 * q + 15.5
                        act.wait_ge(s("unit_used"), i * 16 + (8 + 4 * q))
                        if work == "rwkv":
                            act.wait_ge(s("bonus_taken" if q == 1 else "pads_made"), i)
                        A(xt[:, PAD:TP], tiles[(q + 1) % 2][:, EDGE:EDGE + L], ACT.Copy,
                          scale=column(om_mu, mu, i)).then_inc(s("x_based"), 1)
                yield 63.5
                act.wait_ge(s("unit_used"), i * 16 + 20)
                A(tanh_g[:], tiles[0][:, 0:SEQ], ACT.Tanh, scale=0.5).then_inc(s("gate_tanh"), 1)

            def gn_act(i, work):
                n = i - 1
                yield GN_AT + 2.5
                act.wait_ge(s("centre_done"), n)
                act.wait_ge(s("tile_freed"), i * 4 + 1)
                A(t512, mb[:, 0:SEQ], ACT.Copy).then_inc(s("centre_taken"), 1)
                A(t512b, mb[:, 0:SEQ], ACT.Square).then_inc(s("centre_taken"), 1)
                yield GN_AT + 6
                act.wait_ge(s("gn_powed"), n)
                A(t512b.rearrange("p (m d) -> p m d", d=HD), gn_pow.unsqueeze(2).broadcast_to([P, 8, HD]),
                  ACT.Copy).then_inc(s("gn_spread"), 1)

            def stage_act(i, gn):
                n = i
                yield 0
                act.wait_ge(s("tile_freed"), i * 4 - 2)
                if gn:
                    act.wait_ge(s("bonus_taken"), n - 1)
                A(rkp[:, 0:TP], xk[:], ACT.Square, scale=column(par, PC["k_k"], i - 1)).then_inc(s("sq_made"), 1)
                yield 1.5
                act.wait_ge(s("z_added"), n)
                A(zt, zt, ACT.Tanh, scale=0.5).then_inc(s("z_tanh"), 1)
                yield 2.5
                act.wait_ge(s("a_done"), n)
                act.wait_ge(s("zeroed"), 1)
                A(tha, mb[:, 0:TP], ACT.Tanh, scale=0.5, bias=column(half_a0, 0, i - 1)).then_inc(s("a_made"), 1)
                yield 3
                act.wait_ge(s("kk_powed"), n)
                A(emi.rearrange("p (m d) -> p m d", d=HD), kk_pow.unsqueeze(2).broadcast_to([P, 2 * TG, HD]),
                  ACT.Copy).then_inc(s("kk_spread"), 1)
                yield 4
                act.wait_ge(s("c_done"), n)
                act.wait_ge(s("kk_turned"), n)
                cum = ma[:, 0:TP]
                A(emi[:, 0:TP], cum, ACT.Exp, scale=-1.0).then_inc(s("e_made"), 1)
                A(ew3[:, :, 1:], cum.rearrange("p (c t) -> p c t", c=NC), ACT.Exp).then_inc(s("e_made"), 1)
                yield 5
                act.wait_ge(s("tile_freed"), i * 4 - 1)
                for h in range(2):
                    A(vpad[h * HD:(h + 1) * HD, :, h * CH:(h + 1) * CH],
                      xv[h * HD:(h + 1) * HD, :].rearrange("p (c t) -> p c t", c=NC),
                      ACT.Copy).then_inc(s("vpad_made"), 1)
                yield 14.5
                if gn:
                    act.wait_ge(s("s_taken"), n * NC - NC)
                    act.wait_ge(s("s_scaled"), n * NC - NC)
                A(w_end, ew3[:, :, CH], ACT.Copy).then_inc(s("ends_made"), 1)
                yield GN_AT + 12
                if gn:
                    act.wait_ge(s("y_made"), n - 1)
                act.wait_ge(s("tile_freed"), i * 4 + 1)
                A(gate2[:], gate[:], ACT.Copy).then_inc(s("gate_moved"), 1)

            def inv_act(i, g):
                b = g % 2
                n = groups_so_far(i, g)
                W = GC * P
                yield inv_at(g, 0.5)
                act.wait_ge(s("bk_turned"), n)
                if g == 2 or not (isinstance(i, int) and i == 1):
                    act.wait_ge(s("s_done"), n * GC - (1, 3, 2)[g] * GC)
                A(bk_tok[b][:, 0:W], ma[:, 0:W], ACT.Copy).then_inc(s("bk_taken"), 1)
                yield inv_at(g, 5.5)
                act.wait_ge(s("t0_done"), n)
                A(x16, ma[:, 0:W], ACT.Copy).then_inc(s("t0_taken"), 1)
                for l in range(1, LEVELS):
                    yield inv_at(g, 5.5 + 2 * l)
                    if l < LEVELS - 1:
                        act.wait_ge(s("t_done"), n * 5 + (l - 5))
                        A(x16, ma[:, 0:W], ACT.Copy).then_inc(s("x_taken"), 1)
                yield inv_at(g, 16.5)
                act.wait_ge(s("xx_done"), n)
                A(x16, ma[:, 0:W], ACT.Copy).then_inc(s("x_taken"), 1)
                yield inv_at(g, 17.5)
                act.wait_ge(s("r_done"), n)
                A(r16, ma[:, 512:512 + W], ACT.Copy).then_inc(s("r_taken"), 1)

            def chain_act(i, g, late, work, gn):
                n = groups_so_far(i, g, late)
                for c in range(GC):
                    ch = g * GC + c
                    m = chunks_so_far(i, ch, late)
                    yield chain_at(g, 0.8 + 3 * c, late)
                    if ch == 0:
                        act.wait_ge(s("ends_made"), i)
                        act.wait_ge(s("state_zeroed"), i)
                    else:
                        act.wait_ge(s("s_taken"), m - 1)
                    A(state0, state, ACT.Copy, scale=w_end[:, ch:ch + 1]).then_inc(s("s_scaled"), 1)
                yield chain_at(g, 9, late)
                act.wait_ge(s("y_done"), n)
                lo = max(0, g * GC * CH - CH)
                w = (g + 1) * GC * CH - CH - lo
                A(ysum[:, lo:lo + w], mb[:, 512 + GC * CH - w:512 + GC * CH], ACT.Copy).then_inc(s("y_taken"), 1)

            def attn_act(i, gn):
                n = i - NP_
                at = attn_stage_at(gn)
                yield at + 3.5
                act.wait_ge(s("vt_turned"), n)
                A(vt[:, 0:SEQ], ma[:, 0:SEQ], ACT.Copy).then_inc(s("vt_taken"), 1)
                A(vt[0:META, 512:512 + P], ma[0:META, 512:512 + P], ACT.Copy).then_inc(s("vt_taken"), 1)
                if gn:
                    act.wait_ge(s("y_made"), NP_)
                else:
                    act.wait_ge(s("o_made"), n - 1)
                act.wait_ge(s("tile_freed"), i * 4 + 1)
                A(gate2[:], gate[:], ACT.Copy).then_inc(s("gate_moved"), 1)
                for qi in range(4):
                    base = attn_at(gn, qi)
                    c = n * 4 + (qi - 3)
                    at = EDGE if qi == 3 else 0
                    width = META + (qi + 1) * P
                    for m, o in ((0, ma), (1, mb)):
                        yield base + 3 + m
                        act.wait_ge(s("neg_made"), c * 2 + (m - 1))
                        A(prob[m][:, 0:width], o[:, at:at + width], ACT.Exp, scale=HD ** -0.5,
                          bias=at_neg[:, m:m + 1], accum_out=at_sum[:, m:m + 1]).then_inc(s("exp_made"), 1)
                    yield base + 8
                    act.wait_ge(s("at_turned"), c)
                    w = (qi + 1) * P
                    steps.quiet(A(attn_t[:, 0:w], ma[:, 0:w], ACT.Copy))
                    A(attn_t[0:META, 512:512 + P], ma[0:META, 512:512 + P], ACT.Copy).then_inc(s("at_taken"), 1)
                    yield base + 11.5
                    act.wait_ge(s("o_taken"), c)
                    A(o_sq[:, qi * P:(qi + 1) * P], o_sb[:, qi * P:(qi + 1) * P], ACT.Square).then_inc(s("o_squared"), 1)

                at = attn_at(gn, 3)
                yield at + 13
                act.wait_ge(s("o_powed"), n)
                A(at_bc.rearrange("p (m d) -> p m d", d=P), at_pow.unsqueeze(2).broadcast_to([P, 4, P]),
                  ACT.Copy).then_inc(s("o_spread"), 1)

            def split_y_act():
                act.wait_ge(s("unit_used"), UPT * N_TILES)
                for k in range(KT):
                    yield max(4 * k - 7, -1) if k < KT - 1 else 200
                    act.wait_ge(s("y_made" if k < NP_ else "o_made"), k % NP_ + 1)
                    A(hn_hi[:, k, 0:SEQ], ymix[:, k, :], ACT.Copy).then_inc(s("y_hi"), 1)

            def body(i, proj, work, gn):
                gens = rwkv_work(i, work, gn, stage_act, gn_act, inv_act, chain_act)
                if work == "attn":
                    gens.append(attn_act(i, gn))
                if proj is not None:
                    gens.append(tile_act(i, proj, work))
                else:
                    gens.append(split_y_act())
                gens = begin(*gens)
                for k in range(16):
                    split_hi(unit_of(i, k + AHEAD), (k + AHEAD) % RING, i * 4 + (2 + (k + AHEAD) // UPT))
                    upto(gens, k * UK + 3)
                upto(gens, 1000)
                steps.clear()

            iterations(act, body)

            for n in range(1, 4):
                for k in range(KT):
                    u = UPT * N_TILES + n * KT + k + AHEAD
                    if u < UPT * N_TILES + 4 * KT:
                        split_hi(u, u % RING, u // RING + 1)
                    if k == 1:
                        squares(act, n - 1)
            squares(act, 3)
            act.wait_ge(s("out_taken"), 16)
            act.wait_ge(s("tot_powed"), 1)
            for h in range(2):
                v = proj_out[:, 3, h * (D // 2):(h + 1) * (D // 2)]
                A(v, v, ACT.Copy, scale=sq_tot[:, 7:8]).then_inc(s("out_scaled"), 1)

        @block.gpsimd
        def _(pool):
            T = nc.gpsimd.tensor_tensor

            def split_lo(u, slot):
                pool.wait_ge(s("hi_done"), u + 1)
                T(w_lo[:, slot, :], w_raw[:, slot, :], w_hi[:, slot, :].bitcast(F32),
                  ALU.subtract).then_inc(s("lo_done"), 1)

            nc.gpsimd.memset(power[:], -0.5).then_inc(s("power_made"), 1)
            pool.wait_ge(s("power_made"), 1)
            for n, t in enumerate((4, 0, 1, 2, 3)):
                rows = P if t < 4 else META
                pool.wait_ge(s("norm_var"), n + 1)
                T(norm_s[0:rows, 10 + t:11 + t], norm_s[0:rows, 5 + t:6 + t], power[0:rows, 0:1],
                  ALU.pow).then_inc(s("norm_pow"), 1)
            for u in range(UPT + AHEAD):
                split_lo(u, u % RING)

            def powed(done, out_, in_, w, name, n):
                pool.wait_ge(s(done), n)
                T(out_[:, 0:w], in_[:, 0:w], power[:, 0:w], ALU.pow).then_inc(s(name), 1)

            def stage_pool(i):
                yield 2
                powed("n2_taken", kk_pow, kk_small, 2 * TG, "kk_powed", i)

            def gn_pool(i, work):
                yield GN_AT + 5
                powed("var_taken", gn_pow, gn_small, 8, "gn_powed", i - 1)

            def attn_pool(i, gn):
                yield attn_at(gn, 3) + 12.7
                powed("ovar_taken", at_pow, at_var, 4, "o_powed", i - NP_)

            def body(i, proj, work, gn):
                gens = []
                if work == "rwkv":
                    gens.append(stage_pool(i))
                if gn:
                    gens.append(gn_pool(i, work))
                if work == "attn":
                    gens.append(attn_pool(i, gn))
                gens = begin(*gens)
                for k in range(16):
                    split_lo(unit_of(i, k + AHEAD), (k + AHEAD) % RING)
                    upto(gens, k * UK + 3)
                upto(gens, 1000)

            iterations(pool, body)
            for u in range(UPT * N_TILES + KT + AHEAD, UPT * N_TILES + 4 * KT):
                split_lo(u, u % RING)
            powed("tot_made", sq_tot[:, 4:8], sq_tot[:, 0:4], 4, "tot_powed", 1)
            pool.wait_ge(s("x_back"), 64)
            for h in range(2):
                cols = slice(h * (D // 2), (h + 1) * (D // 2))
                pool.wait_ge(s("out_scaled"), h + 1)
                T(proj_out[:, 3, cols], proj_out[:, 3, cols], x_again[3][:, cols], ALU.add
                  ).then_inc(s("out_made_pool"), 1)

        @block.vector
        def _(dve):
            V = nc.vector
            steps = Steps(dve, "dve_step")
            TT, STT, TS = V.tensor_tensor, V.scalar_tensor_tensor, V.tensor_scalar

            for n, t in enumerate((4, 0, 1, 2, 3)):
                rows = P if t < 4 else META
                dve.wait_ge(s("norm_sq"), n + 1)
                TS(norm_s[0:rows, 5 + t:6 + t], norm_s[0:rows, t:t + 1], 1.0 / D, EPS, ALU.mult,
                   ALU.add).then_inc(s("norm_var"), 1)
            dve.wait_ge(s("const_in"), 16)
            for n, t in enumerate((4, 0, 1, 2, 3)):
                rows = P if t < 4 else META
                dve.wait_ge(s("norm_pow"), n + 1)
                TS(norm_d[0:rows, t * P:t * P + rows], ident[0:rows, 0:rows], norm_s[0:rows, 10 + t:11 + t], None,
                   ALU.mult).then_inc(s("norm_spread"), 1)
            dve.wait_ge(s("par_turned"), 1)
            V.tensor_copy(par[:], ma[:, 0:N_PAR]).then_inc(s("par_made"), 1)
            dve.wait_ge(s("par_made"), 1)
            TS(om_mu[:], par[:, 0:25], -1.0, 1.0, ALU.mult, ALU.add)
            TS(half_a0[:], par[:, PC["a0"]:PC["a0"] + 8], 0.5, None, ALU.mult)
            steps(TS(half_ka[:], par[:, PC["k_a"]:PC["k_a"] + 8], 0.5, None, ALU.mult))
            TS(om_ka[:], half_ka[:], -1.0, 1.0, ALU.mult, ALU.add)
            TS(gate_sub[:], par[:, PC["sub"]:PC["sub"] + 1], 0.5 * (1.0 - LAM0), None, ALU.mult)
            for k in range(KT):
                dve.wait_ge(s("hn_hi_made"), k + 1)
                o = (ma, mb)[k % 2]
                STT(hn_lo[:, k, :], o[:, EDGE:EDGE + L], par[:, PC["pre"] + k:PC["pre"] + k + 1],
                    hn_hi[:, k, :].bitcast(F32), ALU.mult, ALU.subtract).then_inc(s("hn_lo_made"), 1)
            dve.wait_ge(s("const16_in"), 16)
            dve.wait_ge(s("lam_in"), 64)
            for n in range(2):
                steps(TT(lam_p, lam_in[:, 2 * n * HD:(2 * n + 1) * HD], lam_in[:, (2 * n + 1) * HD:(2 * n + 2) * HD],
                         ALU.mult))
                V.reduce_sum(lam_s[:, n:n + 1], lam_p, AX).then_inc(s("lam_dots"), 1)
                dve.wait_ge(s("lam_dots"), n + 1)
            dve.wait_ge(s("lam_exp"), 1)
            steps(TT(lam[:], lam_s[:, 2:3], lam_s[:, 3:4], ALU.subtract))
            steps(TS(lam[:], lam[:], LAM0, None, ALU.add))
            for v in (xk, xv, xr, lora):
                V.memset(v[:, 0:PAD], 0.0)
            V.memset(lora[:, TP:TPX], 0.0)
            for v in (apad, bpad, kpad, vpad):
                V.memset(v, 0.0)
            V.memset(wu[HD:P, :], 0.0)
            V.memset(rkp[:, TP:TPX], 0.0)
            V.memset(au[0:HD, :], 0.0)
            V.memset(ew3[:, :, 0:1], 1.0).then_inc(s("zeroed"), 1)
            dve.wait_ge(s("lora_base"), 1)
            STT(lora[:, PAD + 1:TP], tiles[0][:, EDGE:EDGE + L - 1], par[:, PC["mu_l"]:PC["mu_l"] + 1],
                lora[:, PAD + 1:TP], ALU.mult, ALU.add).then_inc(s("tile_freed"), 1)

            def tile_dve(i, proj, work, gn):
                for q in range(3):
                    yield 29.5 if q == 0 and gn and work == "attn" else 16 * q + 15.6
                    o = tiles[(q + 1) % 2]
                    xt = (xk, xv, xr)[q]
                    if proj == "rwkv":
                        dve.wait_ge(s("x_based"), i * 3 + (q + 1))
                        STT(xt[:, PAD + 1:TP], o[:, EDGE:EDGE + L - 1], column(par, (8, 16, 0)[q], i),
                            xt[:, PAD + 1:TP], ALU.mult, ALU.add).then_inc(s("tile_freed"), 1)
                    else:
                        dve.wait_ge(s("unit_used"), i * 16 + (8 + 4 * q))
                        if work == "rwkv":
                            dve.wait_ge(s("bonus_taken" if q == 1 else "pads_made"), NP_)
                            dve.wait_ge(s("vpad_made"), 2 * NP_)
                        else:
                            dve.wait_ge(s("vt_turned"), i - NP_)
                        full = FULL[proj][q]
                        n, at = (L, EDGE) if full else (SEQ, 0)
                        V.tensor_copy(xt[:, 0:n], o[:, at:at + n]).then_inc(s("tile_freed"), 1)
                yield 63.6
                dve.wait_ge(s("gate_tanh"), i + 1)
                STT(gate[:], tanh_g[:], 1.0, tiles[0][:, 0:SEQ], ALU.add, ALU.mult).then_inc(s("tile_freed"), 1)

            def gn_dve(i, work):
                n = i - 1
                yield GN_AT + 4.5
                dve.wait_ge(s("var_done"), n)
                TS(gn_small, mb[:, 512:520], GN_EPS, None, ALU.add).then_inc(s("var_taken"), 1)
                yield GN_AT + 7.5
                dve.wait_ge(s("gn_turned"), n)
                steps(TT(t512, t512, mb[:, 512:1024], ALU.mult))
                yield GN_AT + 8.5
                steps(TS(t512, t512, column(par, PC["gn_w"], i - 2), column(par, PC["gn_b"], i - 2),
                         ALU.mult, ALU.add))
                yield GN_AT + 9.5
                dst = mixed(i - 2)
                steps(TT(t512, t512, dst, ALU.add))
                yield GN_AT + 10.5
                dve.wait_ge(s("gate_moved"), n)
                STT(dst, gate2[:], 0.5, t512, ALU.mult, ALU.mult).then_inc(s("y_made"), 1)

            def stage_dve(i, gn):
                n = i
                yield 1
                dve.wait_ge(s("z_done"), n)
                dve.wait_ge(s("lora_w_in"), n * 48)
                TT(zt.rearrange("p (g c) -> p g c", g=TG), ma[:, 0:TPX].rearrange("p (g c) -> p g c", g=TG),
                   w0b.unsqueeze(1).broadcast_to([P, TG, P]), ALU.add).then_inc(s("z_added"), 1)
                yield 1.5
                dve.wait_ge(s("n2_done"), n)
                TS(kk_small, mb[:, 0:2 * TG], 1e-24, None, ALU.max).then_inc(s("n2_taken"), 1)
                yield 2
                dve.wait_ge(s("z_tanh"), n)
                TS(zt, zt, 1.0, -0.5 * C_DECAY, ALU.add, ALU.mult).then_inc(s("z_made"), 1)
                yield 3
                dve.wait_ge(s("a_made"), n)
                steps(TS(kp, tha, column(half_ka, 0, i - 1), column(om_ka, 0, i - 1), ALU.mult, ALU.add))
                steps(TT(kp, kp, xk[:], ALU.mult))
                STT(rkp[:, 0:TP], xr[:], column(par, PC["r_k"], i - 1), kp, ALU.mult, ALU.mult).then_inc(s("rkp_made"), 1)
                yield 4
                dve.wait_ge(s("kk_turned"), n)
                STT(kk, xk[:], column(par, PC["k_k"], i - 1), mb[:, 0:TP], ALU.mult, ALU.mult).then_inc(s("kk_made"), 1)
                dve.wait_ge(s("kk_made"), n)
                dve.wait_ge(s("e_made"), n * 2)
                e0, e1 = ew3[:, :, 0:CH], ew3[:, :, 1:CH + 1]
                c3 = lambda v: v[:, 0:TP].rearrange("p (c t) -> p c t", c=NC)
                steps(STT(tmp[:, 0:TP], tha, 1.0, kk, ALU.add, ALU.mult))
                yield 6
                for h in range(2):
                    r = slice(h * HD, (h + 1) * HD)
                    STT(bpad[r, :, h * CH:(h + 1) * CH], c3(tmp)[r], 0.5, c3(emi)[r], ALU.mult, ALU.mult)
                    ins = TT(kpad[r, :, h * CH:(h + 1) * CH], c3(kp)[r], c3(emi)[r], ALU.mult)
                ins.then_inc(s("bk_made"), 1)
                yield chain_at(NG - 1, 3 * GC - 1, True)
                if gn:
                    dve.wait_ge(s("u_done"), n * NC - NC)
                for h in range(2):
                    r = slice(h * HD, (h + 1) * HD)
                    STT(apad[r, :, h * CH:(h + 1) * CH], c3(kk)[r], -1.0, e0[r], ALU.mult, ALU.mult)
                TT(c3(rc), c3(xr), e1, ALU.mult).then_inc(s("pads_made"), 1)
                yield BONUS_AT + 0.5
                dve.wait_ge(s("bonus_done"), n)
                TT(mixed(i - 1), mb[:, 0:SEQ], xv[:, CH:TP], ALU.mult).then_inc(s("bonus_taken"), 1)
                yield chain_at(0, 0, 0) - 0.5
                if gn:
                    dve.wait_ge(s("s_scaled"), (n - 1) * NC)
                    dve.wait_ge(s("y_done"), (n - 1) * NG)
                V.memset(state, 0.0).then_inc(s("state_zeroed"), 1)

            def inv_dve(i, g):
                b = g % 2
                n = groups_so_far(i, g)
                W = GC * P
                g3 = lambda v: v.rearrange("p (c t) -> p c t", c=GC)
                strict = c32v("strict").unsqueeze(1).broadcast_to([P, GC, P])
                incl = c32v("incl").unsqueeze(1).broadcast_to([P, GC, CH])
                yield inv_at(g, 0.5)
                dve.wait_ge(s("bk_turned"), n)
                if g == 2 or not (isinstance(i, int) and i == 1):
                    dve.wait_ge(s("s_done"), n * GC - (1, 3, 2)[g] * GC)
                steps.quiet(V.tensor_copy(bk_tok[b][:, W:2 * W], ma[:, 512:512 + W]))
                yield inv_at(g, 1.5)
                dve.wait_ge(s("v_turned"), n)
                V.tensor_copy(v_tok[b], ma[:, 0:W]).then_inc(s("v_taken"), 1)
                yield inv_at(g, 2.5)
                dve.wait_ge(s("ab_done"), n)
                steps.quiet(TT(g3(ab32), g3(ma[:, 0:W]), strict, ALU.mult))
                TT(g3(rb_t[b]), g3(ma[:, 512:512 + GC * CH]), incl, ALU.mult).then_inc(s("ab_taken"), 1)
                dve.wait_ge(s("ab_taken"), n)
                steps(V.tensor_copy(ab_hi, ab32))
                l4 = lv.rearrange("p (l c t) -> p l c t", l=LEVELS, c=GC)
                level = lambda l: TT(l4[:, l], g3(ab_hi), level_masks[:, l, :].unsqueeze(1).broadcast_to([P, GC, P]),
                                     ALU.mult)
                steps(level(0))
                TT(g3(xt16), l4[:, 0], ident16.unsqueeze(1).broadcast_to([P, GC, P]),
                   ALU.add).then_inc(s("first_made"), 1)
                yield inv_at(g, 3.5)
                dve.wait_ge(s("kb_done"), n)
                TT(g3(ak_t[b]), g3(ma[:, 0:W]), strict, ALU.mult)
                TT(g3(rk_t[b]), g3(ma[:, 512:512 + GC * CH]), incl, ALU.mult).then_inc(s("kb_taken"), 1)
                yield inv_at(g, 4.5)
                for l in range(1, LEVELS):
                    level(l)
                TT(ab_lo, ab32, ab_hi, ALU.subtract).then_inc(s("levels_made"), 1)
                for l in range(1, LEVELS):
                    yield inv_at(g, 4.5 + 2 * l)
                    dve.wait_ge(s("zz_done"), n * 5 + (l - 5))
                    TT(g3(z16), g3(ma[:, 512:512 + W]), ident16.unsqueeze(1).broadcast_to([P, GC, P]),
                       ALU.add).then_inc(s("zz_taken"), 1)
                    yield inv_at(g, 5.5 + 2 * l)
                    dve.wait_ge(s("t_done"), n * 5 + (l - 5))
                    V.tensor_copy(xt16, ma[:, 512:512 + W]).then_inc(s("xt_taken"), 1)
                yield inv_at(g, 18.5)
                dve.wait_ge(s("inv_done"), n)
                TT(t_t[b], ma[:, 0:W], xt16, ALU.add).then_inc(s("inv_taken"), 1)

            def chain_dve(i, g, late, work, gn):
                for c in range(GC):
                    ch = g * GC + c
                    m = chunks_so_far(i, ch, late)
                    yield chain_at(g, 0.8 + 3 * c, late)
                    dve.wait_ge(s("g_done"), m)
                    V.tensor_copy(g_sb, mb[:, 0:P]).then_inc(s("g_taken"), 1)
                    yield chain_at(g, 1.8 + 3 * c, late)
                    dve.wait_ge(s("u_done"), m)
                    V.tensor_copy(u_sb, mb[:, 0:P]).then_inc(s("u_taken"), 1)
                    yield chain_at(g, 2.8 + 3 * c, late)
                    dve.wait_ge(s("s_done"), m)
                    dve.wait_ge(s("s_scaled"), m)
                    STT(state, mb[:, 0:P], w_end[:, ch:ch + 1], state0, ALU.mult, ALU.add).then_inc(s("s_taken"), 1)

            def attn_dve(i, gn):
                n = i - NP_
                at = attn_stage_at(gn)
                yield at - 0.5
                if gn:
                    dve.wait_ge(s("s_taken"), NP_ * NC)
                    dve.wait_ge(s("y_taken"), NP_ * NG)
                    V.memset(qpad[0][HD:P, :], 0.0)
                    V.memset(qpad[1][0:HD, :], 0.0)
                    dve.wait_ge(s("rope_in"), 32)
                yield at + 0.5
                if not gn:
                    dve.wait_ge(s("roped"), n * 2 - 2)
                steps.quiet(TT(rt1[:, 0:SEQ], xk[:, 0:SEQ], cos_t[:, META:L], ALU.mult))
                dve.wait_ge(s("rotq_done"), n)
                steps(TT(rt2[:, 0:SEQ], ma[:, 0:SEQ], sin_t[:, META:L], ALU.mult))
                TT(qpad[0][0:HD, :], rt1[0:HD, 0:SEQ], rt2[0:HD, 0:SEQ], ALU.add)
                TT(qpad[1][HD:P, :], rt1[HD:P, 0:SEQ], rt2[HD:P, 0:SEQ], ALU.add).then_inc(s("roped"), 1)
                yield at + 1.5
                dve.wait_ge(s("roped"), n * 2 - 1)
                steps.quiet(TT(rt1, xv[:, 0:L], cos_t, ALU.mult))
                dve.wait_ge(s("rotk_done"), n)
                steps(TT(rt2, mb[:, EDGE:EDGE + L], sin_t, ALU.mult))
                TT(kr, rt1, rt2, ALU.add).then_inc(s("roped"), 1)
                for qi in range(4):
                    base = attn_at(gn, qi)
                    c = n * 4 + (qi - 3)
                    at = EDGE if qi == 3 else 0
                    width = META + (qi + 1) * P
                    for m, o in ((0, ma), (1, mb)):
                        yield base + 1 + m
                        dve.wait_ge(s("score_done"), c * 2 + (m - 1))
                        d = o[:, at + width - P:at + width]
                        steps(TT(d, d, c32v("causal"), ALU.add))
                        steps(V.reduce_max(at_max[:, m:m + 1], o[:, at:at + width], AX))
                        TS(at_neg[:, m:m + 1], at_max[:, m:m + 1], -HD ** -0.5, None,
                           ALU.mult).then_inc(s("neg_made"), 1)
                    yield base + 5
                    dve.wait_ge(s("exp_made"), c * 2)
                    steps(V.reciprocal(at_inv, at_sum))
                    steps(TT(at_inv[:, 1:2], at_inv[:, 1:2], lam[:], ALU.mult))
                    steps(TS(prob[1][:, 0:width], prob[1][:, 0:width], at_inv[:, 1:2], None, ALU.mult))
                    STT(prob[0][:, 0:width], prob[0][:, 0:width], at_inv[:, 0:1], prob[1][:, 0:width], ALU.mult,
                        ALU.subtract).then_inc(s("combined"), 1)
                    yield base + 11
                    dve.wait_ge(s("pv_done"), c)
                    V.tensor_copy(o_sb[:, qi * P:(qi + 1) * P], mb[:, 0:P]).then_inc(s("o_taken"), 1)
                at = attn_at(gn, 3)
                yield at + 12.5
                dve.wait_ge(s("ovar_done"), n)
                TS(at_var, mb[:, 512:516], SUB_EPS, None, ALU.add).then_inc(s("ovar_taken"), 1)
                yield at + 14.5
                dve.wait_ge(s("o_turned"), n)
                steps(TT(o_sb, o_sb, ma[:, 0:SEQ], ALU.mult))
                dve.wait_ge(s("gate_moved"), i)
                STT(mixed(i - 1), gate2[:], gate_sub[:], o_sb, ALU.mult, ALU.mult).then_inc(s("o_made"), 1)

            def split_y_dve():
                for k in range(KT):
                    yield max(4 * k - 7, -1) + 0.1 if k < KT - 1 else 200
                    dve.wait_ge(s("y_hi"), k + 1)
                    TT(hn_lo[:, k, 0:SEQ], ymix[:, k, :], hn_hi[:, k, 0:SEQ].bitcast(F32),
                       ALU.subtract).then_inc(s("y_lo"), 1)

            def body(i, proj, work, gn):
                gens = rwkv_work(i, work, gn, stage_dve, gn_dve, inv_dve, chain_dve)
                if work == "attn":
                    gens.append(attn_dve(i, gn))
                gens.append(tile_dve(i, proj, work, gn) if proj is not None else split_y_dve())
                upto(begin(*gens), 1000)
                steps.clear()

            steps.clear()
            iterations(dve, body)

            dve.wait_ge(s("post_in"), 16)
            for n in range(4):
                cols = slice(n * SEQ, (n + 1) * SEQ)
                for t in range(4):
                    dve.wait_ge(s("out_sq"), 4 * n + t + 1)
                    TT(proj_out[:, t, cols], out_banks(n)[t], post_b[:, cols], ALU.mult).then_inc(s("out_taken"), 1)
            steps(V.reduce_sum(sq_tot[:, 0:4], sq_sum.rearrange("p (t n) -> p t n", n=4), AX))
            TS(sq_tot[:, 0:4], sq_tot[:, 0:4], 1.0 / D, EPS, ALU.mult, ALU.add).then_inc(s("tot_made"), 1)
            dve.wait_ge(s("tot_powed"), 1)
            dve.wait_ge(s("out_taken"), 16)
            dve.wait_ge(s("x_back"), 64)
            for h in range(2):
                for t in range(3):
                    cols = slice(h * (D // 2), (h + 1) * (D // 2))
                    STT(proj_out[:, t, cols], proj_out[:, t, cols], sq_tot[:, 4 + t:5 + t], x_again[t][:, cols],
                        ALU.mult, ALU.add).then_inc(s("out_made"), 1)


INPUTS = ("x", "meta_tokens", "pre_norm_w", "w_in", "rwkv_mu", "rwkv_w0", "rwkv_w_up", "rwkv_a0", "rwkv_a_up",
          "rwkv_k_k", "rwkv_k_a", "rwkv_r_k", "rwkv_gn_w", "rwkv_gn_b", "diff_lam_q1", "diff_lam_k1",
          "diff_lam_q2", "diff_lam_k2", "diff_subln_w", "w_out", "post_norm_w")


def kernel(**inputs):
    import concourse.bacc as bacc
    from concourse.bass_utils import run_bass_kernel_spmd

    nc = bacc.Bacc("TRN2", target_bir_lowering=False, num_devices=1)
    arrays, args = {}, []
    tables = dict(zip(("table_f32", "table_f16", "table_rope"), constants()))
    for name, a in [(n, inputs[n]) for n in INPUTS] + list(tables.items()):
        a = np.ascontiguousarray(a)
        arrays[name] = a
        args.append(nc.dram_tensor(name, a.shape, mybir.dt.from_np(a.dtype), kind="ExternalInput").ap())
    out = nc.dram_tensor("out", (1, SEQ, D), F32, kind="ExternalOutput").ap()
    hybrid_layer(nc, *args, out)
    r = run_bass_kernel_spmd(nc, [arrays], core_ids=[0])
    return r.results[0]["out"]
```

```python
import math

import numpy as np
import concourse.bass as bass
from concourse import mybir
from contextlib import ExitStack

F32 = mybir.dt.float32
F32R = mybir.dt.float32r
F16 = mybir.dt.float16
ALU = mybir.AluOpType
ACT = mybir.ActivationFunctionType
AX = mybir.AxisListType.X

P = 128
D = 2048
SEQ = 512
META = 16
L = SEQ + META
KT = D // P
RW = 1024
NP_ = RW // P
HD = 64
CH = 64
PAD = CH - META
TP = PAD + L
NC = TP // CH
TG = 5
TPX = TG * P
GC = 3
NG = NC // GC
UK = 4
UPT = KT // UK
RING = 4
AHEAD = 3
LORA_COL = 3 * RW
G_COL = LORA_COL + P
ATT_COL = G_COL + RW
TILE_COLS = {"rwkv": (RW, 2 * RW, 0, G_COL),
             "attn": (ATT_COL, ATT_COL + RW, ATT_COL + 2 * RW, ATT_COL + 3 * RW)}
FULL = {"rwkv": (True, True, True, False), "attn": (False, True, True, False)}
N_TILES = 1 + 4 * 2 * NP_
EDGE = 248
TURN = 512 - META - 3 * P
EPS, GN_EPS, SUB_EPS = 1e-6, 64e-5, 1e-5
LAM0 = 0.8 - 0.6 * math.exp(0.0)
C_DECAY = math.exp(-0.5)
NEG = -3.0e38
PC = {}
_n = 0
for _name, _rows in (("mu_r", 8), ("mu_k", 8), ("mu_v", 8), ("mu_l", 1), ("w0", 8), ("a0", 8), ("k_k", 8), ("k_a", 8),
                     ("r_k", 8), ("gn_w", 8), ("gn_b", 8), ("pre", 16), ("sub", 1)):
    PC[_name] = _n
    _n += _rows
N_PAR = _n


def constants():
    i = np.arange(P)
    s, t = i[:, None], i[None, :]
    same = (s // CH) == (t // CH)
    ident = (s == t).astype(np.float32)
    strict = (same & (s < t)).astype(np.float32)
    incl = ((s % CH) <= np.arange(CH)[None, :]).astype(np.float32)
    centre = ident - same / CH
    block = same.astype(np.float32)
    heads = np.stack([(i < HD), (i >= HD)], 1).astype(np.float32)
    causal = np.where(t <= s, 0.0, NEG).astype(np.float32)
    f32 = np.concatenate([ident, strict, incl, centre, block, heads, heads / HD, causal], 1).astype(np.float32)
    levels = [ident]
    m = 1
    while m < CH:
        levels.append(same & ((s // (2 * m)) == (t // (2 * m))) & ((s // m) % 2 == 0) & ((t // m) % 2 == 1))
        m *= 2
    inside = np.broadcast_to((np.arange(TP) % CH != 0)[None, :], (P, TP))
    f16 = np.concatenate(levels + [inside], 1).astype(np.float16)
    pos = np.arange(L, dtype=np.float32)
    inv = (np.float32(10000.0) ** (-np.arange(0, HD, 2, dtype=np.float32) / np.float32(HD))).astype(np.float32)
    ang = (pos[:, None] * inv[None, :]).astype(np.float32)
    ang = np.concatenate([ang] * 4, 1).T
    turned = np.where(i % HD < HD // 2, -1.0, 1.0)[:, None]
    rope = np.concatenate([np.cos(ang), turned * np.sin(ang)], 1).astype(np.float32)
    return f32, f16, rope


LEVELS = 6
C32 = {}
_n = 0
for _name, _w in (("ident", P), ("strict", P), ("incl", CH), ("centre", P), ("block", P),
                  ("heads", 2), ("heads_mean", 2), ("causal", P)):
    C32[_name] = (_n, _w)
    _n += _w
C32_W = _n


def hybrid_layer(nc, x, meta_tokens, pre_norm_w, w_in, rwkv_mu, rwkv_w0, rwkv_w_up, rwkv_a0, rwkv_a_up,
                 rwkv_k_k, rwkv_k_a, rwkv_r_k, rwkv_gn_w, rwkv_gn_b, lam_q1, lam_k1, lam_q2, lam_k2,
                 subln_w, w_out, post_norm_w, c32_dram, c16_dram, rope_dram, out):
    ctx = ExitStack()
    with ctx:
        def sb(name, shape, dt=F32):
            return ctx.enter_context(nc.sbuf_tensor(name, shape, dt))

        def sem(name):
            return ctx.enter_context(nc.semaphore(name))

        hn_hi = sb("hn_hi", [P, KT, L], F32R)
        hn_lo = sb("hn_lo", [P, KT, L], F32R)
        w_raw = sb("w_raw", [P, RING, UK * P])
        w_hi = sb("w_hi", [P, RING, UK * P], F32R)
        w_lo = sb("w_lo", [P, RING, UK * P], F32R)
        big = sb("big", [P, 4 * D])
        c32 = sb("c32", [P, C32_W])
        c16 = sb("c16", [P, (1 + LEVELS) * P + TP], F16)
        par = sb("par", [P, N_PAR])
        om_mu = sb("om_mu", [P, 25])
        half_w0 = sb("half_w0", [P, 8])
        half_a0 = sb("half_a0", [P, 8])
        half_ka = sb("half_ka", [P, 8])
        om_ka = sb("om_ka", [P, 8])
        gate_sub = sb("gate_sub", [P, 1])
        lam = sb("lam", [P, 1])
        power = sb("power", [P, 16])
        lora = sb("lora", [P, TPX])
        xk = sb("xk", [P, TP])
        xv = sb("xv", [P, TP])
        xr = sb("xr", [P, TP])
        gate = sb("gate", [P, SEQ])
        gate2 = sb("gate2", [P, SEQ])
        tanh_g = sb("tanh_g", [P, SEQ])
        t512b = tanh_g[:]
        ARENA = 16184
        arena = sb("arena", [P, ARENA])
        taken = {}

        def carve(stage, name, n, dt=F32):
            at = taken.get(stage, 0)
            words = n if dt is F32 else n // 2
            taken[stage] = at + words
            assert taken[stage] <= ARENA, (stage, name, taken[stage])
            v = arena[:, at:at + words]
            return v if dt is F32 else v.bitcast(dt)

        ysum = carve("rwkv", "ysum", SEQ)
        t512 = carve("rwkv", "t512", SEQ)
        gn_small = carve("rwkv", "gn_small", 8)
        gn_pow = carve("rwkv", "gn_pow", 8)
        wu = carve("rwkv", "wu", P)
        au = carve("rwkv", "au", P)
        ew = carve("rwkv", "ew", NC * (CH + 1))
        ew3 = ew.rearrange("p (c t) -> p c t", c=NC)
        w_end = carve("rwkv", "w_end", NC)
        kk_small = carve("rwkv", "kk_small", 2 * TG)
        kk_pow = carve("rwkv", "kk_pow", 2 * TG)
        rkp = carve("rwkv", "rkp", TPX)
        tmp = carve("rwkv", "tmp", TPX)
        apad_r = carve("rwkv", "apad_r", NC * (P + CH)).rearrange("p (c t) -> p c t", c=NC)
        apad, rc = apad_r[:, :, 0:P], apad_r[:, :, P:]
        bpad = carve("rwkv", "bpad", NC * P).rearrange("p (c t) -> p c t", c=NC)
        kpad = carve("rwkv", "kpad", NC * P).rearrange("p (c t) -> p c t", c=NC)
        vpad = carve("rwkv", "vpad", NC * P).rearrange("p (c t) -> p c t", c=NC)

        def two(name, n, dt=F32):
            return [carve("rwkv", f"{name}{b}", n, dt) for b in range(2)]

        bk_tok = two("bk_tok", 2 * GC * P)
        v_tok = two("v_tok", GC * P)
        t_t = two("t_t", GC * P)
        state = carve("rwkv", "state", P)
        state0 = carve("rwkv", "state0", P)
        g_sb = carve("rwkv", "g_sb", P)
        u_sb = carve("rwkv", "u_sb", P)
        b_in0 = carve("rwkv", "b_in0", GC * (P + CH))
        k_in0 = carve("rwkv", "k_in0", GC * (P + CH))
        shared = taken["rwkv"]
        emi = carve("rwkv", "emi", TPX)
        tha = carve("rwkv", "tha", TP)
        kk = carve("rwkv", "kk", TP)
        kp = carve("rwkv", "kp", TP)
        taken["rwkv"] = shared
        b_in1 = carve("rwkv", "b_in1", GC * (P + CH))
        k_in1 = carve("rwkv", "k_in1", GC * (P + CH))
        ab_hi = carve("rwkv", "ab_hi", GC * P, F16)
        ab_lo = carve("rwkv", "ab_lo", GC * P, F16)
        lv = carve("rwkv", "lv", (LEVELS - 1) * GC * P, F16)
        x16 = carve("rwkv", "x16", GC * P, F16)
        xt16 = carve("rwkv", "xt16", GC * P, F16)
        z16 = carve("rwkv", "z16", GC * P, F16)

        def beside(*pair):
            three = [v.rearrange("p (c t) -> p c t", c=GC) for v in pair]
            return three, [v[:, :, 0:P] for v in three], [v[:, :, P:] for v in three]

        b_in, ab_in, rb_t = beside(b_in0, b_in1)
        k_in, ak_t, rk_t = beside(k_in0, k_in1)
        r16 = z16
        taken["start"] = 3 * SEQ + TPX
        xm = carve("start", "xm", D)
        par_rows = carve("start", "par_rows", P)
        lam_in = carve("start", "lam_in", 4 * HD)
        lam_p = carve("start", "lam_p", HD)
        lam_s = carve("start", "lam_s", 4)
        norm_s = carve("start", "norm_s", 16)
        junk = carve("start", "junk", D)
        norm_d = carve("start", "norm_d", 5 * P)
        taken["attn"] = 2 * SEQ + 16
        cos_t = carve("attn", "cos_t", L)
        sin_t = carve("attn", "sin_t", L)
        qpad = [carve("attn", f"qpad{m}", SEQ) for m in range(2)]
        kr = carve("attn", "kr", L)
        vt = carve("attn", "vt", TG * P)
        rt1 = carve("attn", "rt1", L)
        q_swap = carve("attn", "q_swap", SEQ)
        k_swap = carve("attn", "k_swap", L)
        prob = [carve("attn", f"prob{m}", L) for m in range(2)]
        attn_t = carve("attn", "attn_t", TG * P)
        o_sb = carve("attn", "o_sb", SEQ)
        o_sq = carve("attn", "o_sq", P)
        at_max = carve("attn", "at_max", 2)
        at_neg = carve("attn", "at_neg", 2)
        at_sum = carve("attn", "at_sum", 2)
        at_inv = carve("attn", "at_inv", 2)
        at_var = carve("attn", "at_var", 4)
        at_pow = carve("attn", "at_pow", 4)
        post_b = carve("end", "post_b", D)
        x_again = [carve("end", f"x_again{b}", D) for b in range(4)]
        sq_junk = carve("end", "sq_junk", SEQ)
        sq_sum = carve("end", "sq_sum", 16)
        sq_tot = carve("end", "sq_tot", 8)
        xin = big[:].rearrange("p (t d) -> p t d", t=4)
        ymix = big[:].rearrange("p (k t) -> p k t", k=KT)
        proj_out = xin

        def c32v(name):
            at, w = C32[name]
            return c32[:, at:at + w]

        def c16v(k):
            return c16[:, k * P:(k + 1) * P]

        ident, ident16 = c32v("ident"), c16v(0)
        inside = c16[:, (1 + LEVELS) * P:]
        level_masks = c16[:, P:(1 + LEVELS) * P].rearrange("p (l t) -> p l t", l=LEVELS)

        tiles = [ctx.enter_context(nc.psum_tensor(f"tile{b}", [P, 1024], F32)) for b in range(2)]
        ma = ctx.enter_context(nc.psum_tensor("ma", [P, 1024], F32))
        mb = ctx.enter_context(nc.psum_tensor("mb", [P, 1024], F32))

        S = {}

        def s(name):
            if name not in S:
                S[name] = sem(name)
            return S[name]

        arrived = [sem(f"arrived{b}") for b in range(RING)]
        block = ctx.enter_context(nc.Block())

        INV_AT, INV_SPAN, INV_STEPS = 12.5, 16.8, 15.19
        CHAIN_LAG, CHAIN_SPAN, CHAIN_STEPS = 0.18, 16, 11
        LATE_AT, LATE_SPAN = 4.97, 7.71
        GN_AT = 10.68
        BONUS_AT = 24
        GATE_AT = 24
        STAGE_DVE = (3.8, 5.03, 6, 6.7, 8.0, 8.58)
        LORA_LAG = 4
        N2_AT = 0.6
        LEVEL_1, LEVEL_2 = 1.6, 3.92

        LAST_COLS = (slice(0, SEQ), slice(SEQ, D))

        def inv_at(g, step):
            return INV_AT + INV_SPAN * g + INV_SPAN * step / INV_STEPS

        def chain_at(g, step, late, work="rwkv"):
            if late:
                return (LATE_AT if work == "rwkv" else 0.5) + LATE_SPAN * step / CHAIN_STEPS
            return INV_AT + INV_SPAN * (g + 1) + CHAIN_LAG + CHAIN_SPAN * step / CHAIN_STEPS

        def groups_so_far(i, g, late=0):
            return i * NG + (g + 1 - NG * (1 + late))

        def chunks_so_far(i, ch, late=0):
            return i * NC + (ch + 1 - NC * (1 + late))

        def rwkv_work(i, work, gn, stage, group_norm, inverse, chain):
            gens = []
            if gn:
                gens += [chain(i, NG - 1, 1, work, gn), group_norm(i, work)]
            if work == "rwkv":
                gens.append(stage(i, gn))
                for g in range(NG):
                    if g < NG - 1:
                        gens.append(chain(i, g, 0, work, gn))
                    gens.append(inverse(i, g))
            return gens

        def gn_at(work):
            return GN_AT if work == "rwkv" else 8.5

        def attn_stage_at(gn):
            return 12 if gn else 0

        def attn_at(gn, qi):
            return 20.5 + 12.2 * qi if gn else 6.5 + 13.0 * qi

        def mixed(i):
            return ymix[:, i, :] if isinstance(i, int) else ymix[:, bass.ds(i, 1), :].rearrange("p a t -> p (a t)")

        def column(table, at, i):
            return table[:, at + i:at + i + 1] if isinstance(i, int) else table[:, bass.ds(i + at, 1)]

        def out_banks(n):
            a, b = (tiles[0], tiles[1]) if n % 2 == 0 else (ma, mb)
            return [a[:, 0:512], a[:, 512:1024], b[:, 0:512], b[:, 512:1024]]

        def squares(act, n):
            for t in range(4):
                if t < 3:
                    act.wait_ge(s("rows_done"), 3 * n + t + 1)
                else:
                    act.wait_ge(s("unit_used"), UPT * N_TILES + KT * (n + 1))
                if n + t:
                    act.wait_ge(s("out_sq"), 4 * n + t)
                nc.scalar.activation(sq_junk, out_banks(n)[t], ACT.Square,
                                     accum_out=sq_sum[:, 4 * t + n:4 * t + n + 1]).then_inc(s("out_sq"), 1)

        def upto(gens, place):
            while True:
                due = [g for g in gens if g[1] is not None and g[1] <= place]
                if not due:
                    return
                g = min(due, key=lambda g: g[1])
                g[1] = next(g[0], None)

        def begin(*gens):
            return [[g, next(g, None)] for g in gens]

        def unit_of(i, k):
            return i * 16 + (UPT + k)

        class Steps:
            def __init__(self, eng, name):
                self.eng, self.sm, self.n = eng, s(name), 0

            def __call__(self, ins):
                self.n += 1
                ins.then_inc(self.sm, 1)
                self.eng.wait_ge(self.sm, self.n)

            def quiet(self, ins):
                self.n += 1
                ins.then_inc(self.sm, 1)

            def clear(self):
                if self.n:
                    self.eng.wait_ge(self.sm, self.n)
                    self.eng.sem_clear(self.sm)
                self.n = 0

        ITER = ([(0, "rwkv", None, False), (1, "rwkv", "rwkv", False)], (2, 8, "rwkv", "rwkv", True),
                [(8, "attn", "rwkv", True), (9, "attn", "attn", True)], (10, 16, "attn", "attn", False),
                [(16, None, "attn", False)])

        def iterations(eng, body):
            for part in ITER:
                if isinstance(part, list):
                    for i, proj, work, gn in part:
                        body(i, proj, work, gn)
                else:
                    lo, hi, proj, work, gn = part
                    with eng.Fori(lo, hi) as i:
                        body(i, proj, work, gn)

        @block.sync
        def _(sp):
            xs = x[0].rearrange("(t p) d -> p t d", p=P)
            sp.dma_start(xm[0:META, :], meta_tokens).then_inc(s("meta_in"), 16)
            sp.dma_start(xin[:, 0, :], xs[:, 0, :]).then_inc(s("x_in0"), 16)
            sp.dma_start(c32[:], c32_dram).then_inc(s("const_in"), 16)
            for t in range(1, 4):
                sp.dma_start(xin[:, t, :], xs[:, t, :]).then_inc(s(f"x_in{t}"), 16)
            sp.dma_start(par_rows[0:25, :], rwkv_mu[0].rearrange("(r c) -> r c", c=P)).then_inc(s("par_in"), 16)
            for name, src in (("w0", rwkv_w0[0]), ("a0", rwkv_a0[0]), ("k_k", rwkv_k_k[0]), ("k_a", rwkv_k_a[0]),
                              ("gn_w", rwkv_gn_w[0]), ("gn_b", rwkv_gn_b[0]),
                              ("r_k", rwkv_r_k[0].rearrange("h d -> (h d)")),
                              ("pre", pre_norm_w[0]), ("sub", subln_w[0])):
                rows = src.shape[0] // P
                sp.dma_start(par_rows[PC[name]:PC[name] + rows, :],
                             src.rearrange("(r c) -> r c", c=P)).then_inc(s("par_in"), 16)

            def load_unit(slot, col, rows0):
                src = w_in[0, rows0:rows0 + UK * P, col].rearrange("(k p) c -> p k c", p=P)
                sp.dma_start(w_raw[:, slot, :].rearrange("p (k c) -> p k c", k=UK),
                             src).then_inc(arrived[slot], 16)

            for h in range(UPT):
                load_unit(h, slice(LORA_COL, LORA_COL + P), h * UK * P)
            sp.dma_start(c16[:], c16_dram).then_inc(s("const16_in"), 16)
            for n, v in enumerate((lam_q1, lam_k1, lam_q2, lam_k2)):
                sp.dma_start(lam_in[:, n * HD:(n + 1) * HD],
                             v[0:1, :].broadcast_to([P, HD])).then_inc(s("lam_in"), 16)

            def body(i, proj, work, gn):
                if proj is None:
                    return
                first = 0 if proj == "rwkv" else NP_
                for k in range(16):
                    if k == 9 and isinstance(i, int) and i == 9:
                        sp.wait_ge(s("s_taken"), NP_ * NC)
                        sp.wait_ge(s("y_done"), NP_ * NG)
                        sp.dma_start(cos_t, rope_dram[:, 0:L]).then_inc(s("rope_in"), 16)
                        sp.dma_start(sin_t, rope_dram[:, L:2 * L]).then_inc(s("rope_in"), 16)
                    lora_next = k == 7 and proj == "rwkv"
                    q, h = divmod(k, UPT)
                    at = i * P + (TILE_COLS[proj][q] - first * P)
                    col = bass.ds(at if isinstance(i, int) else sp.snap(at), P)
                    sp.wait_ge(s("lo_done"), unit_of(i, k) - (RING - 1))
                    if lora_next and isinstance(i, int) and i == 0:
                        sp.wait_ge(s("zeroed"), 1)
                    elif lora_next:
                        sp.wait_ge(s("z_done"), i)
                        sp.wait_ge(s("a_done"), i)
                    load_unit(h, col, h * UK * P)
                    if lora_next:
                        c = slice(0, P) if isinstance(i, int) and i == 0 else bass.ds(i * P, P)
                        sp.dma_start(wu[0:HD, :], rwkv_w_up[0, :, c]).then_inc(s("lora_w_in"), 16)
                        sp.dma_start(au[HD:P, :], rwkv_a_up[0, :, c]).then_inc(s("lora_w_in"), 16)

            iterations(sp, body)
            def out_units(n, features=range(KT)):
                for k in features:
                    src = w_out[0, k * P:(k + 1) * P, bass.ds(n * SEQ, SEQ)]
                    sp.wait_ge(s("lo_done"), n * KT + (UPT * N_TILES + k - (RING - 1)))
                    sp.dma_start(w_raw[:, k % RING, :], src
                                 ).then_inc(arrived[k % RING], 16)

            out_units(0)
            out_units(1, range(0, RING))
            sp.wait_ge(s("o_made"), NP_)
            sp.dma_start(post_b, post_norm_w[0:1, :].broadcast_to([P, D])).then_inc(s("post_in"), 16)
            out_units(1, range(RING, KT))
            for t in range(4):
                sp.dma_start(x_again[t], xs[:, t, :]).then_inc(s("x_back"), 16)
            with sp.Fori(2, 4) as n:
                out_units(n)
            outs = out[0].rearrange("(t p) d -> p t d", p=P)
            for h, cols in enumerate(LAST_COLS):
                for t in range(4):
                    if t < 3:
                        sp.wait_ge(s("out_made"), 3 * h + t + 1)
                    else:
                        sp.wait_ge(s("out_made_pool"), h + 1)
                    sp.dma_start(outs[:, t, cols], proj_out[:, t, cols]).then_inc(s("out_stored"), 16)
            sp.wait_ge(s("out_stored"), 16 * 8)

        @block.tensor
        def _(pe):
            mm = nc.tensor.matmul

            def feature_tile(o, slot, h, kk_, full, gens=(), place=0):
                kt = h * UK + kk_
                cols = slice(kk_ * P, (kk_ + 1) * P)
                parts = (((EDGE, 0, L // 2), (512, L // 2, L // 2)) if full else ((0, META, SEQ),))
                for part, (w, t) in enumerate(((w_hi, hn_hi), (w_hi, hn_lo), (w_lo, hn_hi))):
                    if part:
                        upto(gens, place - 1 + part / 3)
                    for at, tok, n in parts:
                        last = mm(o[:, at:at + n], w[:, slot, cols], t[:, kt, tok:tok + n],
                                  start=(kt == 0 and w is w_hi and t is hn_hi),
                                  stop=(kt == KT - 1 and w is w_lo))
                return last

            pe.wait_ge(s("const_in"), 16)
            pe.wait_ge(s("par_in"), 16 * 10)
            nc.tensor.transpose(ma[:, 0:N_PAR], par_rows[0:N_PAR, :], ident[0:N_PAR, 0:N_PAR]
                                ).then_inc(s("par_turned"), 1)
            pe.wait_ge(s("par_made"), 1)
            pe.wait_ge(s("norm_spread"), 5)
            for k in range(KT + LORA_LAG):
                if k < KT:
                    o = (ma, mb)[k % 2]
                    if k >= 2:
                        pe.wait_ge(s("hn_lo_made"), k - 1)
                    mm(o[:, TURN:TURN + META], xm[0:META, k * P:(k + 1) * P], norm_d[0:META, 4 * P:4 * P + META],
                       start=True, stop=True)
                    for t in range(4):
                        at = TURN + META + t * P
                        last = mm(o[:, at:at + P], xin[:, t, k * P:(k + 1) * P], norm_d[:, t * P:(t + 1) * P],
                                  start=True, stop=True)
                    last.then_inc(s("x_turned"), 1)
                if k >= LORA_LAG:
                    h, c = divmod(k - LORA_LAG, UK)
                    pe.wait_ge(s("hn_lo_made"), k - LORA_LAG + 1)
                    pe.wait_ge(s("lo_done"), h + 1)
                    last = feature_tile(tiles[0], h, h, c, True)
                    if c == UK - 1:
                        last.then_inc(s("unit_used"), 1)

            pe.wait_ge(s("const16_in"), 16)

            def gn_pe(i, work):
                n = i - 1
                yield gn_at(work) + 2
                if work == "rwkv":
                    pe.wait_ge(s("a_made"), i)
                pe.wait_ge(s("y_taken"), n * NG)
                pe.wait_ge(s("s_taken"), n * NC)
                mm(mb[:, 0:SEQ], c32v("centre"), ysum, start=True, stop=True).then_inc(s("centre_done"), 1)
                yield gn_at(work) + 4
                pe.wait_ge(s("centre_taken"), n * 2)
                for m in range(4):
                    last = mm(mb[:, 512 + 2 * m:514 + 2 * m], t512b[:, m * P:(m + 1) * P], c32v("heads_mean"),
                              start=True, stop=True)
                last.then_inc(s("var_done"), 1)
                yield gn_at(work) + 7
                pe.wait_ge(s("gn_spread"), n)
                for m in range(4):
                    last = nc.tensor.transpose(mb[:, 512 + m * P:512 + (m + 1) * P], t512b[:, m * P:(m + 1) * P],
                                               ident)
                last.then_inc(s("gn_turned"), 1)

            def stage_pe(i, gn):
                n = i
                yield 0
                pe.wait_ge(s("lora_made"), 1)
                pe.wait_ge(s("lora_w_in"), n * 32)
                if gn:
                    pe.wait_ge(s("inv_taken"), n * NG - NG)
                    pe.wait_ge(s("s_taken"), n * NC - (NC + GC))
                    pe.wait_ge(s("y_taken"), n * NG - (NG + 1))
                mm(ma[:, 0:512], wu, lora[:, 0:512], start=True, stop=True)
                mm(ma[:, 512:TP], wu, lora[:, 512:TP], start=True, stop=True).then_inc(s("z_done"), 1)
                yield N2_AT
                pe.wait_ge(s("sq_made"), n)
                for m in range(TG):
                    last = mm(mb[:, 2 * m:2 * m + 2], rkp[:, m * P:(m + 1) * P], c32v("heads"), start=True, stop=True)
                last.then_inc(s("n2_done"), 1)
                yield 1.5
                pe.wait_ge(s("n2_taken"), n)
                mm(mb[:, 0:512], au, lora[:, 0:512], start=True, stop=True)
                mm(mb[:, 512:TP], au, lora[:, 512:TP], start=True, stop=True).then_inc(s("a_done"), 1)
                yield 3.5
                pe.wait_ge(s("a_made"), n)
                pe.wait_ge(s("kk_spread"), n)
                for m in range(TG):
                    last = nc.tensor.transpose(mb[:, m * P:(m + 1) * P], emi[:, m * P:(m + 1) * P], ident)
                last.then_inc(s("kk_turned"), 1)
                yield BONUS_AT
                pe.wait_ge(s("rkp_made"), n)
                pe.wait_ge(s("kk_made"), n)
                if gn:
                    pe.wait_ge(s("y_made"), n - 1)
                mm(mb[:, 0:SEQ], c32v("block"), rkp[:, CH:TP], start=True, stop=True).then_inc(s("bonus_done"), 1)

            def inv_pe(i, g):
                n = groups_so_far(i, g)
                cs = [g * GC + c for c in range(GC)]
                bl = lambda v, c: v[:, c * P:(c + 1) * P]
                bank = lambda k, c: ma[:, k * 512 + c * P:k * 512 + (c + 1) * P]
                yield inv_at(g, 0)
                if g == 0:
                    pe.wait_ge(s("bk_made"), i)
                    pe.wait_ge(s("pads_made"), i)
                    pe.wait_ge(s("z_tanh"), i)
                else:
                    pe.wait_ge(s("inv_taken"), n - 1)
                for f, (pad, done) in enumerate(((bpad, "ab_done"), (kpad, "kb_done"))):
                    if f:
                        yield inv_at(g, 1)
                        pe.wait_ge(s("ab_taken"), n)
                    for c in range(GC):
                        last = mm(ma[:, c * 256:c * 256 + P + CH], pad[:, cs[c], :], apad_r[:, cs[c], :],
                                  start=True, stop=True)
                    last.then_inc(s(done), 1)
                yield inv_at(g, 2.2)
                pe.wait_ge(s("kb_taken"), n)
                pe.wait_ge(s("first_made"), n)
                for c in range(GC):
                    last = mm(bank(0, c), bl(xt16, c), ident16, start=True, stop=True)
                last.then_inc(s("t0_done"), 1)
                turns = ((bpad, "b_turned", "b_taken"), (kpad, "k_turned", "k_taken"), (vpad, "v_turned", "v_taken"))
                for l in range(1, LEVELS):
                    yield inv_at(g, 1.2 + 2 * l)
                    if l == 1:
                        pe.wait_ge(s("t0_taken"), n)
                        pe.wait_ge(s("level_1_made"), n)
                    else:
                        pe.wait_ge(s("x_taken"), n * 5 + (l - 1 - 5))
                        pe.wait_ge(s("xt_taken"), n * 5 + (l - 1 - 5))
                        if l == 2:
                            pe.wait_ge(s("levels_made"), n)
                    for c in range(GC):
                        last = mm(bank(1, c), bl(lv, (l - 1) * GC + c), bl(x16, c), start=True, stop=True)
                    last.then_inc(s("zz_done"), 1)
                    if l <= 3:
                        pad, turned, _ = turns[l - 1]
                        if g == 0 and l == 3:
                            pe.wait_ge(s("vpad_made"), i * 2)
                        for c in range(GC):
                            last = nc.tensor.transpose(bank(0, c), pad[:, cs[c], :], ident)
                        last.then_inc(s(turned), 1)
                    yield inv_at(g, 2.2 + 2 * l)
                    pe.wait_ge(s("zz_taken"), n * 5 + (l - 5))
                    if l <= 3:
                        pe.wait_ge(s(turns[l - 1][2]), n)
                    for c in range(GC):
                        last = mm(bank(0, c), bl(xt16, c), bl(z16, c), start=True, stop=True)
                    last.then_inc(s("x_done"), 1)
                    for c in range(GC):
                        last = mm(bank(1, c), bl(z16, c), bl(xt16, c), start=True, stop=True)
                    last.then_inc(s("xt_done"), 1)
                yield inv_at(g, 13.2)
                pe.wait_ge(s("xt_taken"), n * 5)
                pe.wait_ge(s("x_taken"), n * 5)
                for c in range(GC):
                    mm(bank(1, c), bl(ab_hi, c), bl(x16, c), start=True, stop=False)
                    last = mm(bank(1, c), bl(ab_lo, c), bl(x16, c), start=False, stop=True)
                last.then_inc(s("r_done"), 1)
                yield inv_at(g, 14.2)
                pe.wait_ge(s("r_taken"), n)
                for c in range(GC):
                    mm(bank(0, c), bl(x16, c), ident16, start=True, stop=False)
                    last = mm(bank(0, c), bl(r16, c), bl(xt16, c), start=False, stop=True)
                last.then_inc(s("inv_done"), 1)

            def chain_pe(i, g, late, work, gn):
                b = g % 2
                n = groups_so_far(i, g, late)
                for c in range(GC):
                    ch = g * GC + c
                    m = chunks_so_far(i, ch, late)
                    yield chain_at(g, 0.5 + 3 * c, late, work)
                    if c == 0:
                        pe.wait_ge(s("inv_taken"), n)
                        if late and work == "rwkv":
                            pe.wait_ge(s("kk_made"), i)
                        if g == 0:
                            pe.wait_ge(s("state_zeroed"), i)
                            pe.wait_ge(s("bonus_taken"), i)
                    if ch > 0:
                        pe.wait_ge(s("s_taken"), m - 1)
                        if g > 0 and c == 0:
                            pe.wait_ge(s("y_taken"), n - 1)
                    o = mb[:, 0:P]
                    vb = v_tok[b][:, c * P:(c + 1) * P]
                    if ch > 0:
                        mm(o, apad[:, ch, :], state, start=True, stop=False)
                    mm(o, ak_t[b][:, c, :], vb, start=(ch == 0), stop=True).then_inc(s("g_done"), 1)
                    yo = mb[:, 512 + c * CH:512 + (c + 1) * CH]
                    if ch > 0:
                        mm(yo, state, rc[:, ch, :], start=True, stop=False)
                        mm(yo, vb, rk_t[b][:, c, :], start=False, stop=False)
                    yield chain_at(g, 1.5 + 3 * c, late, work)
                    pe.wait_ge(s("g_taken"), m)
                    mm(o, t_t[b][:, c * P:(c + 1) * P], g_sb, start=True, stop=True).then_inc(s("u_done"), 1)
                    yield chain_at(g, 2.5 + 3 * c, late, work)
                    pe.wait_ge(s("u_taken"), m)
                    mm(o, bk_tok[b][:, c * P:(c + 1) * P], u_sb, start=True, stop=False)
                    mm(o, bk_tok[b][:, (GC + c) * P:(GC + c + 1) * P], vb, start=False,
                       stop=True).then_inc(s("s_done"), 1)
                    if ch > 0:
                        last = mm(yo, u_sb, rb_t[b][:, c, :], start=False, stop=True)
                        if c == GC - 1:
                            last.then_inc(s("y_done"), 1)

            def attn_stage_pe(i, gn):
                n = i - NP_
                at = attn_stage_at(gn)
                yield at
                if gn:
                    pe.wait_ge(s("inv_taken"), NP_ * NG)
                else:
                    pe.wait_ge(s("o_made"), n - 1)
                pe.wait_ge(s("tile_freed"), i * 4)
                for m in range(4):
                    nc.tensor.transpose(ma[:, m * P:(m + 1) * P], xr[:, m * P:(m + 1) * P], ident)
                nc.tensor.transpose(ma[0:META, 512:512 + P], xr[:, 512:L], ident).then_inc(s("vt_turned"), 1)

            def attn_pe(i, gn):
                n = i - NP_
                for qi in range(4):
                    base = attn_at(gn, qi)
                    c = n * 4 + (qi - 3)
                    width = META + (qi + 1) * P
                    yield base
                    if qi == 0:
                        if gn:
                            pe.wait_ge(s("y_made"), NP_)
                        pe.wait_ge(s("roped"), n * 2)
                        pe.wait_ge(s("vt_taken"), n * 2)
                    else:
                        pe.wait_ge(s("at_taken"), c - 1)
                        pe.wait_ge(s("o_taken"), c - 1)
                        pe.wait_ge(s("o_squared"), c - 1)
                    for m, o in ((0, ma), (1, mb)):
                        lhs = qpad[m][:, qi * P:(qi + 1) * P]
                        if qi == 3:
                            mm(o[:, EDGE:512], lhs, kr[:, 0:L // 2], start=True, stop=True)
                            last = mm(o[:, 512:EDGE + L], lhs, kr[:, L // 2:L], start=True, stop=True)
                        else:
                            last = mm(o[:, 0:width], lhs, kr[:, 0:width], start=True, stop=True)
                        last.then_inc(s("score_done"), 1)
                    yield base + 7
                    pe.wait_ge(s("combined"), c)
                    for m in range(qi + 1):
                        nc.tensor.transpose(ma[:, m * P:(m + 1) * P], prob[0][:, m * P:(m + 1) * P], ident)
                    m = qi + 1
                    nc.tensor.transpose(ma[0:META, 512:512 + P], prob[0][:, m * P:m * P + META],
                                        ident).then_inc(s("at_turned"), 1)
                    yield base + 10
                    pe.wait_ge(s("at_taken"), c)
                    o = mb[:, 0:P]
                    for m in range(qi + 1):
                        mm(o, attn_t[:, m * P:(m + 1) * P], vt[:, m * P:(m + 1) * P], start=(m == 0), stop=False)
                    m = qi + 1
                    mm(o, attn_t[0:META, 4 * P:5 * P], vt[0:META, m * P:(m + 1) * P], start=False,
                       stop=True).then_inc(s("pv_done"), 1)
                at = attn_at(gn, 3)
                yield at + 14
                pe.wait_ge(s("o_scaled"), n)
                for m in range(4):
                    last = nc.tensor.transpose(ma[:, m * P:(m + 1) * P], o_sb[:, m * P:(m + 1) * P], ident)
                last.then_inc(s("o_turned"), 1)

            def out_feature(n, k, gens=()):
                banks = out_banks(n)
                pe.wait_ge(s("lo_done"), UPT * N_TILES + n * KT + k + 1)
                if n == 0:
                    pe.wait_ge(s("y_lo"), k + 1)
                for t in range(4):
                    y = slice(t * P, (t + 1) * P)
                    mm(banks[t], hn_hi[:, k, y], w_hi[:, k % RING, :], start=(k == 0), stop=False)
                    mm(banks[t], hn_hi[:, k, y], w_lo[:, k % RING, :], start=False, stop=False)
                    last = mm(banks[t], hn_lo[:, k, y], w_hi[:, k % RING, :], start=False, stop=(k == KT - 1))
                    if t == 3:
                        last.then_inc(s("unit_used"), 1)
                    elif k == KT - 1:
                        last.then_inc(s("rows_done"), 1)
                    upto(gens, 4 * k + t)

            def body(i, proj, work, gn):
                gens = rwkv_work(i, work, gn, stage_pe, gn_pe, inv_pe, chain_pe)
                if work == "attn":
                    gens += [attn_stage_pe(i, gn), attn_pe(i, gn)]
                gens = begin(*gens)
                if proj is None:
                    upto(gens, -1)
                    pe.wait_ge(s("tile_freed"), N_TILES)
                    for k in range(KT - 1):
                        out_feature(0, k, gens)
                    upto(gens, 1000)
                    out_feature(0, KT - 1)
                    return
                for k in range(16):
                    q, h = divmod(k, UPT)
                    if proj is not None:
                        u = unit_of(i, k)
                        g = i * 4 + (q + 1)
                        if h == 0 and not (isinstance(i, int) and i == 0 and q == 0):
                            pe.wait_ge(s("tile_freed"), g - 1)
                        pe.wait_ge(s("lo_done"), u + 1)
                    for c in range(UK):
                        if proj is not None:
                            last = feature_tile(tiles[(q + 1) % 2], h, h, c, FULL[proj][q],
                                                gens if work == "rwkv" else (), k * UK + c)
                            if c == UK - 1:
                                last.then_inc(s("unit_used"), 1)
                        upto(gens, k * UK + c)
                upto(gens, 1000)

            iterations(pe, body)

            pe.wait_ge(s("o_made"), NP_)
            for n in range(1, 4):
                if n >= 2:
                    pe.wait_ge(s("out_taken"), 4 * (n - 1))
                for k in range(KT):
                    out_feature(n, k)

        @block.scalar
        def _(act):
            A = nc.scalar.activation
            steps = Steps(act, "act_step")

            def split_hi(u, slot, turn):
                act.wait_ge(arrived[slot], turn * 16)
                if not (isinstance(u, int) and u < RING):
                    act.wait_ge(s("unit_used"), u - (RING - 1))
                nc.scalar.copy(w_hi[:, slot, :], w_raw[:, slot, :]).then_inc(s("hi_done"), 1)

            for n, t in enumerate((4, 0, 1, 2, 3)):
                act.wait_ge(s(f"x_in{t}" if t < 4 else "meta_in"), 16)
                if n:
                    act.wait_ge(s("norm_sq"), n)
                v = xin[:, t, :] if t < 4 else xm[0:META, :]
                rows = P if t < 4 else META
                A(junk[0:rows, :], v, ACT.Square, accum_out=norm_s[0:rows, t:t + 1]).then_inc(s("norm_sq"), 1)
            act.wait_ge(s("par_made"), 1)
            for k in range(KT):
                act.wait_ge(s("x_turned"), k + 1)
                o = (ma, mb)[k % 2]
                A(hn_hi[:, k, :], o[:, TURN:TURN + L], ACT.Copy,
                  scale=par[:, PC["pre"] + k:PC["pre"] + k + 1]).then_inc(s("hn_hi_made"), 1)
                if k < UPT:
                    split_hi(k, k, 1)
                elif k % UK == 2 and k >= UPT + UK:
                    u = UPT + (k - UPT) // UK - 1
                    split_hi(u, u % RING, 2)
            split_hi(UPT + 2, (UPT + 2) % RING, 2)
            act.wait_ge(s("lam_dots"), 2)
            A(lam_s[:, 2:4], lam_s[:, 0:2], ACT.Exp).then_inc(s("lam_exp"), 1)
            split_hi(UPT + AHEAD, (UPT + AHEAD) % RING, 2)
            act.wait_ge(s("unit_used"), UPT)
            act.wait_ge(s("zeroed"), 1)
            A(lora[:, PAD:TP], tiles[0][:, EDGE:EDGE + L], ACT.Copy, scale=om_mu[:, 24:25]).then_inc(s("lora_base"), 1)
            act.wait_ge(s("tile_freed"), 1)
            A(lora[0:HD, PAD:TP], lora[0:HD, PAD:TP], ACT.Tanh).then_inc(s("lora_made"), 1)

            def swap_halves(f):
                swap, src, w = ((q_swap, xk, SEQ), (k_swap, xv, L))[f]
                for rows in range(0, P, HD // 2):
                    other = rows ^ (HD // 2)
                    A(swap[rows:rows + HD // 2, 0:w], src[other:other + HD // 2, 0:w],
                      ACT.Copy).then_inc(s("swapped"), 1)

            def tile_act(i, proj, work, gn):
                if proj == "rwkv":
                    for q, (xt, mu) in enumerate(((xk, 8), (xv, 16), (xr, 0))):
                        yield 16 * q + 15.5
                        act.wait_ge(s("unit_used"), i * 16 + (8 + 4 * q))
                        if work == "rwkv":
                            act.wait_ge(s("bonus_taken" if q == 1 else "pads_made"), i)
                        A(xt[:, PAD:TP], tiles[(q + 1) % 2][:, EDGE:EDGE + L], ACT.Copy,
                          scale=column(om_mu, mu, i)).then_inc(s("x_based"), 1)
                elif work == "attn":
                    for f in range(2):
                        yield 20.8 if gn and f == 0 else 16 * f + 16.3
                        act.wait_ge(s("tile_freed"), i * 4 + (f + 2))
                        act.wait_ge(s("roped"), (i - NP_) * 2 + (f - 1))
                        swap_halves(f)
                yield 63.5
                act.wait_ge(s("unit_used"), i * 16 + 20)
                A(tanh_g[:], tiles[0][:, 0:SEQ], ACT.Tanh, scale=0.5).then_inc(s("gate_tanh"), 1)

            def gn_act(i, work):
                n = i - 1
                yield gn_at(work) + 2.5
                act.wait_ge(s("centre_done"), n)
                act.wait_ge(s("tile_freed"), i * 4 + 1)
                A(t512, mb[:, 0:SEQ], ACT.Copy).then_inc(s("centre_taken"), 1)
                A(t512b, mb[:, 0:SEQ], ACT.Square).then_inc(s("centre_taken"), 1)
                yield gn_at(work) + 6
                act.wait_ge(s("gn_powed"), n)
                A(t512b.rearrange("p (m d) -> p m d", d=HD), gn_pow.unsqueeze(2).broadcast_to([P, 8, HD]),
                  ACT.Copy).then_inc(s("gn_spread"), 1)

            def stage_act(i, gn):
                n = i
                yield 0
                act.wait_ge(s("tile_freed"), i * 4 - 2)
                if gn:
                    act.wait_ge(s("bonus_taken"), n - 1)
                A(rkp[:, 0:TP], xk[:], ACT.Square, scale=column(par, PC["k_k"], i - 1)).then_inc(s("sq_made"), 1)
                yield 1.5
                act.wait_ge(s("z_done"), n)
                act.wait_ge(s("zeroed"), 1)
                A(tmp[:, PAD:TP], ma[:, PAD:TP], ACT.Tanh, scale=0.5,
                  bias=column(half_w0, 0, i - 1)).then_inc(s("z_tanh"), 1)
                yield 2.5
                act.wait_ge(s("a_done"), n)
                act.wait_ge(s("zeroed"), 1)
                A(tha, mb[:, 0:TP], ACT.Tanh, scale=0.5, bias=column(half_a0, 0, i - 1)).then_inc(s("a_made"), 1)
                yield 3
                act.wait_ge(s("kk_powed"), n)
                A(emi.rearrange("p (m d) -> p m d", d=HD), kk_pow.unsqueeze(2).broadcast_to([P, 2 * TG, HD]),
                  ACT.Copy).then_inc(s("kk_spread"), 1)
                yield 4
                act.wait_ge(s("cum_made"), n)
                act.wait_ge(s("kk_turned"), n)
                if gn:
                    act.wait_ge(s("ends_made"), n - 1)
                cum = tmp[:, 0:TP]
                A(emi[:, 0:TP], cum, ACT.Exp, scale=-1.0).then_inc(s("e_made"), 1)
                A(ew3[:, :, 1:], cum.rearrange("p (c t) -> p c t", c=NC), ACT.Exp).then_inc(s("e_made"), 1)
                yield 5
                act.wait_ge(s("tile_freed"), i * 4 - 1)
                for h in range(2):
                    A(vpad[h * HD:(h + 1) * HD, :, h * CH:(h + 1) * CH],
                      xv[h * HD:(h + 1) * HD, :].rearrange("p (c t) -> p c t", c=NC),
                      ACT.Copy).then_inc(s("vpad_made"), 1)
                yield 14.5
                if gn:
                    act.wait_ge(s("s_taken"), n * NC - NC)
                    act.wait_ge(s("s_scaled"), n * NC - NC)
                act.wait_ge(s("e_made"), n * 2)
                A(w_end, ew3[:, :, CH], ACT.Copy).then_inc(s("ends_made"), 1)
                yield GATE_AT
                if gn:
                    act.wait_ge(s("y_made"), n - 1)
                act.wait_ge(s("tile_freed"), i * 4 + 1)
                A(gate2[:], gate[:], ACT.Copy).then_inc(s("gate_moved"), 1)

            def inv_act(i, g):
                b = g % 2
                n = groups_so_far(i, g)
                W = GC * P
                yield inv_at(g, 2.7)
                act.wait_ge(s("t0_done"), n)
                A(x16, ma[:, 0:W], ACT.Copy).then_inc(s("t0_taken"), 1)
                turns = ((bk_tok[b][:, 0:W], "b_turned", "b_taken"), (bk_tok[b][:, W:2 * W], "k_turned", "k_taken"),
                         (v_tok[b], "v_turned", "v_taken"))
                for l in range(1, LEVELS):
                    if l <= 3:
                        yield inv_at(g, 1.7 + 2 * l)
                        dst, turned, taken_ = turns[l - 1]
                        act.wait_ge(s(turned), n)
                        if l == 1 and (g == 2 or not (isinstance(i, int) and i == 1)):
                            act.wait_ge(s("s_done"), n * GC - (1, 3, 2)[g] * GC)
                        A(dst, ma[:, 0:W], ACT.Copy).then_inc(s(taken_), 1)
                    yield inv_at(g, 2.7 + 2 * l)
                    act.wait_ge(s("x_done"), n * 5 + (l - 5))
                    A(x16, ma[:, 0:W], ACT.Copy).then_inc(s("x_taken"), 1)

            def chain_act(i, g, late, work, gn):
                n = groups_so_far(i, g, late)
                for c in range(GC):
                    ch = g * GC + c
                    m = chunks_so_far(i, ch, late)
                    yield chain_at(g, 0.8 + 3 * c, late, work)
                    if ch == 0:
                        act.wait_ge(s("ends_made"), i)
                        act.wait_ge(s("state_zeroed"), i)
                    else:
                        act.wait_ge(s("s_taken"), m - 1)
                    A(state0, state, ACT.Copy, scale=w_end[:, ch:ch + 1]).then_inc(s("s_scaled"), 1)
                yield chain_at(g, 9, late, work)
                act.wait_ge(s("y_done"), n)
                lo = max(0, g * GC * CH - CH)
                w = (g + 1) * GC * CH - CH - lo
                A(ysum[:, lo:lo + w], mb[:, 512 + GC * CH - w:512 + GC * CH], ACT.Copy).then_inc(s("y_taken"), 1)

            def attn_act(i, gn):
                n = i - NP_
                at = attn_stage_at(gn)
                if gn:
                    for f in range(2):
                        yield 11.6 + 4 * f
                        act.wait_ge(s("tile_freed"), i * 4 - 1)
                        act.wait_ge(s("arena_freed"), 1)
                        swap_halves(f)
                yield at + 1
                act.wait_ge(s("vt_turned"), n)
                A(vt[:, 0:SEQ], ma[:, 0:SEQ], ACT.Copy).then_inc(s("vt_taken"), 1)
                A(vt[0:META, 512:512 + P], ma[0:META, 512:512 + P], ACT.Copy).then_inc(s("vt_taken"), 1)
                yield 20.9 if gn else at + 1
                if gn:
                    act.wait_ge(s("y_made"), NP_)
                else:
                    act.wait_ge(s("o_made"), n - 1)
                act.wait_ge(s("tile_freed"), i * 4 + 1)
                A(gate2[:], gate[:], ACT.Copy).then_inc(s("gate_moved"), 1)
                for qi in range(4):
                    base = attn_at(gn, qi)
                    c = n * 4 + (qi - 3)
                    at = EDGE if qi == 3 else 0
                    width = META + (qi + 1) * P
                    for m, o in ((0, ma), (1, mb)):
                        yield base + 3 + m
                        act.wait_ge(s("neg_made"), c * 2 + (m - 1))
                        A(prob[m][:, 0:width], o[:, at:at + width], ACT.Exp, scale=HD ** -0.5,
                          bias=at_neg[:, m:m + 1], accum_out=at_sum[:, m:m + 1]).then_inc(s("exp_made"), 1)
                    yield base + 8
                    act.wait_ge(s("at_turned"), c)
                    w = (qi + 1) * P
                    steps.quiet(A(attn_t[:, 0:w], ma[:, 0:w], ACT.Copy))
                    A(attn_t[0:META, 512:512 + P], ma[0:META, 512:512 + P], ACT.Copy).then_inc(s("at_taken"), 1)
                    yield base + 11.5
                    act.wait_ge(s("o_taken"), c)
                    A(o_sq, o_sb[:, qi * P:(qi + 1) * P], ACT.Square,
                      accum_out=at_var[:, qi:qi + 1]).then_inc(s("o_squared"), 1)

            def split_y_act():
                act.wait_ge(s("unit_used"), UPT * N_TILES)
                for k in range(KT):
                    yield max(4 * k - 7, -1) if k < KT - 1 else 200
                    act.wait_ge(s("y_made" if k < NP_ else "o_made"), k % NP_ + 1)
                    A(hn_hi[:, k, 0:SEQ], ymix[:, k, :], ACT.Copy).then_inc(s("y_hi"), 1)

            def body(i, proj, work, gn):
                gens = rwkv_work(i, work, gn, stage_act, gn_act, inv_act, chain_act)
                if work == "attn":
                    gens.append(attn_act(i, gn))
                if proj is not None:
                    gens.append(tile_act(i, proj, work, gn))
                else:
                    gens.append(split_y_act())
                gens = begin(*gens)
                for k in range(16):
                    if not (isinstance(i, int) and i == 0 and k == 0):
                        split_hi(unit_of(i, k + AHEAD), (k + AHEAD) % RING, i * 4 + (2 + (k + AHEAD) // UPT))
                    upto(gens, k * UK + 3)
                upto(gens, 1000)
                steps.clear()

            iterations(act, body)

            for n in range(1, 4):
                for k in range(KT):
                    u = UPT * N_TILES + n * KT + k + AHEAD
                    if u < UPT * N_TILES + 4 * KT:
                        split_hi(u, u % RING, u // RING + 1)
                    if k == 1:
                        squares(act, n - 1)
            squares(act, 3)
            act.wait_ge(s("out_taken"), 16)
            act.wait_ge(s("tot_powed"), 1)
            for cols in LAST_COLS:
                v = proj_out[:, 3, cols]
                A(v, v, ACT.Copy, scale=sq_tot[:, 7:8]).then_inc(s("out_scaled"), 1)

        @block.gpsimd
        def _(pool):
            T = nc.gpsimd.tensor_tensor

            def split_lo(u, slot):
                pool.wait_ge(s("hi_done"), u + 1)
                T(w_lo[:, slot, :], w_raw[:, slot, :], w_hi[:, slot, :].bitcast(F32),
                  ALU.subtract).then_inc(s("lo_done"), 1)

            nc.gpsimd.memset(power[:], -0.5).then_inc(s("power_made"), 1)
            pool.wait_ge(s("power_made"), 1)
            for n, t in enumerate((4, 0, 1, 2, 3)):
                rows = P if t < 4 else META
                pool.wait_ge(s("norm_var"), n + 1)
                T(norm_s[0:rows, 10 + t:11 + t], norm_s[0:rows, 5 + t:6 + t], power[0:rows, 0:1],
                  ALU.pow).then_inc(s("norm_pow"), 1)
            for u in range(UPT + AHEAD):
                split_lo(u, u % RING)

            def powed(done, out_, in_, w, name, n):
                pool.wait_ge(s(done), n)
                T(out_[:, 0:w], in_[:, 0:w], power[:, 0:w], ALU.pow).then_inc(s(name), 1)

            def stage_pool(i):
                yield 2
                powed("n2_taken", kk_pow, kk_small, 2 * TG, "kk_powed", i)

            def gn_pool(i, work):
                yield gn_at(work) + 5
                powed("var_taken", gn_pow, gn_small, 8, "gn_powed", i - 1)

            def attn_pool(i, gn):
                yield attn_at(gn, 3) + 12.7
                powed("ovar_taken", at_pow, at_var, 4, "o_powed", i - NP_)

            def body(i, proj, work, gn):
                gens = []
                if work == "rwkv":
                    gens.append(stage_pool(i))
                if gn:
                    gens.append(gn_pool(i, work))
                if work == "attn":
                    gens.append(attn_pool(i, gn))
                gens = begin(*gens)
                for k in range(16):
                    split_lo(unit_of(i, k + AHEAD), (k + AHEAD) % RING)
                    upto(gens, k * UK + 3)
                upto(gens, 1000)

            iterations(pool, body)
            for u in range(UPT * N_TILES + KT + AHEAD, UPT * N_TILES + 4 * KT):
                split_lo(u, u % RING)
            powed("tot_made", sq_tot[:, 4:8], sq_tot[:, 0:4], 4, "tot_powed", 1)
            pool.wait_ge(s("x_back"), 64)
            for h, cols in enumerate(LAST_COLS):
                pool.wait_ge(s("out_scaled"), h + 1)
                T(proj_out[:, 3, cols], proj_out[:, 3, cols], x_again[3][:, cols], ALU.add
                  ).then_inc(s("out_made_pool"), 1)

        @block.vector
        def _(dve):
            V = nc.vector
            steps = Steps(dve, "dve_step")
            TT, STT, TS = V.tensor_tensor, V.scalar_tensor_tensor, V.tensor_scalar

            for n, t in enumerate((4, 0, 1, 2, 3)):
                rows = P if t < 4 else META
                dve.wait_ge(s("norm_sq"), n + 1)
                TS(norm_s[0:rows, 5 + t:6 + t], norm_s[0:rows, t:t + 1], 1.0 / D, EPS, ALU.mult,
                   ALU.add).then_inc(s("norm_var"), 1)
            dve.wait_ge(s("const_in"), 16)
            for n, t in enumerate((4, 0, 1, 2, 3)):
                rows = P if t < 4 else META
                dve.wait_ge(s("norm_pow"), n + 1)
                TS(norm_d[0:rows, t * P:t * P + rows], ident[0:rows, 0:rows], norm_s[0:rows, 10 + t:11 + t], None,
                   ALU.mult).then_inc(s("norm_spread"), 1)
            dve.wait_ge(s("par_turned"), 1)
            V.tensor_copy(par[:], ma[:, 0:N_PAR]).then_inc(s("par_made"), 1)
            dve.wait_ge(s("par_made"), 1)
            TS(om_mu[:], par[:, 0:25], -1.0, 1.0, ALU.mult, ALU.add)
            TS(half_w0[:], par[:, PC["w0"]:PC["w0"] + 8], 0.5, None, ALU.mult)
            TS(half_a0[:], par[:, PC["a0"]:PC["a0"] + 8], 0.5, None, ALU.mult)
            steps(TS(half_ka[:], par[:, PC["k_a"]:PC["k_a"] + 8], 0.5, None, ALU.mult))
            TS(om_ka[:], half_ka[:], -1.0, 1.0, ALU.mult, ALU.add)
            TS(gate_sub[:], par[:, PC["sub"]:PC["sub"] + 1], 0.5 * (1.0 - LAM0), None, ALU.mult)
            for k in range(KT):
                dve.wait_ge(s("hn_hi_made"), k + 1)
                o = (ma, mb)[k % 2]
                STT(hn_lo[:, k, :], o[:, TURN:TURN + L], par[:, PC["pre"] + k:PC["pre"] + k + 1],
                    hn_hi[:, k, :].bitcast(F32), ALU.mult, ALU.subtract).then_inc(s("hn_lo_made"), 1)
            dve.wait_ge(s("const16_in"), 16)
            dve.wait_ge(s("lam_in"), 64)
            for n in range(2):
                steps(TT(lam_p, lam_in[:, 2 * n * HD:(2 * n + 1) * HD], lam_in[:, (2 * n + 1) * HD:(2 * n + 2) * HD],
                         ALU.mult))
                V.reduce_sum(lam_s[:, n:n + 1], lam_p, AX).then_inc(s("lam_dots"), 1)
                dve.wait_ge(s("lam_dots"), n + 1)
            dve.wait_ge(s("lam_exp"), 1)
            steps(TT(lam[:], lam_s[:, 2:3], lam_s[:, 3:4], ALU.subtract))
            steps(TS(lam[:], lam[:], LAM0, None, ALU.add))
            for v in (xk, xv, xr, lora):
                V.memset(v[:, 0:PAD], 0.0)
            V.memset(lora[:, TP:TPX], 0.0)
            for v in (apad_r, bpad, kpad, vpad):
                V.memset(v, 0.0)
            V.memset(wu[HD:P, :], 0.0)
            V.memset(rkp[:, TP:TPX], 0.0)
            V.memset(tmp[:, 0:PAD], 0.0)
            V.memset(au[0:HD, :], 0.0)
            V.memset(ew3[:, :, 0:1], 1.0).then_inc(s("zeroed"), 1)
            dve.wait_ge(s("lora_base"), 1)
            STT(lora[:, PAD + 1:TP], tiles[0][:, EDGE:EDGE + L - 1], par[:, PC["mu_l"]:PC["mu_l"] + 1],
                lora[:, PAD + 1:TP], ALU.mult, ALU.add).then_inc(s("tile_freed"), 1)

            def tile_dve(i, proj, work, gn):
                for q in range(3):
                    yield 20 if q == 0 and gn and work == "attn" else 16 * q + 15.6
                    o = tiles[(q + 1) % 2]
                    xt = (xk, xv, xr)[q]
                    if proj == "rwkv":
                        dve.wait_ge(s("x_based"), i * 3 + (q + 1))
                        STT(xt[:, PAD + 1:TP], o[:, EDGE:EDGE + L - 1], column(par, (8, 16, 0)[q], i),
                            xt[:, PAD + 1:TP], ALU.mult, ALU.add).then_inc(s("tile_freed"), 1)
                    else:
                        dve.wait_ge(s("unit_used"), i * 16 + (8 + 4 * q))
                        if work == "rwkv":
                            dve.wait_ge(s("bonus_taken" if q == 1 else "pads_made"), NP_)
                            dve.wait_ge(s("vpad_made"), 2 * NP_)
                        else:
                            if q < 2:
                                dve.wait_ge(s("roped"), (i - NP_) * 2 + (q - 1))
                            else:
                                dve.wait_ge(s("vt_turned"), i - NP_)
                        full = FULL[proj][q]
                        n, at = (L, EDGE) if full else (SEQ, 0)
                        V.tensor_copy(xt[:, 0:n], o[:, at:at + n]).then_inc(s("tile_freed"), 1)
                yield 63.6
                dve.wait_ge(s("gate_tanh"), i + 1)
                STT(gate[:], tanh_g[:], 1.0, tiles[0][:, 0:SEQ], ALU.add, ALU.mult).then_inc(s("tile_freed"), 1)

            def gn_dve(i, work):
                n = i - 1
                yield gn_at(work) + 4.5
                dve.wait_ge(s("var_done"), n)
                TS(gn_small, mb[:, 512:520], GN_EPS, None, ALU.add).then_inc(s("var_taken"), 1)
                yield gn_at(work) + 7.5
                dve.wait_ge(s("gn_turned"), n)
                steps(TT(t512, t512, mb[:, 512:1024], ALU.mult))
                yield gn_at(work) + 8.5
                steps(TS(t512, t512, column(par, PC["gn_w"], i - 2), column(par, PC["gn_b"], i - 2),
                         ALU.mult, ALU.add))
                yield gn_at(work) + 9.5
                dst = mixed(i - 2)
                steps(TT(t512, t512, dst, ALU.add))
                yield gn_at(work) + 10.5
                dve.wait_ge(s("gate_moved"), n)
                STT(dst, gate2[:], 0.5, t512, ALU.mult, ALU.mult).then_inc(s("y_made"), 1)

            def stage_dve(i, gn):
                n = i
                yield 1.5
                dve.wait_ge(s("n2_done"), n)
                TS(kk_small, mb[:, 0:2 * TG], 1e-24, None, ALU.max).then_inc(s("n2_taken"), 1)
                yield 2
                dve.wait_ge(s("z_tanh"), n)
                steps(TS(tmp[:, PAD:TP], tmp[:, PAD:TP], 1.0, -0.5 * C_DECAY, ALU.add, ALU.mult))
                V.tensor_tensor_scan(tmp[:, 0:TP], inside, tmp[:, 0:TP], 0.0, ALU.mult,
                                     ALU.add).then_inc(s("cum_made"), 1)
                e0, e1 = ew3[:, :, 0:CH], ew3[:, :, 1:CH + 1]
                c3 = lambda v: v[:, 0:TP].rearrange("p (c t) -> p c t", c=NC)
                heads = [slice(h * HD, (h + 1) * HD) for h in range(2)]
                yield 3.3
                dve.wait_ge(s("kk_turned"), n)
                STT(kk, xk[:], column(par, PC["k_k"], i - 1), mb[:, 0:TP], ALU.mult, ALU.mult).then_inc(s("kk_made"), 1)
                yield STAGE_DVE[0]
                dve.wait_ge(s("a_made"), n)
                steps(TS(kp, tha, column(half_ka, 0, i - 1), column(om_ka, 0, i - 1), ALU.mult, ALU.add))
                yield STAGE_DVE[1]
                steps(TT(kp, kp, xk[:], ALU.mult))
                yield STAGE_DVE[2]
                dve.wait_ge(s("e_made"), n * 2)
                dve.wait_ge(s("kk_made"), n)
                steps(STT(tmp[:, 0:TP], tha, 1.0, kk, ALU.add, ALU.mult))
                yield STAGE_DVE[3]
                for h, rows in enumerate(heads):
                    TT(kpad[rows, :, h * CH:(h + 1) * CH], c3(kp)[rows], c3(emi)[rows], ALU.mult)
                yield STAGE_DVE[4]
                for h, rows in enumerate(heads):
                    ins = STT(bpad[rows, :, h * CH:(h + 1) * CH], c3(tmp)[rows], 0.5, c3(emi)[rows], ALU.mult, ALU.mult)
                ins.then_inc(s("bk_made"), 1)
                yield STAGE_DVE[5]
                STT(rkp[:, 0:TP], xr[:], column(par, PC["r_k"], i - 1), kp, ALU.mult,
                    ALU.mult).then_inc(s("rkp_made"), 1)
                yield chain_at(NG - 1, 3 * GC - 1, True)
                if gn:
                    dve.wait_ge(s("u_done"), n * NC - NC)
                for h, rows in enumerate(heads):
                    STT(apad[rows, :, h * CH:(h + 1) * CH], c3(kk)[rows], -1.0, e0[rows], ALU.mult, ALU.mult)
                TT(rc, c3(xr), e1, ALU.mult).then_inc(s("pads_made"), 1)
                yield BONUS_AT + 0.5
                dve.wait_ge(s("bonus_done"), n)
                TT(mixed(i - 1), mb[:, 0:SEQ], xv[:, CH:TP], ALU.mult).then_inc(s("bonus_taken"), 1)
                yield chain_at(0, 0, 0) - 0.5
                if gn:
                    dve.wait_ge(s("s_scaled"), (n - 1) * NC)
                    dve.wait_ge(s("y_done"), (n - 1) * NG)
                V.memset(state, 0.0).then_inc(s("state_zeroed"), 1)

            def inv_dve(i, g):
                b = g % 2
                n = groups_so_far(i, g)
                W = GC * P
                g3 = lambda v: v.rearrange("p (c t) -> p c t", c=GC)
                ma3 = ma[:, 0:GC * 256].rearrange("p (c t) -> p c t", c=GC)[:, :, 0:P + CH]
                at = C32["strict"][0]
                masks = c32[:, at:at + P + CH].unsqueeze(1).broadcast_to([P, GC, P + CH])
                yield inv_at(g, 0.5)
                dve.wait_ge(s("ab_done"), n)
                TT(b_in[b], ma3, masks, ALU.mult).then_inc(s("ab_taken"), 1)
                dve.wait_ge(s("ab_taken"), n)
                ab32 = ab_in[b]
                steps(V.tensor_copy(g3(ab_hi), ab32))
                l4 = lv.rearrange("p (l c t) -> p l c t", l=LEVELS - 1, c=GC)
                level = lambda l, o: TT(o, g3(ab_hi), level_masks[:, l, :].unsqueeze(1).broadcast_to([P, GC, P]),
                                        ALU.mult)
                steps(level(0, g3(xt16)))
                TT(g3(xt16), g3(xt16), ident16.unsqueeze(1).broadcast_to([P, GC, P]),
                   ALU.add).then_inc(s("first_made"), 1)
                yield inv_at(g, 1.5)
                dve.wait_ge(s("kb_done"), n)
                TT(k_in[b], ma3, masks, ALU.mult).then_inc(s("kb_taken"), 1)
                yield inv_at(g, LEVEL_1)
                level(1, l4[:, 0]).then_inc(s("level_1_made"), 1)
                for l in range(1, LEVELS):
                    yield inv_at(g, 1.7 + 2 * l)
                    dve.wait_ge(s("zz_done"), n * 5 + (l - 5))
                    TT(g3(z16), g3(ma[:, 512:512 + W]), ident16.unsqueeze(1).broadcast_to([P, GC, P]),
                       ALU.add).then_inc(s("zz_taken"), 1)
                    if l == 1:
                        yield inv_at(g, LEVEL_2)
                        for l2 in range(2, LEVELS):
                            level(l2, l4[:, l2 - 1])
                        TT(g3(ab_lo), ab32, g3(ab_hi), ALU.subtract).then_inc(s("levels_made"), 1)
                    yield inv_at(g, 2.7 + 2 * l)
                    dve.wait_ge(s("xt_done"), n * 5 + (l - 5))
                    V.tensor_copy(xt16, ma[:, 512:512 + W]).then_inc(s("xt_taken"), 1)
                yield inv_at(g, 13.3)
                dve.wait_ge(s("x_taken"), n * 5)
                steps(TT(ab32, ident16.unsqueeze(1).broadcast_to([P, GC, P]), g3(x16), ALU.subtract))
                yield inv_at(g, 13.7)
                dve.wait_ge(s("r_done"), n)
                TT(g3(r16), g3(ma[:, 512:512 + W]), ab32, ALU.add).then_inc(s("r_taken"), 1)
                yield inv_at(g, 14.7)
                dve.wait_ge(s("inv_done"), n)
                V.tensor_copy(t_t[b], ma[:, 0:W]).then_inc(s("inv_taken"), 1)

            def chain_dve(i, g, late, work, gn):
                for c in range(GC):
                    ch = g * GC + c
                    m = chunks_so_far(i, ch, late)
                    yield chain_at(g, 0.8 + 3 * c, late, work)
                    dve.wait_ge(s("g_done"), m)
                    V.tensor_copy(g_sb, mb[:, 0:P]).then_inc(s("g_taken"), 1)
                    yield chain_at(g, 1.8 + 3 * c, late, work)
                    dve.wait_ge(s("u_done"), m)
                    V.tensor_copy(u_sb, mb[:, 0:P]).then_inc(s("u_taken"), 1)
                    yield chain_at(g, 2.8 + 3 * c, late, work)
                    dve.wait_ge(s("s_done"), m)
                    dve.wait_ge(s("s_scaled"), m)
                    STT(state, mb[:, 0:P], w_end[:, ch:ch + 1], state0, ALU.mult, ALU.add).then_inc(s("s_taken"), 1)

            def attn_dve(i, gn):
                n = i - NP_
                at = attn_stage_at(gn)
                yield 9.3 if gn else at - 0.5
                if gn:
                    dve.wait_ge(s("s_taken"), NP_ * NC)
                    dve.wait_ge(s("y_taken"), NP_ * NG)
                    V.memset(qpad[0][HD:P, :], 0.0)
                    V.memset(qpad[1][0:HD, :], 0.0).then_inc(s("arena_freed"), 1)
                yield 15 if gn else at - 0.3
                if gn:
                    dve.wait_ge(s("rope_in"), 32)
                if not gn:
                    dve.wait_ge(s("roped"), n * 2 - 2)
                dve.wait_ge(s("tile_freed"), i * 4 - 1)
                steps.quiet(TT(rt1[:, 0:SEQ], xk[:, 0:SEQ], cos_t[:, META:L], ALU.mult))
                dve.wait_ge(s("swapped"), n * 8 - 4)
                steps(TT(q_swap, q_swap, sin_t[:, META:L], ALU.mult))
                TT(qpad[0][0:HD, :], rt1[0:HD, 0:SEQ], q_swap[0:HD, :], ALU.add)
                TT(qpad[1][HD:P, :], rt1[HD:P, 0:SEQ], q_swap[HD:P, :], ALU.add).then_inc(s("roped"), 1)
                yield 19.2 if gn else at + 0.2
                dve.wait_ge(s("roped"), n * 2 - 1)
                steps.quiet(TT(rt1, xv[:, 0:L], cos_t, ALU.mult))
                dve.wait_ge(s("swapped"), n * 8)
                steps(TT(k_swap, k_swap, sin_t, ALU.mult))
                TT(kr, rt1, k_swap, ALU.add).then_inc(s("roped"), 1)
                for qi in range(4):
                    base = attn_at(gn, qi)
                    c = n * 4 + (qi - 3)
                    at = EDGE if qi == 3 else 0
                    width = META + (qi + 1) * P
                    for m, o in ((0, ma), (1, mb)):
                        yield base + 1 + m
                        dve.wait_ge(s("score_done"), c * 2 + (m - 1))
                        d = o[:, at + width - P:at + width]
                        steps(TT(d, d, c32v("causal"), ALU.add))
                        steps(V.reduce_max(at_max[:, m:m + 1], o[:, at:at + width], AX))
                        TS(at_neg[:, m:m + 1], at_max[:, m:m + 1], -HD ** -0.5, None,
                           ALU.mult).then_inc(s("neg_made"), 1)
                    yield base + 5
                    dve.wait_ge(s("exp_made"), c * 2)
                    steps(V.reciprocal(at_inv, at_sum))
                    steps(TT(at_inv[:, 1:2], at_inv[:, 1:2], lam[:], ALU.mult))
                    steps(TS(prob[1][:, 0:width], prob[1][:, 0:width], at_inv[:, 1:2], None, ALU.mult))
                    STT(prob[0][:, 0:width], prob[0][:, 0:width], at_inv[:, 0:1], prob[1][:, 0:width], ALU.mult,
                        ALU.subtract).then_inc(s("combined"), 1)
                    yield base + 11
                    dve.wait_ge(s("pv_done"), c)
                    V.tensor_copy(o_sb[:, qi * P:(qi + 1) * P], mb[:, 0:P]).then_inc(s("o_taken"), 1)
                at = attn_at(gn, 3)
                yield at + 12.5
                dve.wait_ge(s("o_squared"), n * 4)
                TS(at_var, at_var, 1.0 / P, SUB_EPS, ALU.mult, ALU.add).then_inc(s("ovar_taken"), 1)
                yield at + 13
                dve.wait_ge(s("o_powed"), n)
                o3 = o_sb.rearrange("p (m d) -> p m d", m=4)
                TT(o3, o3, at_pow.unsqueeze(2).broadcast_to([P, 4, P]), ALU.mult).then_inc(s("o_scaled"), 1)
                yield at + 14.5
                dve.wait_ge(s("o_turned"), n)
                dve.wait_ge(s("gate_moved"), i)
                STT(mixed(i - 1), gate2[:], gate_sub[:], ma[:, 0:SEQ], ALU.mult, ALU.mult).then_inc(s("o_made"), 1)

            def split_y_dve():
                for k in range(KT):
                    yield max(4 * k - 7, -1) + 0.1 if k < KT - 1 else 200
                    dve.wait_ge(s("y_hi"), k + 1)
                    TT(hn_lo[:, k, 0:SEQ], ymix[:, k, :], hn_hi[:, k, 0:SEQ].bitcast(F32),
                       ALU.subtract).then_inc(s("y_lo"), 1)

            def body(i, proj, work, gn):
                gens = rwkv_work(i, work, gn, stage_dve, gn_dve, inv_dve, chain_dve)
                if work == "attn":
                    gens.append(attn_dve(i, gn))
                gens.append(tile_dve(i, proj, work, gn) if proj is not None else split_y_dve())
                upto(begin(*gens), 1000)
                steps.clear()

            steps.clear()
            iterations(dve, body)

            dve.wait_ge(s("post_in"), 16)
            for n in range(4):
                cols = slice(n * SEQ, (n + 1) * SEQ)
                for t in range(4):
                    dve.wait_ge(s("out_sq"), 4 * n + t + 1)
                    TT(proj_out[:, t, cols], out_banks(n)[t], post_b[:, cols], ALU.mult).then_inc(s("out_taken"), 1)
            steps(V.reduce_sum(sq_tot[:, 0:4], sq_sum.rearrange("p (t n) -> p t n", n=4), AX))
            TS(sq_tot[:, 0:4], sq_tot[:, 0:4], 1.0 / D, EPS, ALU.mult, ALU.add).then_inc(s("tot_made"), 1)
            dve.wait_ge(s("tot_powed"), 1)
            dve.wait_ge(s("out_taken"), 16)
            dve.wait_ge(s("x_back"), 64)
            for cols in LAST_COLS:
                for t in range(3):
                    STT(proj_out[:, t, cols], proj_out[:, t, cols], sq_tot[:, 4 + t:5 + t], x_again[t][:, cols],
                        ALU.mult, ALU.add).then_inc(s("out_made"), 1)


INPUTS = ("x", "meta_tokens", "pre_norm_w", "w_in", "rwkv_mu", "rwkv_w0", "rwkv_w_up", "rwkv_a0", "rwkv_a_up",
          "rwkv_k_k", "rwkv_k_a", "rwkv_r_k", "rwkv_gn_w", "rwkv_gn_b", "diff_lam_q1", "diff_lam_k1",
          "diff_lam_q2", "diff_lam_k2", "diff_subln_w", "w_out", "post_norm_w")


def kernel(**inputs):
    import concourse.bacc as bacc
    from concourse.bass_utils import run_bass_kernel_spmd

    nc = bacc.Bacc("TRN2", target_bir_lowering=False, num_devices=1)
    arrays, args = {}, []
    tables = dict(zip(("table_f32", "table_f16", "table_rope"), constants()))
    for name, a in [(n, inputs[n]) for n in INPUTS] + list(tables.items()):
        a = np.ascontiguousarray(a)
        arrays[name] = a
        args.append(nc.dram_tensor(name, a.shape, mybir.dt.from_np(a.dtype), kind="ExternalInput").ap())
    out = nc.dram_tensor("out", (1, SEQ, D), F32, kind="ExternalOutput").ap()
    hybrid_layer(nc, *args, out)
    r = run_bass_kernel_spmd(nc, [arrays], core_ids=[0])
    return r.results[0]["out"]
```
